# Optimizing a Trainium2 kernel written in Bass

```python
import math
import jax, jax.numpy as jnp
from jax import lax
import numpy as np
import jax
import jax.numpy as jnp

D_MODEL = 1024
BATCH = 1
SEQ = 512
DEPTH = 1

CHUNK = 64
SSD_HEADS = 16
SSD_HEAD_DIM = 64
SSD_INNER = SSD_HEADS * SSD_HEAD_DIM
SSD_GROUPS = 2
SSD_STATE = 128
SSD_CONV = 4
SSD_SCAN_CHUNK = CHUNK
CONV_DIM = SSD_INNER + 2 * SSD_GROUPS * SSD_STATE
SB_HEADS = 16
SB_HEAD_DIM = 64
SB_INNER = SB_HEADS * SB_HEAD_DIM
SB_BLOCK = 128
N_BRANCH = 2
IN_SIZES = (SSD_INNER, CONV_DIM, SSD_HEADS, SB_INNER, SB_INNER, SB_INNER, SB_INNER, N_BRANCH * D_MODEL)
IN_COLS = sum(IN_SIZES)
EPS = 1e-6


def _split_points():
    pts, acc = [], 0
    for s in IN_SIZES[:-1]:
        acc += s
        pts.append(acc)
    return pts

def rmsnorm(x, w):
    xf = x.astype(jnp.float32)
    y = xf * lax.rsqrt(jnp.mean(xf * xf, axis=-1, keepdims=True) + EPS)
    return (y * w.astype(jnp.float32)).astype(x.dtype)

def gated_group_rmsnorm(y, z, w, groups):
    g = (y.astype(jnp.float32) * jax.nn.silu(z.astype(jnp.float32)))
    g = g.reshape(y.shape[:-1] + (groups, y.shape[-1] // groups))
    g = g * lax.rsqrt(jnp.mean(g * g, axis=-1, keepdims=True) + EPS)
    return (g.reshape(y.shape) * w.astype(jnp.float32)).astype(y.dtype)

def ssd_scan(xh, dt, a, bmat, cmat, d_skip):
    bsz, L, H, P = xh.shape
    G, N = bmat.shape[2], bmat.shape[3]
    R = H // G
    T = SSD_SCAN_CHUNK
    NC = L // T
    x_dt = (xh * dt[..., None]).reshape(bsz, NC, T, G, R, P)
    a_dt = jnp.transpose((dt * a).reshape(bsz, NC, T, G, R), (0, 3, 4, 1, 2))
    a_cs = jnp.cumsum(a_dt, axis=-1)
    bc = bmat.reshape(bsz, NC, T, G, N)
    cc = cmat.reshape(bsz, NC, T, G, N)
    seg = a_cs[..., :, None] - a_cs[..., None, :]
    causal = jnp.tril(jnp.ones((T, T), dtype=bool))
    decay = jnp.exp(jnp.where(causal, seg, -jnp.inf))
    scores = jnp.einsum('bclgn,bcsgn->bgcls', cc, bc)
    attn = scores[:, :, None] * decay
    y_diag = jnp.einsum('bgrcls,bcsgrp->bclgrp', attn, x_dt)
    decay_states = jnp.exp(a_cs[..., -1:] - a_cs)
    states = jnp.einsum('bclgn,bgrcl,bclgrp->bcgrpn', bc, decay_states, x_dt)
    chunk_decay = jnp.exp(a_cs[..., -1])

    def step(carry, inp):
        st, dec = inp
        new = carry * dec[..., None, None] + st
        return new, carry

    init = jnp.zeros((bsz, G, R, P, N), dtype=xh.dtype)
    _, prev = lax.scan(step, init, (jnp.moveaxis(states, 1, 0), jnp.moveaxis(chunk_decay, -1, 0)))
    prev = jnp.moveaxis(prev, 0, 1)
    y_off = jnp.einsum('bclgn,bcgrpn,bgrcl->bclgrp', cc, prev, jnp.exp(a_cs))
    y = (y_diag + y_off).reshape(bsz, L, H, P)
    return y + xh * d_skip[:, None]

def stick_breaking(q, k, v):
    bsz, L, H, Dh = q.shape
    scale = Dh ** -0.5
    outs = []
    for blk in range(L // SB_BLOCK):
        q0 = blk * SB_BLOCK
        kend = q0 + SB_BLOCK
        logits = jnp.einsum('bqhd,bkhd->bhqk', q[:, q0:kend], k[:, :kend]).astype(jnp.float32) * scale
        qi = q0 + jnp.arange(SB_BLOCK)[:, None]
        ki = jnp.arange(kend)[None, :]
        mask = ki < qi
        log_fail = jnp.where(mask, jax.nn.log_sigmoid(-logits), 0.0)
        between = lax.cumsum(log_fail, axis=3, reverse=True) - log_fail
        w = jnp.where(mask, jnp.exp(jax.nn.log_sigmoid(logits) + between), 0.0)
        outs.append(jnp.einsum('bhqk,bkhd->bqhd', w.astype(v.dtype), v[:, :kend]))
    return jnp.concatenate(outs, axis=1)

def hybrid_layer(x, norm_pre, w_in, b_gate, conv_w, conv_b, dt_bias, a_log, d_skip,
                 ssd_norm, w_ssd_proj, w_sb_proj, w_out, norm_post):
    bsz, L, _ = x.shape
    h = rmsnorm(x, norm_pre)
    proj = jnp.einsum('bld,de->ble', h, w_in)
    z_ssd, xbc, dt_raw, q, k, v, z_sb, gates = jnp.split(proj, _split_points(), axis=-1)

    xbc = lax.conv_general_dilated(
        xbc, conv_w[:, None, :], window_strides=(1,), padding=[(SSD_CONV - 1, 0)],
        dimension_numbers=('NWC', 'WIO', 'NWC'), feature_group_count=CONV_DIM) + conv_b
    xbc = jax.nn.silu(xbc)
    xs, bm, cm = jnp.split(xbc, [SSD_INNER, SSD_INNER + SSD_GROUPS * SSD_STATE], axis=-1)
    dt = jax.nn.softplus(dt_raw.astype(jnp.float32) + dt_bias.astype(jnp.float32))
    a = -jnp.exp(a_log.astype(jnp.float32))
    y = ssd_scan(xs.reshape(bsz, L, SSD_HEADS, SSD_HEAD_DIM).astype(jnp.float32), dt, a,
                 bm.reshape(bsz, L, SSD_GROUPS, SSD_STATE).astype(jnp.float32),
                 cm.reshape(bsz, L, SSD_GROUPS, SSD_STATE).astype(jnp.float32),
                 d_skip.astype(jnp.float32))
    y = y.reshape(bsz, L, SSD_INNER).astype(x.dtype)
    y = gated_group_rmsnorm(y, z_ssd, ssd_norm, SSD_GROUPS)
    y_ssd = jnp.einsum('ble,ed->bld', y, w_ssd_proj)

    o = stick_breaking(q.reshape(bsz, L, SB_HEADS, SB_HEAD_DIM),
                       k.reshape(bsz, L, SB_HEADS, SB_HEAD_DIM),
                       v.reshape(bsz, L, SB_HEADS, SB_HEAD_DIM)).reshape(bsz, L, SB_INNER)
    y_sb = jnp.einsum('ble,ed->bld', o * jax.nn.silu(z_sb), w_sb_proj)

    g = jax.nn.sigmoid(gates + b_gate)
    g_ssd, g_sb = jnp.split(g, [D_MODEL], axis=-1)
    merged = g_ssd * y_ssd + g_sb * y_sb
    out = jnp.einsum('bld,de->ble', merged, w_out)
    return x + rmsnorm(out, norm_post)

def first_inputs(seed: int = 0) -> dict:
    key = jax.random.key(seed)
    ks = jax.random.split(key, 16)
    f32 = jnp.float32
    x = jax.random.normal(ks[0], (BATCH, SEQ, D_MODEL), f32)
    norm_pre = 1.0 + 0.05 * jax.random.normal(ks[1], (DEPTH, D_MODEL), f32)
    w_in = jax.random.normal(ks[2], (DEPTH, D_MODEL, IN_COLS), f32) * D_MODEL ** -0.5
    b_gate = 0.02 * jax.random.normal(ks[3], (DEPTH, N_BRANCH * D_MODEL), f32)
    conv_w = jax.random.normal(ks[4], (DEPTH, SSD_CONV, CONV_DIM), f32) * SSD_CONV ** -0.5
    conv_b = 0.02 * jax.random.normal(ks[5], (DEPTH, CONV_DIM), f32)
    u = jax.random.uniform(ks[6], (DEPTH, SSD_HEADS), f32)
    dt0 = jnp.exp(u * (math.log(0.1) - math.log(0.001)) + math.log(0.001))
    dt_bias = dt0 + jnp.log(-jnp.expm1(-dt0))
    a_log = jnp.log(jax.random.uniform(ks[7], (DEPTH, SSD_HEADS), f32, 1.0, 16.0))
    d_skip = 1.0 + 0.05 * jax.random.normal(ks[8], (DEPTH, SSD_HEADS), f32)
    ssd_norm = 1.0 + 0.05 * jax.random.normal(ks[9], (DEPTH, SSD_INNER), f32)
    w_ssd_proj = jax.random.normal(ks[10], (DEPTH, SSD_INNER, D_MODEL), f32) * SSD_INNER ** -0.5
    w_sb_proj = jax.random.normal(ks[11], (DEPTH, SB_INNER, D_MODEL), f32) * SB_INNER ** -0.5
    w_out = jax.random.normal(ks[12], (DEPTH, D_MODEL, D_MODEL), f32) * D_MODEL ** -0.5
    norm_post = 1.0 + 0.05 * jax.random.normal(ks[13], (DEPTH, D_MODEL), f32)
    return {"x": x, "norm_pre": norm_pre, "w_in": w_in, "b_gate": b_gate,
            "conv_w": conv_w, "conv_b": conv_b, "dt_bias": dt_bias, "a_log": a_log,
            "d_skip": d_skip, "ssd_norm": ssd_norm, "w_ssd_proj": w_ssd_proj,
            "w_sb_proj": w_sb_proj, "w_out": w_out, "norm_post": norm_post}

def first_block(x, norm_pre, w_in, b_gate, conv_w, conv_b, dt_bias, a_log, d_skip,
              ssd_norm, w_ssd_proj, w_sb_proj, w_out, norm_post):
    for layer in range(DEPTH):
        x = hybrid_layer(x, norm_pre[layer], w_in[layer], b_gate[layer], conv_w[layer],
                         conv_b[layer], dt_bias[layer], a_log[layer], d_skip[layer],
                         ssd_norm[layer], w_ssd_proj[layer], w_sb_proj[layer],
                         w_out[layer], norm_post[layer])
    return x


NSA_HEADS = 8
NSA_KV_GROUPS = 2
NSA_HEAD_DIM = 64
CMP_LEN = 32
CMP_STRIDE = 16
CMP_HIDDEN = 128
SLC_LEN = 64
N_SELECT = 16
WINDOW = 512
Q_BLOCK = 128
FORCE_SCORE = 1e4
HGRN_HEADS = 4
HGRN_KEY_DIM = 128
HGRN_VAL_DIM = 128
HGRN_CHUNK = 64
D_FF = -(-8 * D_MODEL // (3 * 256)) * 256
RMS_EPS = 1e-6

NSA_WIDTH = NSA_HEADS * NSA_HEAD_DIM
NSA_KV_WIDTH = NSA_KV_GROUPS * NSA_HEAD_DIM
HGRN_KEY_WIDTH = HGRN_HEADS * HGRN_KEY_DIM
HGRN_VAL_WIDTH = HGRN_HEADS * HGRN_VAL_DIM
MIX_WIDTH = NSA_WIDTH + HGRN_VAL_WIDTH
IN_SIZES_2 = (NSA_WIDTH,) + (NSA_KV_WIDTH,) * 6 + (3 * NSA_HEADS, HGRN_KEY_WIDTH, HGRN_KEY_WIDTH, HGRN_VAL_WIDTH, HGRN_VAL_WIDTH)
IN_WIDTH = sum(IN_SIZES_2)


def rms_norm(x, g):
    xf = x.astype(jnp.float32)
    y = xf * lax.rsqrt(jnp.mean(xf * xf, axis=-1, keepdims=True) + RMS_EPS)
    return (y * g.astype(jnp.float32)).astype(x.dtype)

def masked_softmax(s, mask):
    s = jnp.where(mask, s.astype(jnp.float32), -1e30)
    p = jax.nn.softmax(s, axis=-1)
    return jnp.where(mask, p, 0.0)

def compress(seq, pos, w1, w2):
    B, T, G, dh = seq.shape
    ratio = CMP_LEN // CMP_STRIDE
    nseg = T // CMP_STRIDE
    ncmp = nseg - ratio + 1
    seg = seq.reshape(B, nseg, CMP_STRIDE, G, dh)
    blocks = jnp.concatenate([seg[:, r:r + ncmp] for r in range(ratio)], axis=2)
    blocks = blocks + pos[None, None, :, None, :]
    flat = blocks.transpose(0, 1, 3, 2, 4).reshape(B, ncmp, G, CMP_LEN * dh)
    return jax.nn.gelu(flat @ w1) @ w2

def nsa_mixer(q, kc, vc, ks, vs, kw, vw, gates):
    B, T, H, dh = q.shape
    G = NSA_KV_GROUPS
    R = H // G
    ncmp = kc.shape[1]
    nslc = T // SLC_LEN
    n_sel = min(N_SELECT, nslc)
    scale = dh ** -0.5
    cmp_start = jnp.arange(ncmp) * CMP_STRIDE
    cmp_end = cmp_start + CMP_LEN - 1
    slc_start = jnp.arange(nslc) * SLC_LEN
    overlap = ((cmp_start[:, None] < slc_start[None, :] + SLC_LEN)
               & (cmp_start[:, None] + CMP_LEN > slc_start[None, :])).astype(jnp.float32)
    ks_blk = ks.reshape(B, nslc, SLC_LEN, G, dh).transpose(0, 3, 1, 2, 4)
    vs_blk = vs.reshape(B, nslc, SLC_LEN, G, dh).transpose(0, 3, 1, 2, 4)
    pad = ((0, 0), (WINDOW, 0), (0, 0), (0, 0))
    kw_pad = jnp.pad(kw, pad)
    vw_pad = jnp.pad(vw, pad)
    bi = jnp.arange(B)[:, None, None, None]
    gi = jnp.arange(G)[None, :, None, None]
    j = jnp.arange(nslc)

    def block(qb):
        s = qb * Q_BLOCK
        t = s + jnp.arange(Q_BLOCK)
        qblk = lax.dynamic_slice_in_dim(q, s, Q_BLOCK, 1).reshape(B, Q_BLOCK, G, R, dh)
        sc = jnp.einsum('bqgrd,bngd->bgrqn', qblk, kc) * scale
        p_cmp = masked_softmax(sc, cmp_end[None, :] <= t[:, None])
        o_cmp = jnp.einsum('bgrqn,bngd->bqgrd', p_cmp, vc.astype(jnp.float32))
        imp = jnp.einsum('bgrqn,nj->bgqj', p_cmp, overlap)
        jcur = t // SLC_LEN
        forced = (j[None, :] == 0) | (j[None, :] == jcur[:, None]) | (j[None, :] == jcur[:, None] - 1)
        future = j[None, :] > jcur[:, None]
        imp = jnp.where(forced, FORCE_SCORE, jnp.where(future, -1.0, imp))
        _, idx = lax.top_k(imp, n_sel)
        k_sel = ks_blk[bi, gi, idx].reshape(B, G, Q_BLOCK, n_sel * SLC_LEN, dh)
        v_sel = vs_blk[bi, gi, idx].reshape(B, G, Q_BLOCK, n_sel * SLC_LEN, dh)
        pos_sel = (idx[..., None] * SLC_LEN + jnp.arange(SLC_LEN)).reshape(B, G, Q_BLOCK, n_sel * SLC_LEN)
        ss = jnp.einsum('bqgrd,bgqkd->bgrqk', qblk, k_sel) * scale
        p_sel = masked_softmax(ss, (pos_sel <= t[None, None, :, None])[:, :, None])
        o_sel = jnp.einsum('bgrqk,bgqkd->bqgrd', p_sel, v_sel.astype(jnp.float32))
        k_win = lax.dynamic_slice_in_dim(kw_pad, s, WINDOW + Q_BLOCK, 1)
        v_win = lax.dynamic_slice_in_dim(vw_pad, s, WINDOW + Q_BLOCK, 1)
        pos_win = s - WINDOW + jnp.arange(WINDOW + Q_BLOCK)
        diff = t[:, None] - pos_win[None, :]
        win_mask = (diff >= 0) & (diff < WINDOW) & (pos_win[None, :] >= 0)
        sw = jnp.einsum('bqgrd,bkgd->bgrqk', qblk, k_win) * scale
        p_win = masked_softmax(sw, win_mask)
        o_win = jnp.einsum('bgrqk,bkgd->bqgrd', p_win, v_win.astype(jnp.float32))
        g = lax.dynamic_slice_in_dim(gates, s, Q_BLOCK, 1).reshape(B, Q_BLOCK, G, R, 3)
        o = g[..., 0:1] * o_cmp + g[..., 1:2] * o_sel + g[..., 2:3] * o_win
        return o.reshape(B, Q_BLOCK, H * dh)

    out = lax.map(block, jnp.arange(T // Q_BLOCK))
    return out.transpose(1, 0, 2, 3).reshape(B, T, H * dh)

def hgrn2_mixer(hq, hf, hi, hg, lb, o_gain):
    B, T, _ = hq.shape
    H, dk, dv, C = HGRN_HEADS, HGRN_KEY_DIM, HGRN_VAL_DIM, HGRN_CHUNK
    f32 = jnp.float32
    q = jax.nn.silu(hq.astype(f32)).reshape(B, T, H, dk)
    f = lb + (1.0 - lb) * jax.nn.sigmoid(hf.astype(f32))
    logf = jnp.log(f).reshape(B, T, H, dk)
    k = (1.0 - f).reshape(B, T, H, dk)
    v = hi.astype(f32).reshape(B, T, H, dv)
    nc = T // C

    def to_chunks(a):
        return a.reshape(B, nc, C, H, a.shape[-1]).transpose(1, 0, 3, 2, 4)

    causal = jnp.tril(jnp.ones((C, C), dtype=bool))

    def step(S, xs):
        qc, kc, vc, gc = xs
        b = jnp.cumsum(gc, axis=-2)
        b_last = b[:, :, -1:, :]
        o_inter = jnp.einsum('bhcd,bhde->bhce', qc * jnp.exp(b), S)
        decay = jnp.exp(jnp.where(causal[:, :, None], b[:, :, :, None, :] - b[:, :, None, :, :], -jnp.inf))
        attn = jnp.einsum('bhtd,bhsd,bhtsd->bhts', qc, kc, decay)
        o = o_inter + jnp.einsum('bhts,bhse->bhte', attn, vc)
        S = jnp.exp(b_last[:, :, 0, :])[..., None] * S + jnp.einsum('bhsd,bhse->bhde', kc * jnp.exp(b_last - b), vc)
        return S, o

    S0 = jnp.zeros((B, H, dk, dv), f32)
    _, o = lax.scan(step, S0, (to_chunks(q), to_chunks(k), to_chunks(v), to_chunks(logf)))
    o = o.transpose(1, 0, 3, 2, 4).reshape(B, T, H, dv)
    o = rms_norm(o, o_gain) * jax.nn.silu(hg.astype(f32)).reshape(B, T, H, dv)
    return o.reshape(B, T, H * dv)

def second_inputs(seed: int = 0) -> dict:
    key = jax.random.key(seed)
    k = jax.random.split(key, 17)
    f32 = jnp.float32
    dh = NSA_HEAD_DIM

    def nrm(kk, shape, scale):
        return jax.random.normal(kk, shape, f32) * scale

    return {
        'x': nrm(k[0], (BATCH, SEQ, D_MODEL), 1.0),
        'norm_mix': 1.0 + nrm(k[1], (DEPTH, D_MODEL), 0.02),
        'w_in': nrm(k[2], (DEPTH, D_MODEL, IN_WIDTH), D_MODEL ** -0.5),
        'q_norm': 1.0 + nrm(k[3], (DEPTH, dh), 0.02),
        'k_norm': 1.0 + nrm(k[4], (DEPTH, 3, dh), 0.02),
        'cmp_pos_k': nrm(k[5], (DEPTH, CMP_LEN, dh), 0.5),
        'cmp_pos_v': nrm(k[6], (DEPTH, CMP_LEN, dh), 0.5),
        'cmp_k_w1': nrm(k[7], (DEPTH, CMP_LEN * dh, CMP_HIDDEN), (CMP_LEN * dh) ** -0.5),
        'cmp_k_w2': nrm(k[8], (DEPTH, CMP_HIDDEN, dh), CMP_HIDDEN ** -0.5),
        'cmp_v_w1': nrm(k[9], (DEPTH, CMP_LEN * dh, CMP_HIDDEN), (CMP_LEN * dh) ** -0.5),
        'cmp_v_w2': nrm(k[10], (DEPTH, CMP_HIDDEN, dh), CMP_HIDDEN ** -0.5),
        'hgrn_lb_logits': nrm(k[11], (DEPTH + 1, HGRN_KEY_WIDTH), 0.5),
        'hgrn_o_norm': 1.0 + nrm(k[12], (DEPTH, HGRN_VAL_DIM), 0.02),
        'w_out': nrm(k[13], (DEPTH, MIX_WIDTH, D_MODEL), MIX_WIDTH ** -0.5),
        'norm_ffn': 1.0 + nrm(k[14], (DEPTH, D_MODEL), 0.02),
        'w_gate_up': nrm(k[15], (DEPTH, D_MODEL, 2 * D_FF), D_MODEL ** -0.5),
        'w_down': nrm(k[16], (DEPTH, D_FF, D_MODEL), D_FF ** -0.5),
    }

def second_block(x, norm_mix, w_in, q_norm, k_norm, cmp_pos_k, cmp_pos_v, cmp_k_w1, cmp_k_w2, cmp_v_w1, cmp_v_w2,
              hgrn_lb_logits, hgrn_o_norm, w_out, norm_ffn, w_gate_up, w_down):
    B, T, _ = x.shape
    H, G, dh = NSA_HEADS, NSA_KV_GROUPS, NSA_HEAD_DIM
    split_points = [int(v) for v in np.cumsum(IN_SIZES_2)[:-1]]
    lower_bounds = jnp.cumsum(jax.nn.softmax(hgrn_lb_logits.astype(jnp.float32), axis=0), axis=0)
    for l in range(DEPTH):
        h = rms_norm(x, norm_mix[l])
        proj = h @ w_in[l]
        (q, kc_raw, vc_raw, ks, vs, kw, vw, gate_logits, hq, hf, hi, hg) = jnp.split(proj, split_points, axis=-1)
        q = rms_norm(q.reshape(B, T, H, dh), q_norm[l])
        kc = rms_norm(compress(kc_raw.reshape(B, T, G, dh), cmp_pos_k[l], cmp_k_w1[l], cmp_k_w2[l]), k_norm[l, 0])
        vc = compress(vc_raw.reshape(B, T, G, dh), cmp_pos_v[l], cmp_v_w1[l], cmp_v_w2[l])
        ks = rms_norm(ks.reshape(B, T, G, dh), k_norm[l, 1])
        kw = rms_norm(kw.reshape(B, T, G, dh), k_norm[l, 2])
        gates = jax.nn.sigmoid(gate_logits.astype(jnp.float32)).reshape(B, T, H, 3)
        o_nsa = nsa_mixer(q, kc, vc, ks, vs.reshape(B, T, G, dh), kw, vw.reshape(B, T, G, dh), gates)
        o_hgrn = hgrn2_mixer(hq, hf, hi, hg, lower_bounds[l], hgrn_o_norm[l])
        mix = jnp.concatenate([o_nsa.astype(x.dtype), o_hgrn.astype(x.dtype)], axis=-1)
        x = x + mix @ w_out[l]
        h = rms_norm(x, norm_ffn[l])
        gate, up = jnp.split(h @ w_gate_up[l], 2, axis=-1)
        x = x + (jax.nn.silu(gate) * up) @ w_down[l]
    return x


def setup_inputs(seed=0):
    out = dict(first_inputs(seed))
    for name, value in second_inputs(seed + 1).items():
        if name != "x":
            out[name + "_2"] = value
    return out


def reference(
    x, norm_pre, w_in, b_gate, conv_w, conv_b, dt_bias, a_log, d_skip, ssd_norm, w_ssd_proj,
    w_sb_proj, w_out, norm_post, norm_mix_2, w_in_2, q_norm_2, k_norm_2, cmp_pos_k_2,
    cmp_pos_v_2, cmp_k_w1_2, cmp_k_w2_2, cmp_v_w1_2, cmp_v_w2_2, hgrn_lb_logits_2,
    hgrn_o_norm_2, w_out_2, norm_ffn_2, w_gate_up_2, w_down_2,
):
    x = first_block(
        x, norm_pre, w_in, b_gate, conv_w, conv_b, dt_bias, a_log, d_skip, ssd_norm, w_ssd_proj,
        w_sb_proj, w_out, norm_post,
    )
    return second_block(
        x, norm_mix_2, w_in_2, q_norm_2, k_norm_2, cmp_pos_k_2, cmp_pos_v_2, cmp_k_w1_2,
        cmp_k_w2_2, cmp_v_w1_2, cmp_v_w2_2, hgrn_lb_logits_2, hgrn_o_norm_2, w_out_2,
        norm_ffn_2, w_gate_up_2, w_down_2,
    )


_drawn_inputs = setup_inputs


def setup_inputs(seed=0):
    import zlib

    import numpy as np

    out = dict(_drawn_inputs(seed))
    spreads = {}
    factors = {'b_gate': 8.0,
     'd_skip': 2.67,
     'norm_mix_2': 6.008,
     'q_norm_2': 8.0,
     'k_norm_2': 8.0,
     'cmp_pos_k_2': 3.506,
     'hgrn_lb_logits_2': 3.363,
     'hgrn_o_norm_2': 8.0,
     'norm_ffn_2': 16.727,
     'cmp_pos_v_2': 6.54}
    for name, (base, spread) in spreads.items():
        noise = np.random.default_rng([zlib.crc32(name.encode()), seed]).standard_normal(out[name].shape)
        drawn = base * np.exp(spread * noise) if base else spread * noise
        out[name] = jnp.asarray(drawn.astype(out[name].dtype))
    for name, factor in factors.items():
        out[name] = (out[name] * factor).astype(out[name].dtype)
    return out
```

```python
from contextlib import ExitStack

import numpy as np

import concourse.bass as bass
from concourse import mybir

ALU = mybir.AluOpType
ACT = mybir.ActivationFunctionType
AX = mybir.AxisListType
F32 = mybir.dt.float32
F32R = mybir.dt.float32r
BF16 = mybir.dt.bfloat16
U8 = mybir.dt.uint8

P = 128
T = 512
D = 1024
NT = T // P
NK = D // P
EPS = 1e-6
NEG = -1e30
HD = 64
SCALE = HD ** -0.5

Z0, XBC0 = 0, 1024
DT0 = XBC0 + 1536
Q0 = DT0 + 16
K0, V0, ZS0, G0 = Q0 + 1024, Q0 + 2048, Q0 + 3072, Q0 + 4096
SH = 16
XC = 12
TAPS = 4
KC0 = 512
KS0, GL0, HQ0, HF0, HI0, HG0 = 768, 1280, 1304, 1816, 2328, 2840
NH = 8
NG = 2
NCMP = 31
CL, CS = 32, 16
HH = 4
DFF = 2816
FFP = ((0, 8), (8, 16), (16, 22))
LEVELS = 9
GEMM_BANKS = 4
BLK = 2048



def plan():
    blocks, tiles, steps = [], [], []

    def tile(kind, i):
        tiles.append((kind, i))
        return len(tiles) - 1

    def feature(w, spans, kinds, srcs):
        gs = [tile(k, i) for k, i in kinds]
        blocks.append(dict(w=w, form="feature", spans=spans, k0=0, kn=NK, tiles=gs, srcs=srcs, opens=gs, closes=gs))
        return len(blocks) - 1

    def token(w, col, kind, half, src, k0=0, kn=NK):
        gs = [tile(kind, (t, half)) for t in range(NT)]
        a = kn // 2
        out = []
        for j in range(2):
            blocks.append(dict(w=w, form="token", spans=[(col, 512)], k0=k0 + j * a, kn=a, tiles=gs, srcs=[src] * 4,
                               opens=gs if j == 0 else [], closes=gs if j == 1 else [], first=j == 0,
                               last=j == 1, kb=j * a))
            out.append(len(blocks) - 1)
        return out

    def turn(name, c):
        steps.append(("turn", name, c, tile("turn_" + name, c)))

    def gemm(*ns):
        steps.extend(("gemm", n) for n in ns)

    steps.append(("norm", "x"))
    for c in range(NK):
        turn("x", c)
    for j in range(XC // 2):
        gemm(feature("w_in", [(XBC0 + 256 * j, 256)], [("xbc", 2 * j), ("xbc", 2 * j + 1)], "AA"))
        if j >= 1:
            steps.extend([("xturn", 2 * j - 2), ("xturn", 2 * j - 1)])
    steps.append(("small", "dt", tile("dt", 0)))
    for half in range(2):
        gemm(*token("w_in", Z0 + 512 * half, "z", half, "A"))
    steps.append(("ssd_decay",))
    for c in range(NT):
        for part in range(5):
            steps.append(("ssd", c, part))
            if part == 2:
                gemm(feature("w_in", [(K0 + 256 * c, 256)], [("k", 2 * c), ("k", 2 * c + 1)], "AA"))
    steps.append(("norm", "y"))
    for j in range(4):
        gemm(feature("w_in", [(Q0 + 256 * j, 256)], [("q", 2 * j), ("q", 2 * j + 1)], "AA"))
    for half in range(2):
        gemm(*token("w_in", V0 + 512 * half, "v", half, "A"))
    for c in range(NK):
        turn("y", c)
    units = SH * NT
    lag = 0
    for c in range(NK):
        gemm(feature("gate_ssd", [(G0 + P * c, P), (P * c, P)], [("gate", c), ("y_ssd", c)], "AB"))
        for u in range(c * units // NK, (c + 1) * units // NK):
            steps.append(("sb", u))
    steps.append(("sb", units))
    steps.append(("sb", units + 1))
    for j in range(4):
        gemm(feature("w_in", [(ZS0 + 256 * j, 256)], [("z_sb", 2 * j), ("z_sb", 2 * j + 1)], "AA"))
    for c in range(NK):
        gemm(feature("gate_sb", [(G0 + D + P * c, P), (P * c, P)], [("gate2", c), ("y_sb", c)], "AB"))
    for c in range(NK):
        steps.append(("merge", c))
    for half in range(2):
        gemm(*token("w_out", 512 * half, "out1", half, "A"))

    steps.append(("norm", "out1"))
    steps.append(("norm", "mix"))
    for c in range(NK):
        turn("mix", c)
    gemm(*token("w_in_2", KS0, "kv", 0, "A"))
    gemm(*token("w_in_2", 0, "qn", 0, "A"))
    gemm(feature("w_in_2", [(KC0, 256)], [("kcv", 0), ("kcv", 1)], "AA"))
    steps.append(("small", "gates", tile("gates", 0)))
    steps.append(("norm", "qk"))
    for i in range(6):
        steps.append(("qkturn", i, tile("turn_qk", i)))
    steps.append(("compress",))
    for qt in range(NT):
        steps.append(("cmp", qt))
    units = 2 * NH * NT
    hblocks = token("w_in_2", HI0, "hi", 0, "A") + token("w_in_2", HG0, "hg", 0, "A")
    for i, n in enumerate(hblocks):
        gemm(n)
        for u in range(i * units // 4, (i + 1) * units // 4):
            steps.append(("nsa", u))
    steps.append(("nsa", units))
    steps.append(("nsa", units + 1))
    for h in range(HH):
        gemm(feature("w_in_2", [(HQ0 + P * h, P), (HF0 + P * h, P)], [("hq", h), ("hf", h)], "AA"))
        if h >= 1:
            steps.append(("hgrn", h - 1))
    steps.append(("hgrn", HH - 1))
    steps.append(("norm", "hgrn"))
    for c in range(NK):
        turn("heads", c)
    for half in range(2):
        gemm(*token("w_out_2", 512 * half, "out2", half, "B"))
    steps.append(("norm", "ffn"))
    for c in range(NK):
        turn("ffn", c)
    for a, e in FFP:
        for c in range(a, e):
            gemm(feature("w_gate_up", [(P * c, P), (DFF + P * c, P)], [("ff_gate", (c, c - a)), ("ff_up", (c, c - a))], "AA"))
        for half in range(2):
            gemm(*token("w_down", 512 * half, "down", (a, half), "B", k0=a, kn=e - a))
    return blocks, tiles, steps



BLOCKS, TILES, STEPS = plan()
NB = len(BLOCKS)

READER = {"turn_x": "V", "xbc": "V", "dt": "V", "z": "V", "k": "S", "q": "S", "v": "S", "turn_y": "V", "gate": "S",
          "y_ssd": "V", "z_sb": "V", "gate2": "S", "y_sb": "V", "out1": "S",
          "turn_mix": "V", "kv": "S", "qn": "S", "kcv": "S", "gates": "S", "turn_qk": "S", "hi": "S", "hg": "V",
          "hq": "V", "hf": "V", "turn_heads": "V", "out2": "V", "turn_ffn": "V", "ff_gate": "V", "ff_up": "V",
          "down": "V"}


class Ring:

    def __init__(self, size):
        self.size, self.ends, self.count, self.at = size, [], {"V": 0, "S": 0}, {}

    def use(self, key, reader):
        self.count[reader] += 1
        self.at[key] = len(self.ends)
        self.ends.append((reader, self.count[reader]))

    def slot(self, key):
        return self.at[key] % self.size

    def before(self, key):
        i = self.at[key] - self.size
        return self.ends[i] if i >= 0 else None


def plan_tiles():
    ring = Ring(GEMM_BANKS)
    for g, (kind, _) in enumerate(TILES):
        ring.use(g, READER[kind])
    return ring


TILE_RING = plan_tiles()


def plan_aux():
    ring = Ring(2)
    for s in STEPS:
        if s[0] == "xturn":
            ring.use(s, "S")
        if s[0] == "ssd_decay":
            ring.use("decay", "V")
        if s[0] == "ssd":
            _, c, part = s
            if part == 0:
                ring.use(("scores", c), "V")
            if part < 4:
                ring.use(("decay", c, part), "S")
            if part == 4:
                for g in range(2):
                    if c > 0:
                        ring.use(("y_off", c, g), "V")
                for g in range(2):
                    if c < NT - 1:
                        ring.use(("state", c, g), "V")
    return ring


AUX = plan_aux()
SIGMOID = {"z", "gate", "z_sb", "gate2", "hg", "hq", "hf", "ff_gate"}
CONSUMER = {"z": 0, "gate": 1, "z_sb": 0, "gate2": 1, "hg": 0, "hq": 0, "hf": 0, "ff_gate": 1}
SIG_TILES = [g for g, (kind, _) in enumerate(TILES) if kind in SIGMOID]
FILLS = {"x": "A", "y": "B", "mix": "A", "heads": "B", "ffn": "A"}
TURN_SCALE = {"x": "norm_pre", "y": "ssd_norm", "mix": "norm_mix", "ffn": "norm_ffn"}
NORMS = ("x", "y", "out1", "mix", "qk", "kc", "hgrn", "ffn")
SPLIT_TILES = {"z_sb": "B", "ff_up": "B"}


def plan_splits():
    order, need, seen = [], {}, {"A": 0, "B": 0}

    def done(key, dst):
        order.append(key)
        seen[dst] = len(order)

    for s in STEPS:
        if s[0] == "turn":
            done(s, FILLS[s[1]])
        if s[0] == "merge":
            done(s, "A")
        if s[0] in ("gemm", "small"):
            srcs = "A" if s[0] == "small" else BLOCKS[s[1]]["srcs"]
            need[s[:2]] = max(seen[x] for x in srcs)
        if s[0] == "gemm":
            for g in BLOCKS[s[1]]["closes"]:
                if TILES[g][0] in SPLIT_TILES:
                    done(("tile", g), SPLIT_TILES[TILES[g][0]])
    return order, need


SPLITS, SPLIT_NEED = plan_splits()
PRODUCTS = [s for s in SPLITS if s[0] in ("tile", "merge")]


class Columns:

    def __init__(self, spans):
        self.spans, self.width = {}, 0
        for name, n in spans:
            self.spans[name] = slice(self.width, self.width + n)
            self.width += n

    def at(self, name):
        return self.spans[name]


CST = Columns([("ident", P), ("tri", P), ("ones", P)])
CSTB = Columns([("ident", P), ("strict", P), ("after", P)])
VEC = Columns([("norm_pre", 8), ("b_gate", 16), ("conv_w", 48), ("conv_b", 12), ("ssd_norm", 8), ("dt_bias", 16),
               ("a_log", 16), ("d_skip", 16), ("norm_mix", 8), ("norm_ffn", 8), ("q_norm", 1), ("k_norm", 3),
               ("lower", 8)])
CST2 = Columns([("w2", 2 * HD), ("pos", 2 * CL), ("heads", 4)])
CMASK0 = 540
HALVES = Columns([(f"level{i}", 256) for i in range(7)])
ARENA = 22528
STAT = 672
BANK_LOGITS, BANK_WT, BANK_O = 4, 6, 7


LATE = max(n for n, b in enumerate(BLOCKS) if b["w"] == "gate_sb") - 4
LAST_MIX = max(g for g, (kind, _) in enumerate(TILES) if kind == "turn_mix")
W1V = min(n for n, b in enumerate(BLOCKS) if b["w"] == "w_in_2")
HC = min(n for n, b in enumerate(BLOCKS) if TILES[b["tiles"][0]][0] == "hq") + 1
LAST_DOWN = len(TILES) - 8
KQV_READ = max(TILE_RING.ends[g][1] for g, (kind, _) in enumerate(TILES) if kind == "v")
MERGE_AFTER = max(n for n, b in enumerate(BLOCKS) if b["w"] == "gate_sb")


UNITS = 2 * NH * NT
TURNS = [s for s in SPLITS if s[0] == "turn"]


def last_read(kind):
    return max(TILE_RING.ends[g][1] for g, (k, _) in enumerate(TILES) if k == kind)


KCV_READ, QK_READ, GATES_READ, QN_READ = last_read("kcv"), last_read("turn_qk"), last_read("gates"), last_read("qn")
OUT1_READ, OUT2_READ = last_read("out1"), last_read("out2")
NORMED, _n = {}, 0
for _name, _k in (("x", 4), ("y", 4), ("out1", 4), ("mix", 4), ("qk", 16), ("kc", 1), ("hgrn", 4), ("ffn", 4)):
    _n += _k
    NORMED[_name] = _n
T_READY = [sum(s[0] == "tile" for s in PRODUCTS[:p + 1]) for p in range(len(PRODUCTS))]


def emit(nc, dram, out, debug=None):
    ctx = ExitStack()
    with ctx:
        def sb(name, shape, dt=F32):
            return ctx.enter_context(nc.sbuf_tensor(name, shape, dt))

        def sem(name):
            return ctx.enter_context(nc.semaphore(name))

        wraw = [sb(f"wraw{i}", [P, BLK]) for i in range(2)]
        whi = [sb(f"whi{i}", [P, BLK], F32R) for i in range(2)]
        wlo = [sb(f"wlo{i}", [P, BLK], F32R) for i in range(2)]
        swraw = sb("swraw", [P, NK * 24])
        swhi = sb("swhi", [P, NK * 24], F32R)
        swlo = sb("swlo", [P, NK * 24], F32R)
        a_hi, a_lo = sb("a_hi", [P, NK, T], F32R), sb("a_lo", [P, NK, T], F32R)
        b_hi, b_lo = sb("b_hi", [P, NK, T], F32R), sb("b_lo", [P, NK, T], F32R)
        ACTS = {"A": (a_hi, a_lo), "B": (b_hi, b_lo)}
        cst = sb("cst", [P, CST.width])
        cstb = sb("cstb", [P, CSTB.width], BF16)
        vec = sb("vec", [P, VEC.width])
        stat = sb("stat", [P, STAT])
        arena = sb("arena", [P, ARENA])

        def mem(kb, shape):
            n = int(np.prod(shape))
            v = arena[:, int(kb * 256):int(kb * 256) + n]
            assert kb * 256 + n <= ARENA, (kb, shape)
            if len(shape) == 2:
                v = v.rearrange("p (a b) -> p a b", b=shape[1])
            if len(shape) == 3:
                v = v.rearrange("p (a b c) -> p a b c", b=shape[1], c=shape[2])
            return v

        used = [0]

        def small(n):
            used[0] += n
            assert used[0] <= STAT
            return stat[:, used[0] - n:used[0]]

        bank = [ctx.enter_context(nc.psum_tensor(f"bank{i}", [P, 512], F32)) for i in range(8)]

        ident = cst[:, CST.at("ident")]
        tri = cst[:, CST.at("tri")]
        ones = cst[:, CST.at("ones")]
        w2 = cst[:, P:P + 2 * HD].rearrange("p (a b) -> p a b", b=HD)
        pos = cst[:, P + 2 * HD:P + 2 * HD + 2 * CL].rearrange("p (a b) -> p a b", b=CL)
        heads4 = cst[:, P + 2 * HD + 2 * CL:P + 2 * HD + 2 * CL + 4]
        identb = cstb[:, CSTB.at("ident")]
        strict = cstb[:, CSTB.at("strict")]
        after = cstb[:, CSTB.at("after")]

        def V(name, i=0, n=1):
            a = VEC.at(name).start
            return vec[:, a + i:a + i + n]

        xt = mem(72, [NT, D])
        zt = mem(0, [NT, D])
        xs = mem(16, [NT, D])
        bct = mem(32, [4, T])
        btok = mem(40, [NT, 256])
        state = mem(44, [2, 512])
        xdt = mem(48, [2, D])
        xdd = mem(56, [D])
        sc = mem(60, [2, P])
        ee = mem(61, [2, 4, P])
        ytmp = mem(65, [2, 512])
        kf = mem(72, [NK, T])
        qf = mem(16, [NK, T])
        vt = mem(32, [NT, D])
        mg = mem(0, [NK, T])
        cacc = mem(48, [2, T])
        csig = mem(52, [2, T])
        cx = mem(56, [2, T])
        junk = mem(60, [D])
        sgt = mem(68, [2, T])
        sb_sig = mem(48, [2, T])
        sb_fail = mem(52, [2 * 516])
        sb_w = mem(57, [2, T])
        sb_wT = mem(61, [2, T])
        zeros = mem(65, [T])
        tt = mem(48, [2, T])
        oraw = mem(16, [NT, D])
        xres = mem(32, [NT, D])
        npost = mem(52, [D])

        x1 = xres
        xn = mem(16, [NT, D])
        kvt = mem(0, [NT, 512])
        qt_ = mem(8, [NT, 512])
        qn_ = mem(64, [NT, 4, P])
        kcf = mem(48, [2, T])
        qT = mem(52, [4, T])
        kT = mem(60, [2, T])
        w1 = [mem(72, [CL, P]), mem(16, [CL, P])]
        cs_ = [mem(8 + i, [NH, 32]) for i in range(2)]
        cpT = mem(10, [2, 2, P])
        vcd = mem(12, [2, 4, HD])
        hid = mem(14, [2, 2, 32])
        hid4 = mem(8, [2, 4, 32])
        kcn = mem(14.5, [P])
        kcT = mem(15, [32])
        nsq = mem(15.25, [P])
        np_ = mem(64, [2, T])
        npT = mem(48, [2, T])
        ntmp = mem(8, [512])
        mixt = mem(72, [NT, D])
        hit = mem(16, [NT, 512])
        hgt = mem(24, [NT, 512])
        hset = [[mem(8 * i + 2 * j, [T]) for j in range(4)] for i in range(2)]
        hqk = [[mem(48 + 4 * i + 2 * j, [T]) for j in range(2)] for i in range(2)]
        hat = [mem(56 + 5 * i, [1280]) for i in range(2)]
        halves = mem(66, [7 * 64]).bitcast(U8)
        halves_f = mem(48, [7 * 256])
        hsq = mem(0, [512])
        sq_ = mem(64, [NT, 4, P])[:, 3, :, :].rearrange("p a b -> p (a b)")

        sso, rso = small(8), small(8)
        t8 = [small(8) for _ in range(2)]
        dt_ = small(64)
        adt = small(64)
        acs_n = small(64)
        ecs = small(64)
        edec = small(64)
        dtend = small(64)
        t64 = [small(64) for _ in range(3)]
        aexp = small(16)
        ssx, rsx = small(4), small(4)
        ssy, rsy = small(8), small(8)
        used[0] = 0
        nmx, nsum = small(64), small(64)
        onorm = stat[:, 0:P]
        gl = small(96)
        ss32, rs32 = small(48), small(48)
        cmx, csum = small(16), small(16)
        posb = small(2)
        kcs, kcr = small(2), small(2)
        lbs, lbn = small(4), small(4)
        f8 = small(16)
        hss, hrs = small(16), small(16)
        ss1, rs1 = small(8), small(8)
        t48 = small(48)
        cmask = stat[:, CMASK0:CMASK0 + P].rearrange("p (a b) -> p a b", b=32)
        assert used[0] <= CMASK0

        s_w = [sem(f"s_w{i}") for i in range(2)]
        s_sw = sem("s_small_weights")
        s_cst = sem("s_constants")
        s_x = sem("s_x")
        s_hi, s_lo = sem("s_weights_hi"), sem("s_weights_lo")
        s_shi, s_slo = sem("s_small_hi"), sem("s_small_lo")
        s_blk, s_tile = sem("s_block_used"), sem("s_tile_summed")
        s_small = sem("s_small_used")
        s_end = {"V": sem("s_tile_read_v"), "S": sem("s_tile_read_s")}
        s_split = sem("s_chunk_split")
        s_round = sem("s_chunk_rounded")
        s_sg = sem("s_sigmoid")
        s_conv, s_csig, s_cx, s_xt = sem("s_conv"), sem("s_conv_sigmoid"), sem("s_conv_silu"), sem("s_x_turned")
        s_aux = sem("s_aux_summed")
        s_auxend = {"V": sem("s_aux_read_v"), "S": sem("s_aux_read_s")}
        s_ss, s_rec, s_rt, s_norm = sem("s_squares"), sem("s_mean"), sem("s_root"), sem("s_normed")
        s_dt, s_dte, s_ex = sem("s_dt"), sem("s_dt_exp"), sem("s_decays")
        s_xd = sem("s_x_dt")
        s_attn, s_yd, s_y, s_st = sem("s_ssd_attn"), sem("s_y_diag"), sem("s_y_read"), sem("s_state")
        s_qk, s_sig, s_scan, s_wgt = sem("s_logits"), sem("s_sb_sigmoids"), sem("s_sb_products"), sem("s_sb_weights")
        s_tr, s_wT, s_pv, s_o = sem("s_sb_turned"), sem("s_sb_wT"), sem("s_sb_summed"), sem("s_sb_out")
        s_t, s_tround, s_mg = sem("s_product"), sem("s_product_rounded"), sem("s_merged")
        s_res, s_zero = sem("s_residual"), sem("s_zero")
        s_vc, s_ac, s_pc = sem("s_vector_chain"), sem("s_scalar_chain"), sem("s_pool_chain")
        s_out = sem("s_stored")
        s_hid4 = sem("s_hidden_repeated")
        s_hc_pos = sem("s_positions_hidden")
        s_late, s_w1v, s_hc = sem("s_late_constants"), sem("s_w1_v"), sem("s_hgrn_constants")
        s_hid, s_gelu, s_kc, s_kct, s_kcr, s_vcd = (sem("s_hidden"), sem("s_gelu"), sem("s_kc"), sem("s_kc_turned"),
                                                    sem("s_kc_read"), sem("s_vc_ready"))
        s_cqk, s_cs, s_ce, s_cp, s_ctr, s_cpt, s_cpv, s_cm = (
            sem("s_cmp_logits"), sem("s_cmp_shifted"), sem("s_cmp_exp"), sem("s_cmp_weights"), sem("s_cmp_turned"),
            sem("s_cmp_wT"), sem("s_cmp_summed"), sem("s_cmp_out"))
        s_nqk, s_nmx, s_np, s_ntr, s_npt, s_npv, s_nm = (
            sem("s_nsa_logits"), sem("s_nsa_max"), sem("s_nsa_exp"), sem("s_nsa_turned"), sem("s_nsa_wT"),
            sem("s_nsa_summed"), sem("s_nsa_out"))
        s_hlb, s_hin, s_hlev, s_hprod, s_hread, s_ho, s_hoc = (
            sem("s_lower"), sem("s_hgrn_inputs"), sem("s_hgrn_operands"), sem("s_hgrn_product"),
            sem("s_hgrn_product_read"), sem("s_hgrn_summed"), sem("s_hgrn_out"))

        f32 = lambda ap: ap.bitcast(F32)

        def width(n):
            return BLOCKS[n]["kn"] * sum(c for _, c in BLOCKS[n]["spans"])

        def used_by_pe(n):
            if BLOCKS[n]["closes"]:
                return s_tile, BLOCKS[n]["closes"][-1] + 1
            return s_blk, sum(not b["closes"] for b in BLOCKS[:n + 1])

        def sigmoid_ready(g):
            if READER[TILES[g][0]] == "S":
                return s_end["S"], TILE_RING.ends[g][1]
            return s_sg, sum(READER[TILES[x][0]] == "V" for x in SIG_TILES[:SIG_TILES.index(g) + 1])

        block = ctx.enter_context(nc.Block())

        @block.sync
        def _(sp):
            sp.dma_start(xt.rearrange("p a b -> p a b"), dram["x"].rearrange("(a p) d -> p a d", p=P)).then_inc(s_x, 16)
            sp.dma_start(vec[:, :], dram["vec"]).then_inc(s_cst, 16)
            sp.dma_start(cst[:, :], dram["cst"]).then_inc(s_cst, 16)
            sp.dma_start(cstb[:, :], dram["cstb"]).then_inc(s_cst, 16)
            sp.dma_start(swraw[:, 0:NK * SH], dram["w_dt"]).then_inc(s_sw, 16)
            for n, b in enumerate(BLOCKS):
                if n >= 2:
                    sp.wait_ge(s_lo, n - 1)
                cols = width(n)
                sp.dma_start(wraw[n % 2][:, 0:cols], dram["wblk"][n][:, 0:cols]).then_inc(s_w[n % 2], 16)
                if n == LATE:
                    sp.wait_ge(s_pv, SH * NT)
                    sp.dma_start(x1, dram["x"].rearrange("(a p) d -> p a d", p=P)).then_inc(s_res, 16)
                    sp.dma_start(npost, dram["norm_post"]).then_inc(s_res, 16)
                    sp.dma_start(w1[0].rearrange("p a b -> p (a b)"), dram["w1k"]).then_inc(s_late, 16)
                    sp.dma_start(cst[:, P:P + CST2.width], dram["cst2"]).then_inc(s_late, 16)
                    sp.dma_start(cstb[:, CSTB.at("after")], dram["upto"]).then_inc(s_late, 16)
                    sp.dma_start(stat[:, CMASK0:CMASK0 + P], dram["cmask"]).then_inc(s_late, 16)
                    sp.dma_start(swraw[:, :], dram["w_gates"]).then_inc(s_sw, 16)
                if n == W1V:
                    sp.wait_ge(s_tile, LAST_MIX + 1)
                    sp.dma_start(w1[1].rearrange("p a b -> p (a b)"), dram["w1v"]).then_inc(s_w1v, 16)
                if n == HC:
                    sp.wait_ge(s_nm, 2 * NT)
                    sp.dma_start(halves_f, dram["halves"]).then_inc(s_hc, 16)
                    sp.dma_start(onorm, dram["onorm"]).then_inc(s_hc, 16)
            for half in range(2):
                for t in range(NT):
                    sp.wait_ge(s_end["V"], TILE_RING.ends[LAST_DOWN + 4 * half + t][1])
                    sp.dma_start(out.rearrange("(a p) d -> p a d", p=P)[:, t, 512 * half:512 * half + 512],
                                 x1[:, t, 512 * half:512 * half + 512]).then_inc(s_out, 16)
            sp.wait_ge(s_out, 16 * 2 * NT)

        @block.tensor
        def _(pe):
            def mm(o, lhsT, rhs, start, stop, **kw):
                return nc.tensor.matmul(o, lhsT, rhs, start=start, stop=stop, **kw)

            def free_bank(g):
                if TILE_RING.before(g):
                    who, n = TILE_RING.before(g)
                    pe.wait_ge(s_end[who], n)

            def free_aux(key):
                if AUX.before(key):
                    who, n = AUX.before(key)
                    pe.wait_ge(s_auxend[who], n)
                return bank[4 + AUX.slot(key)]

            def gemm(n):
                b, slot = BLOCKS[n], n % 2
                pe.wait_ge(s_hi, n + 1)
                pe.wait_ge(s_lo, n + 1)
                pe.wait_ge(s_split, SPLIT_NEED[("gemm", n)])
                for j, g in enumerate(b["tiles"]):
                    xh, xl = ACTS[b["srcs"][j]]
                    ps = bank[TILE_RING.slot(g)]
                    if g in b["opens"]:
                        free_bank(g)
                    last = None
                    for k in range(b["kn"]):
                        if b["form"] == "feature":
                            w = slice(256 * k + P * j, 256 * k + P * j + P)
                            pairs = [(whi[slot][:, w], xh[:, k, :]), (whi[slot][:, w], xl[:, k, :]),
                                     (wlo[slot][:, w], xh[:, k, :])]
                            first, end = k == 0, k == b["kn"] - 1
                        else:
                            w, kk, ts = slice(512 * k, 512 * k + 512), b["kb"] + k, slice(P * j, P * j + P)
                            pairs = [(xh[:, kk, ts], whi[slot][:, w]), (xh[:, kk, ts], wlo[slot][:, w]),
                                     (xl[:, kk, ts], whi[slot][:, w])]
                            first, end = b["first"] and k == 0, b["last"] and k == b["kn"] - 1
                        for i, (l, r) in enumerate(pairs):
                            last = mm(ps[:, :], l, r, first and i == 0, end and i == 2)
                    if g in b["closes"]:
                        last.then_inc(s_tile, 1)
                if not b["closes"]:
                    last.then_inc(s_blk, 1)

            def turn(name, c, g):
                src = {"x": xt, "y": zt, "mix": xn, "heads": mixt, "ffn": xn}[name]
                if c == 0:
                    pe.wait_ge(s_cst, 48)
                    pe.wait_ge(s_norm, NORMED[{"heads": "hgrn"}.get(name, name)])
                free_bank(g)
                for t in range(NT):
                    last = nc.tensor.transpose(bank[TILE_RING.slot(g)][:, P * t:P * t + P], src[:, t, P * c:P * c + P], ident)
                last.then_inc(s_tile, 1)

            def small_block(kind, g, cols):
                pe.wait_ge(s_slo, 1 if kind == "dt" else 2)
                pe.wait_ge(s_split, SPLIT_NEED[("small", kind)])
                free_bank(g)
                ps = bank[TILE_RING.slot(g)]
                for t in range(NT):
                    for k in range(NK):
                        xh, xl = a_hi[:, k, P * t:P * t + P], a_lo[:, k, P * t:P * t + P]
                        h, l = swhi[:, cols * k:cols * k + cols], swlo[:, cols * k:cols * k + cols]
                        for i, (a, w) in enumerate(((xh, h), (xh, l), (xl, h))):
                            last = mm(ps[:, cols * t:cols * t + cols], a, w, k == 0 and i == 0, k == NK - 1 and i == 2)
                last.then_inc(s_tile, 1)

            def qkturn(i, g):
                if i == 0:
                    pe.wait_ge(s_norm, NORMED["qk"])
                free_bank(g)
                for t in range(NT):
                    src = qn_[:, t, i, :] if i < 4 else kvt[:, t, 256 * (i - 4):256 * (i - 4) + P]
                    last = nc.tensor.transpose(bank[TILE_RING.slot(g)][:, P * t:P * t + P], src, ident)
                last.then_inc(s_tile, 1)

            def compress():
                pe.wait_ge(s_late, 64)
                pe.wait_ge(s_w1v, 16)
                pe.wait_ge(s_end["S"], KCV_READ)
                for b in range(2):
                    for l in range(CL):
                        for g in range(NG):
                            rows = slice(HD * g, HD * g + HD)
                            mm(bank[4 + g][:, 32 * b:32 * b + NCMP], w1[b][rows, l, :],
                               kcf[rows, b, l:l + CS * (NCMP - 1) + 1:CS], l == 0, l == CL - 1)
                    for l in range(CL):
                        last = mm(bank[4][:, P + b:P + b + 1], w1[b][0:HD, l, :], pos[0:HD, b, l:l + 1], l == 0, l == CL - 1)
                last.then_inc(s_hid, 1)
                pe.wait_ge(s_gelu, 4)
                for g in range(NG):
                    last = mm(bank[6][0:32, HD * g:HD * g + HD], hid[:, 0, g, :], w2[:, 0, :], True, True)
                last.then_inc(s_hid, 1)
                pe.wait_ge(s_hid4, NG)
                for g in range(NG):
                    last = mm(bank[7][:, HD * g:HD * g + HD], hid4[:, g, :, :].rearrange("p a b -> p (a b)"),
                              w2[:, 1, :], True, True)
                last.then_inc(s_hid, 1)
                pe.wait_ge(s_norm, NORMED["kc"])
                nc.tensor.transpose(bank[4][:, 0:32], kcn[0:32, :], ident[0:32, 0:32]).then_inc(s_kct, 1)

            def cmp(qt):
                pe.wait_ge(s_kcr, 1)
                if qt == 0:
                    pe.wait_ge(s_vcd, 1)
                pe.wait_ge(s_end["S"], QK_READ)
                if qt >= 1:
                    pe.wait_ge(s_cs, qt)
                for h in range(NH):
                    g, r = divmod(h, 4)
                    rows = slice(HD * g, HD * g + HD)
                    last = mm(bank[4 + 3 * g][:, 32 * r:32 * r + NCMP], qT[rows, r, P * qt:P * qt + P], kcT[rows, 0:NCMP], True, True)
                last.then_inc(s_cqk, 1)
                pe.wait_ge(s_cp, qt + 1)
                for g in range(NG):
                    last = nc.tensor.transpose(bank[5][:, P * g:P * g + P],
                                               cs_[qt % 2][:, 4 * g:4 * g + 4, :].rearrange("p a b -> p (a b)"), ident)
                last.then_inc(s_ctr, 1)
                pe.wait_ge(s_cpt, qt + 1)
                if qt >= 1:
                    pe.wait_ge(s_cm, qt)
                for g in range(NG):
                    last = mm(bank[6][:, 256 * g:256 * g + 256], cpT[:, qt % 2, g, :],
                              vcd[:, g, :, :].rearrange("p a b -> p (a b)"), True, True)
                last.then_inc(s_cpv, 1)

            def nsa(u):
                if u < UNITS:
                    qt, b, h = u // 16, u // 8 % 2, u % 8
                    g, r = divmod(h, 4)
                    rows, kend = slice(HD * g, HD * g + HD), P * (qt + 1)
                    if u == 0:
                        pe.wait_ge(s_cm, NT)
                    if u >= 2:
                        pe.wait_ge(s_np, u - 1)
                    ps = bank[BANK_LOGITS + u % 2]
                    mm(ps[:, 0:kend], qT[rows, r, P * qt:P * qt + P], kT[rows, b, 0:kend], True, False)
                    mm(ps[:, kend - P:kend], identb, after, False, True).then_inc(s_nqk, 1)
                v = u - 1
                if 0 <= v < UNITS:
                    pe.wait_ge(s_np, v + 1)
                    if v >= 1:
                        pe.wait_ge(s_npt, v)
                    for kb in range(v // 16 + 1):
                        last = nc.tensor.transpose(bank[BANK_WT][:, P * kb:P * kb + P], np_[:, v % 2, P * kb:P * kb + P], ident)
                    last.then_inc(s_ntr, 1)
                v = u - 2
                if 0 <= v < UNITS:
                    qt, b, h = v // 16, v // 8 % 2, v % 8
                    pe.wait_ge(s_npt, v + 1)
                    if h == 0 and v >= 8:
                        pe.wait_ge(s_nm, v // 8)
                    for kb in range(qt + 1):
                        last = mm(bank[BANK_O][:, HD * h:HD * h + HD], npT[:, v % 2, P * kb:P * kb + P],
                                  kvt[:, kb, 256 * b + P + HD * (h // 4):256 * b + P + HD * (h // 4) + HD], kb == 0, kb == qt)
                    last.then_inc(s_npv, 1)

            def hgrn(h):
                hq_, hk_ = hset[h % 2][0], hset[h % 2][1]
                at = hat[h % 2]
                for n in range(LEVELS + 1):
                    m = (LEVELS + 1) * h + n
                    pe.wait_ge(s_hlev, m + 1)
                    if m >= 2:
                        pe.wait_ge(s_hread, m - 1)
                    ps = bank[4 + m % 2]
                    if n == 0:
                        for t in range(NT):
                            ts = slice(P * t, P * t + P)
                            last = mm(ps[:, ts], hk_[:, ts], hq_[:, ts], True, True)
                    else:
                        w = 2 ** (n - 1)
                        q_, k_ = hqk[m % 2]
                        if w < P:
                            up = lambda ap: ap.rearrange("p (a b c) -> p a b c", b=2, c=w)[:, :, 1, :]
                            for t in range(NT):
                                ts = slice(P * t, P * t + P)
                                last = mm(up(ps[:, ts]), k_[:, ts], up(q_[:, ts]), True, True)
                        elif w == P:
                            for i in range(2):
                                last = mm(ps[:, P * i:P * i + P], k_[:, 2 * P * i:2 * P * i + P],
                                          q_[:, 2 * P * i + P:2 * P * i + 2 * P], True, True)
                        else:
                            for i in range(2):
                                last = mm(ps[:, 256 * i:256 * i + 256], k_[:, P * i:P * i + P], q_[:, 256:512], True, True)
                    last.then_inc(s_hprod, 1)
                pe.wait_ge(s_hread, (LEVELS + 1) * (h + 1))
                if h >= 2:
                    pe.wait_ge(s_hoc, h - 1)
                for t in range(NT):
                    for s_ in range(t + 1):
                        if s_ == t:
                            lhs = at[:, P * t:P * t + P]
                        elif t >= 2 and s_ < 2:
                            lhs = at[:, 768 + 256 * s_ + P * (t - 2):768 + 256 * s_ + P * (t - 2) + P]
                        else:
                            lhs = at[:, 512 + P * (t // 2):512 + P * (t // 2) + P]
                        last = mm(bank[6 + h % 2][:, P * t:P * t + P], lhs, hit[:, s_, P * h:P * h + P], s_ == 0, s_ == t)
                last.then_inc(s_ho, 1)

            def xturn(c):
                pe.wait_ge(s_cx, c + 1)
                ps = free_aux(("xturn", c))
                src = cx[:, c % 2, :] if c < 8 else bct[:, c - 8, :]
                for t in range(NT):
                    last = nc.tensor.transpose(ps[:, P * t:P * t + P], src[:, P * t:P * t + P], ident)
                last.then_inc(s_aux, 1)

            def ssd_decay():
                pe.wait_ge(s_dt, 1)
                ps = free_aux("decay")
                mm(ps[:, 0:64], tri, adt, True, True)
                mm(ps[:, 64:128], ones, adt, True, True).then_inc(s_aux, 1)

            def ssd(c, part):
                ts = slice(P * c, P * c + P)

                def y_diag(j):
                    pe.wait_ge(s_attn, 4 * c + j + 1)
                    if j == 0:
                        pe.wait_ge(s_xd, 2 * c + 1)
                        if c >= 1:
                            pe.wait_ge(s_y, c)
                    for i in range(4):
                        h = 4 * j + i
                        last = mm(bank[6 + j // 2][:, (h % 8) * HD:(h % 8) * HD + HD], ee[:, j % 2, i, :],
                                  xdt[:, c % 2, h * HD:h * HD + HD], True, True)
                    last.then_inc(s_yd, 1)

                if part == 0:
                    pe.wait_ge(s_cx, XC)
                    ps = free_aux(("scores", c))
                    for g in range(2):
                        last = mm(ps[:, P * g:P * g + P], bct[:, g, ts], bct[:, 2 + g, ts], True, True)
                    last.then_inc(s_aux, 1)
                if part < 4:
                    pe.wait_ge(s_dt, 1)
                    ps = free_aux(("decay", c, part))
                    mm(ps[:, :], identb, after.unsqueeze(1).to_broadcast([P, 4, P]), True, False)
                    for i in range(4):
                        col = SH * c + 4 * part + i
                        last = mm(ps[:, P * i:P * i + P], adt[:, col:col + 1].to_broadcast([P, P]), tri, False, i == 3)
                    last.then_inc(s_aux, 1)
                    if part >= 1:
                        y_diag(part - 1)
                if part == 4:
                    if c > 0:
                        pe.wait_ge(s_st, 2 * c)
                        for g in range(2):
                            ps = free_aux(("y_off", c, g))
                            mm(ps[:, :], bct[:, 2 + g, ts], state[:, g, :], True, True).then_inc(s_aux, 1)
                    y_diag(3)
                    if c < NT - 1:
                        pe.wait_ge(s_xd, 2 * c + 2)
                        for g in range(2):
                            ps = free_aux(("state", c, g))
                            mm(ps[:, :], btok[:, c, P * g:P * g + P], xdd[:, 512 * g:512 * g + 512], True, True)\
                                .then_inc(s_aux, 1)

            def stick(u):
                if u < SH * NT:
                    h, qt = divmod(u, NT)
                    rows, kend = slice(HD * (h % 2), HD * (h % 2) + HD), P * (qt + 1)
                    if u >= 2:
                        pe.wait_ge(s_sig, u - 1)
                    ps = bank[BANK_LOGITS + u % 2]
                    if u == 0:
                        pe.wait_ge(s_end["S"], KQV_READ)
                        pe.wait_ge(s_y, NT)
                    mm(ps[:, 0:kend], qf[rows, h // 2, P * qt:P * qt + P], kf[rows, h // 2, 0:kend], True, False)
                    mm(ps[:, kend - P:kend], identb, strict, False, True).then_inc(s_qk, 1)
                v = u - 1
                if 0 <= v < SH * NT:
                    pe.wait_ge(s_wgt, v + 1)
                    if v >= 1:
                        pe.wait_ge(s_wT, v)
                    for kb in range(v % NT + 1):
                        last = nc.tensor.transpose(bank[BANK_WT][:, P * kb:P * kb + P], sb_w[:, v % 2, P * kb:P * kb + P], ident)
                    last.then_inc(s_tr, 1)
                v = u - 2
                if 0 <= v < SH * NT:
                    h, qt = divmod(v, NT)
                    rows = slice(HD * (h % 2), HD * (h % 2) + HD)
                    pe.wait_ge(s_wT, v + 1)
                    if v >= 1:
                        pe.wait_ge(s_o, v)
                    for kb in range(qt + 1):
                        last = mm(bank[BANK_O][rows, P * (v % 4):P * (v % 4) + P], vt[:, kb, h * HD:h * HD + HD],
                                  sb_wT[:, v % 2, P * kb:P * kb + P], kb == 0, kb == qt)
                    last.then_inc(s_pv, 1)

            for s in STEPS:
                if s[0] == "gemm":
                    gemm(s[1])
                if s[0] == "turn":
                    turn(*s[1:])
                if s[0] == "small":
                    small_block(s[1], s[2], SH if s[1] == "dt" else 24)
                if s[0] == "qkturn":
                    qkturn(*s[1:])
                if s[0] == "compress":
                    compress()
                if s[0] == "cmp":
                    cmp(s[1])
                if s[0] == "nsa":
                    nsa(s[1])
                if s[0] == "hgrn":
                    hgrn(s[1])
                if s[0] == "xturn":
                    xturn(s[1])
                if s[0] == "ssd_decay":
                    ssd_decay()
                if s[0] == "ssd":
                    ssd(s[1], s[2])
                if s[0] == "sb":
                    stick(s[1])

        @block.scalar
        def _(act):
            A = nc.scalar.activation
            chain = [0]

            def link(ins):
                chain[0] += 1
                ins.then_inc(s_ac, 1)
                act.wait_ge(s_ac, chain[0])

            def round_weights(n):
                if n >= NB:
                    return
                act.wait_ge(s_w[n % 2], 16 * (n // 2 + 1))
                if n >= 2:
                    act.wait_ge(*used_by_pe(n - 2))
                cols = width(n)
                A(whi[n % 2][:, 0:cols], wraw[n % 2][:, 0:cols], ACT.Copy).then_inc(s_hi, 1)

            def sigmoid(g, kind, i):
                k = SIG_TILES.index(g)
                if k >= 2:
                    o = SIG_TILES[k - 2]
                    who, n = TILE_RING.ends[o + CONSUMER[TILES[o][0]]]
                    act.wait_ge(s_end[who], n)
                bias = 0.0
                if kind in ("gate", "gate2"):
                    bias = V("b_gate", i + (8 if kind == "gate2" else 0))
                ins = A(sgt[:, k % 2, :], bank[TILE_RING.slot(g)][:, :], ACT.Sigmoid, bias=bias)
                ins.then_inc(s_end["S"] if READER[kind] == "S" else s_sg, 1)

            def tile(g):
                kind, i = TILES[g]
                ps = bank[TILE_RING.slot(g)]
                if kind in ("dt", "y_ssd", "y_sb", "out2", "down"):
                    return
                if kind == "xbc":
                    act.wait_ge(s_conv, i + 1)
                    if i >= 2:
                        act.wait_ge(s_cx, i - 1)
                    A(csig[:, i % 2, :], cacc[:, i % 2, :], ACT.Sigmoid).then_inc(s_csig, 1)
                    return
                act.wait_ge(s_tile, g + 1)
                if kind in SIGMOID:
                    sigmoid(g, kind, i)
                if kind in ("z_sb", "ff_up"):
                    p = PRODUCTS.index(("tile", g))
                    act.wait_ge(s_t, T_READY[p])
                    c = i if kind == "z_sb" else i[1]
                    A(b_hi[:, c, :], tt[:, p % 2, :], ACT.Copy).then_inc(s_tround, 1)
                if kind in ("kv", "qn"):
                    A({"kv": kvt, "qn": qt_}[kind][:, i[0], :], ps[:, :], ACT.Copy).then_inc(s_end["S"], 1)
                if kind == "kcv":
                    A(kcf[:, i, :], ps[:, :], ACT.Copy).then_inc(s_end["S"], 1)
                if kind == "hi":
                    A(hit[:, i[0], :], ps[:, :], ACT.Copy).then_inc(s_end["S"], 1)
                if kind == "k":
                    A(kf[:, i, :], ps[:, :], ACT.Copy).then_inc(s_end["S"], 1)
                if kind == "q":
                    if i == 0:
                        act.wait_ge(s_yd, 4 * NT)
                        act.wait_ge(s_y, NT)
                    A(qf[:, i, :], ps[:, :], ACT.Copy).then_inc(s_end["S"], 1)
                if kind == "v":
                    t, half = i
                    A(vt[:, t, 512 * half:512 * half + 512], ps[:, :], ACT.Copy).then_inc(s_end["S"], 1)
                if kind == "out1":
                    t, half = i
                    A(oraw[:, t, 512 * half:512 * half + 512], ps[:, :], ACT.Copy)
                    if i == (0, 0):
                        act.wait_ge(s_mg, NK)
                    link(A(sgt[:, 0, :], ps[:, :], ACT.Square, accum_out=sso[:, 2 * t + half:2 * t + half + 1]))
                    act.sem_inc(s_end["S"], 1)

            def norm(name):
                if name == "x":
                    act.wait_ge(s_x, 16)
                    for t in range(NT):
                        link(A(junk, xt[:, t, :], ACT.Square, accum_out=ssx[:, t:t + 1]))
                    act.sem_inc(s_ss, 1)
                if name == "y":
                    act.wait_ge(s_y, NT)
                    for t in range(NT):
                        for g in range(2):
                            link(A(ytmp[:, 0, :], zt[:, t, 512 * g:512 * g + 512], ACT.Square,
                                   accum_out=ssy[:, 2 * t + g:2 * t + g + 1]))
                    act.sem_inc(s_ss, 1)
                if name in ("mix", "ffn"):
                    act.wait_ge(s_norm, NORMED["out1"]) if name == "mix" else \
                        act.wait_ge(s_end["V"], OUT2_READ)
                    for t in range(NT):
                        link(A(xn[:, 0, :], x1[:, t, :], ACT.Square, accum_out=ss1[:, t:t + 1]))
                    act.sem_inc(s_ss, 1)
                n = NORMS.index(name)
                act.wait_ge(s_rec, n + 1)
                r = {"x": rsx, "y": rsy, "out1": rso[:, 0:4], "mix": rs1[:, 0:4], "ffn": rs1[:, 0:4], "qk": rs32,
                     "kc": kcr[0:32, :], "hgrn": hrs}[name]
                A(r, r, ACT.Sqrt).then_inc(s_rt, 1)

            def turn(name, c, g):
                act.wait_ge(s_cst, 48)
                act.wait_ge(s_tile, g + 1)
                dst = ACTS[FILLS[name]][0]
                A(dst[:, c, :], bank[TILE_RING.slot(g)][:, :], ACT.Copy,
                  scale=V(TURN_SCALE[name], c) if name in TURN_SCALE else 1.0).then_inc(s_round, 1)

            def stick(u):
                if u < SH * NT:
                    kend = P * (u % NT + 1)
                    act.wait_ge(s_qk, u + 1)
                    if u >= 2:
                        act.wait_ge(s_wgt, u - 1)
                    ps = bank[BANK_LOGITS + u % 2]
                    f0 = 516 * (u % 2)
                    if u < 2:
                        act.wait_ge(s_zero, 1)
                    A(sb_sig[:, u % 2, 0:kend], ps[:, 0:kend], ACT.Sigmoid, scale=SCALE)
                    A(sb_fail[:, f0 + 512 - kend:f0 + 512], ps[:, 0:kend], ACT.Sigmoid, scale=-SCALE).then_inc(s_sig, 1)
                v = u - 1
                if 0 <= v < SH * NT:
                    kend = P * (v % NT + 1)
                    act.wait_ge(s_tr, v + 1)
                    if v >= 2:
                        act.wait_ge(s_pv, v - 1)
                    A(sb_wT[:, v % 2, 0:kend], bank[BANK_WT][:, 0:kend], ACT.Copy).then_inc(s_wT, 1)

            def small_block(kind, g):
                cols = NK * (SH if kind == "dt" else 24)
                act.wait_ge(s_sw, 16 if kind == "dt" else 32)
                if kind == "gates":
                    act.wait_ge(s_tile, g)
                A(swhi[:, 0:cols], swraw[:, 0:cols], ACT.Copy).then_inc(s_shi, 1)
                if kind == "dt":
                    act.wait_ge(s_dte, 1)
                    A(t64[1], t64[1], ACT.Exp).then_inc(s_ex, 1)
                    A(aexp, V("a_log", 0, SH), ACT.Exp).then_inc(s_ex, 1)
                    act.wait_ge(s_dte, 2)
                    A(t64[1], t64[1], ACT.Ln).then_inc(s_ex, 1)
                else:
                    act.wait_ge(s_tile, g + 1)
                    A(gl, bank[TILE_RING.slot(g)][:, 0:96], ACT.Sigmoid).then_inc(s_end["S"], 1)
                    act.wait_ge(s_hlb, 1)
                    A(lbs, lbs, ACT.Sigmoid).then_inc(s_hlb, 1)

            def compress():
                act.wait_ge(s_hc_pos, 1)
                for b in range(2):
                    for g in range(NG):
                        A(hid[:, b, g, 0:NCMP], bank[4 + g][:, 32 * b:32 * b + NCMP], ACT.Gelu_apprx_tanh,
                          bias=posb[:, b:b + 1]).then_inc(s_gelu, 1)
                norm("kc")
                act.wait_ge(s_kct, 1)
                A(kcT, bank[4][:, 0:32], ACT.Copy, scale=V("k_norm", 0)).then_inc(s_kcr, 1)

            def cmp(qt):
                act.wait_ge(s_cs, qt + 1)
                A(cs_[qt % 2][:, :, :], cs_[qt % 2][:, :, :], ACT.Exp, scale=SCALE).then_inc(s_ce, 1)
                act.wait_ge(s_ctr, qt + 1)
                if qt >= 2:
                    act.wait_ge(s_cpv, qt - 1)
                A(cpT[:, qt % 2, :, :], bank[5][:, 0:256].rearrange("p (a b) -> p a b", b=P), ACT.Copy).then_inc(s_cpt, 1)

            def nsa(u):
                if u < UNITS:
                    kend = P * (u // 16 + 1)
                    act.wait_ge(s_nmx, u + 1)
                    if u >= 2:
                        act.wait_ge(s_ntr, u - 1)
                    A(np_[:, u % 2, 0:kend], bank[BANK_LOGITS + u % 2][:, 0:kend], ACT.Exp, scale=SCALE,
                      bias=nmx[:, u:u + 1], accum_out=nsum[:, u:u + 1]).then_inc(s_np, 1)
                v = u - 1
                if 0 <= v < UNITS:
                    kend = P * (v // 16 + 1)
                    act.wait_ge(s_ntr, v + 1)
                    if v >= 2:
                        act.wait_ge(s_npv, v - 1)
                    A(npT[:, v % 2, 0:kend], bank[BANK_WT][:, 0:kend], ACT.Copy).then_inc(s_npt, 1)

            round_weights(0)
            for s in STEPS:
                if s[0] == "small":
                    small_block(s[1], s[2])
                if s[0] == "qkturn":
                    i, g = s[1:]
                    act.wait_ge(s_tile, g + 1)
                    dst = qT[:, i, :] if i < 4 else kT[:, i - 4, :]
                    A(dst, bank[TILE_RING.slot(g)][:, :], ACT.Copy,
                      scale=V("q_norm") if i < 4 else V("k_norm", i - 3)).then_inc(s_end["S"], 1)
                if s[0] == "compress":
                    compress()
                if s[0] == "cmp":
                    cmp(s[1])
                if s[0] == "nsa":
                    nsa(s[1])
                if s[0] == "hgrn":
                    h = s[1]
                    act.wait_ge(s_ho, h + 1)
                    A(mixt[:, :, 512 + P * h:512 + P * h + P],
                      bank[6 + h % 2][:, :].rearrange("p (a b) -> p a b", b=P), ACT.Copy).then_inc(s_hoc, 1)
                if s[0] == "norm":
                    norm(s[1])
                if s[0] == "turn":
                    turn(*s[1:])
                if s[0] == "gemm":
                    round_weights(s[1] + 1)
                    for g in BLOCKS[s[1]]["closes"]:
                        tile(g)
                if s[0] == "xturn":
                    c = s[1]
                    act.wait_ge(s_aux, AUX.at[("xturn", c)] + 1)
                    dst = xs[:, :, P * c:P * c + P] if c < 8 else btok[:, :, P * (c - 8):P * (c - 8) + P]
                    A(dst, bank[4 + AUX.slot(("xturn", c))][:, :].rearrange("p (a b) -> p a b", b=P), ACT.Copy)\
                        .then_inc(s_auxend["S"], 1)
                if s[0] == "ssd_decay":
                    act.wait_ge(s_dte, 3)
                    A(ecs, t64[0], ACT.Exp)
                    A(edec, t64[1], ACT.Exp)
                    A(dtend, t64[2], ACT.Exp).then_inc(s_ex, 1)
                if s[0] == "ssd" and s[2] < 4:
                    _, c, j = s
                    key = ("decay", c, j)
                    act.wait_ge(s_aux, AUX.at[key] + 1)
                    n = 4 * c + j
                    if n >= 2:
                        act.wait_ge(s_yd, n - 1)
                    for i in range(4):
                        col = SH * c + 4 * j + i
                        last = A(ee[:, j % 2, i, :], bank[4 + AUX.slot(key)][:, P * i:P * i + P], ACT.Exp,
                                 bias=acs_n[:, col:col + 1])
                    last.then_inc(s_auxend["S"], 1)
                if s[0] == "sb":
                    stick(s[1])
                if s[0] == "merge":
                    c = s[1]
                    if c == 0:
                        act.wait_ge(*used_by_pe(MERGE_AFTER))
                        act.wait_ge(s_mg, NK)
                    A(a_hi[:, c, :], mg[:, c, :], ACT.Copy).then_inc(s_tround, 1)

        @block.vector
        def _(dve):
            v = nc.vector
            chain = [0]

            def link(ins):
                chain[0] += 1
                ins.then_inc(s_vc, 1)
                dve.wait_ge(s_vc, chain[0])

            def rest_of_weights(n):
                if n >= NB:
                    return
                dve.wait_ge(s_hi, n + 1)
                cols = width(n)
                v.tensor_tensor(wlo[n % 2][:, 0:cols], wraw[n % 2][:, 0:cols], f32(whi[n % 2][:, 0:cols]),
                                ALU.subtract).then_inc(s_lo, 1)

            def tile(g):
                kind, i = TILES[g]
                ps = bank[TILE_RING.slot(g)]
                if kind == "xbc":
                    dve.wait_ge(s_tile, g + 1)
                    if i == 0:
                        dve.wait_ge(s_cst, 48)
                    if i >= 2:
                        dve.wait_ge(s_csig, i - 1)
                    acc = cacc[:, i % 2, :]
                    link(v.tensor_scalar(acc, ps[:, :], V("conv_w", 4 * i + 3), V("conv_b", i), ALU.mult, ALU.add))
                    for j in (1, 2, 3):
                        ins = v.scalar_tensor_tensor(acc[:, j:T], ps[:, 0:T - j], V("conv_w", 4 * i + 3 - j),
                                                     acc[:, j:T], ALU.mult, ALU.add)
                        if j < 3:
                            link(ins)
                    ins.then_inc(s_conv, 1)
                    dve.wait_ge(s_conv, i + 1)
                    dve.sem_inc(s_end["V"], 1)
                    dve.wait_ge(s_csig, i + 1)
                    if 2 <= i < 10:
                        dve.wait_ge(s_aux, AUX.at[("xturn", i - 2)] + 1)
                    dst = cx[:, i % 2, :] if i < 8 else bct[:, i - 8, :]
                    v.tensor_tensor(dst, acc, csig[:, i % 2, :], ALU.mult).then_inc(s_cx, 1)
                if kind == "z":
                    t, half = i
                    dve.wait_ge(*sigmoid_ready(g))
                    v.tensor_tensor(zt[:, t, 512 * half:512 * half + 512], ps[:, :], sgt[:, SIG_TILES.index(g) % 2, :],
                                    ALU.mult).then_inc(s_end["V"], 1)
                if kind in ("y_ssd", "y_sb"):
                    dve.wait_ge(s_tile, g + 1)
                    k = SIG_TILES.index(g - 1)
                    dve.wait_ge(*sigmoid_ready(g - 1))
                    sg = sgt[:, k % 2, :]
                    if kind == "y_ssd":
                        v.tensor_tensor(mg[:, i, :], ps[:, :], sg, ALU.mult).then_inc(s_end["V"], 1)
                    else:
                        link(v.tensor_tensor(sg, ps[:, :], sg, ALU.mult))
                        v.tensor_tensor(mg[:, i, :], mg[:, i, :], sg, ALU.add).then_inc(s_mg, 1)
                        dve.wait_ge(s_mg, i + 1)
                        dve.sem_inc(s_end["V"], 1)
                if kind == "hg":
                    dve.wait_ge(*sigmoid_ready(g))
                    v.tensor_tensor(hgt[:, i[0], :], ps[:, :], sgt[:, SIG_TILES.index(g) % 2, :], ALU.mult)\
                        .then_inc(s_end["V"], 1)
                if kind == "hq":
                    dve.wait_ge(*sigmoid_ready(g))
                    if i == 0:
                        dve.wait_ge(s_nm, 2 * NT)
                    if i >= 2:
                        dve.wait_ge(s_ho, i - 1)
                    v.tensor_tensor(hset[i % 2][0], ps[:, :], sgt[:, SIG_TILES.index(g) % 2, :], ALU.mult)\
                        .then_inc(s_end["V"], 1)
                if kind == "hf":
                    dve.wait_ge(*sigmoid_ready(g))
                    _, hk_, pre, suf = hset[i % 2]
                    link(v.tensor_scalar(pre, sgt[:, SIG_TILES.index(g) % 2, :], lbn[:, i:i + 1], lbs[:, i:i + 1],
                                         ALU.mult, ALU.add))
                    dve.sem_inc(s_end["V"], 1)
                    v.tensor_scalar(hk_, pre, -1.0, 1.0, ALU.mult, ALU.add)
                    link(v.memset(suf, 1.0))
                    dve.sem_inc(s_hin, 1)
                if kind in ("out2", "down"):
                    t, half = i if kind == "out2" else (i[0], i[1][1])
                    dve.wait_ge(s_tile, g + 1)
                    x = x1[:, t, 512 * half:512 * half + 512]
                    v.tensor_tensor(x, x, ps[:, :], ALU.add).then_inc(s_end["V"], 1)
                if kind == "ff_gate":
                    dve.wait_ge(*sigmoid_ready(g))
                    sg = sgt[:, SIG_TILES.index(g) % 2, :]
                    link(v.tensor_tensor(sg, sg, ps[:, :], ALU.mult))
                    dve.sem_inc(s_end["V"], 1)
                if kind == "ff_up":
                    p = PRODUCTS.index(("tile", g))
                    dve.wait_ge(s_tile, g + 1)
                    sg = sgt[:, SIG_TILES.index(g - 1) % 2, :]
                    v.tensor_tensor(tt[:, p % 2, :], sg, ps[:, :], ALU.mult).then_inc(s_t, 1)
                    dve.wait_ge(s_t, T_READY[p])
                    dve.sem_inc(s_end["V"], 1)
                    dve.wait_ge(s_tround, p + 1)
                    v.tensor_tensor(b_lo[:, i[1], :], tt[:, p % 2, :], f32(b_hi[:, i[1], :]), ALU.subtract).then_inc(s_split, 1)
                if kind == "z_sb":
                    k = SIG_TILES.index(g)
                    p = PRODUCTS.index(("tile", g))
                    dve.wait_ge(*sigmoid_ready(g))
                    if i == 0:
                        dve.wait_ge(s_tr, SH * NT)
                    link(v.tensor_tensor(sgt[:, k % 2, :], ps[:, :], sgt[:, k % 2, :], ALU.mult))
                    v.tensor_tensor(tt[:, p % 2, :], qf[:, i, :], sgt[:, k % 2, :], ALU.mult).then_inc(s_t, 1)
                    dve.wait_ge(s_t, T_READY[p])
                    dve.sem_inc(s_end["V"], 1)
                    dve.wait_ge(s_tround, p + 1)
                    v.tensor_tensor(b_lo[:, i, :], tt[:, p % 2, :], f32(b_hi[:, i, :]), ALU.subtract).then_inc(s_split, 1)

            def norm(name):
                n = NORMS.index(name)
                h64 = lambda ap: ap.rearrange("p (a b) -> p a b", b=HD)
                if name == "out1":
                    dve.wait_ge(s_end["S"], OUT1_READ)
                    link(v.tensor_tensor(t8[0][:, 0:4], sso.rearrange("p (a b) -> p b a", b=2)[:, 0, :],
                                         sso.rearrange("p (a b) -> p b a", b=2)[:, 1, :], ALU.add))
                    ss, r, w = t8[0][:, 0:4], rso[:, 0:4], D
                elif name in ("x", "y", "mix", "ffn"):
                    dve.wait_ge(s_ss, ("x", "y", "mix", "ffn").index(name) + 1)
                    ss, r, w = {"x": (ssx, rsx, D), "y": (ssy, rsy, 512)}.get(name, (ss1[:, 0:4], rs1[:, 0:4], D))
                elif name == "qk":
                    dve.wait_ge(s_end["S"], QN_READ)
                    for t in range(NT):
                        link(v.tensor_tensor(sq_, qt_[:, t, :], qt_[:, t, :], ALU.mult))
                        link(v.tensor_reduce(ss32[:, 12 * t:12 * t + 8], h64(sq_), AX.X, ALU.add))
                        k = kvt[:, t, :].rearrange("p (a b) -> p a b", b=256)[:, :, 0:P]
                        k2 = sq_[:, 0:256].rearrange("p (a b) -> p a b", b=P)
                        link(v.tensor_tensor(k2, k, k, ALU.mult))
                        link(v.tensor_reduce(ss32[:, 12 * t + 8:12 * t + 12], h64(sq_[:, 0:256]), AX.X, ALU.add))
                    ss, r, w = ss32, rs32, HD
                elif name == "kc":
                    dve.wait_ge(s_hid, 2)
                    link(v.tensor_copy(kcn[0:32, :], bank[6][0:32, 0:P]))
                    link(v.tensor_tensor(nsq[0:32, :], kcn[0:32, :], kcn[0:32, :], ALU.mult))
                    link(v.tensor_reduce(kcs[0:32, :], h64(nsq[0:32, :]), AX.X, ALU.add))
                    ss, r, w = kcs[0:32, :], kcr[0:32, :], HD
                else:
                    dve.wait_ge(s_hoc, HH)
                    for t in range(NT):
                        o = mixt[:, t, 512:1024]
                        link(v.tensor_tensor(hsq, o, o, ALU.mult))
                        link(v.tensor_reduce(hss[:, 4 * t:4 * t + 4], hsq.rearrange("p (a b) -> p a b", b=P), AX.X, ALU.add))
                    ss, r, w = hss, hrs, P
                m = t48[0:r.shape[0], 0:r.shape[1]] if NORMS.index(name) > 2 else t8[1][:, 0:r.shape[1]]
                link(v.tensor_scalar(m, ss, 1.0 / w, EPS, ALU.mult, ALU.add))
                v.reciprocal(r, m).then_inc(s_rec, 1)
                dve.wait_ge(s_rt, n + 1)
                if name in ("mix", "ffn"):
                    for t in range(NT):
                        v.tensor_scalar(xn[:, t, :], x1[:, t, :], rs1[:, t:t + 1], None, ALU.mult).then_inc(s_norm, 1)
                if name == "qk":
                    for t in range(NT):
                        rs = rs32[:, 12 * t:12 * t + 12]
                        for g in range(NG):
                            v.tensor_tensor(qn_[:, t, :, HD * g:HD * g + HD], h64(qt_[:, t, 256 * g:256 * g + 256]),
                                            rs[:, 4 * g:4 * g + 4].unsqueeze(2).to_broadcast([P, 4, HD]), ALU.mult).then_inc(s_norm, 1)
                        for b in range(2):
                            k = h64(kvt[:, t, 256 * b:256 * b + P])
                            v.tensor_tensor(k, k, rs[:, 8 + 2 * b:10 + 2 * b].unsqueeze(2).to_broadcast([P, 2, HD]),
                                            ALU.mult).then_inc(s_norm, 1)
                if name == "kc":
                    v.tensor_tensor(h64(kcn[0:32, :]), h64(kcn[0:32, :]), kcr[0:32, :].unsqueeze(2).to_broadcast([32, 2, HD]),
                                    ALU.mult).then_inc(s_norm, 1)
                if name == "hgrn":
                    dve.wait_ge(s_hc, 32)
                    for t in range(NT):
                        o = mixt[:, t, 512:1024].rearrange("p (a b) -> p a b", b=P)
                        link(v.tensor_tensor(o, o, hrs[:, 4 * t:4 * t + 4].unsqueeze(2).to_broadcast([P, 4, P]), ALU.mult))
                        link(v.tensor_tensor(o, o, onorm.unsqueeze(1).to_broadcast([P, 4, P]), ALU.mult))
                        v.tensor_tensor(mixt[:, t, 512:1024], mixt[:, t, 512:1024], hgt[:, t, :], ALU.mult).then_inc(s_norm, 1)
                if name == "x":
                    for t in range(NT):
                        v.tensor_scalar(xt[:, t, :], xt[:, t, :], rsx[:, t:t + 1], None, ALU.mult).then_inc(s_norm, 1)
                if name == "y":
                    for t in range(NT):
                        for g in range(2):
                            y = zt[:, t, 512 * g:512 * g + 512]
                            last = v.tensor_scalar(y, y, rsy[:, 2 * t + g:2 * t + g + 1], None, ALU.mult)
                        last.then_inc(s_norm, 1)
                if name == "out1":
                    dve.wait_ge(s_res, 32)
                    for t in range(NT):
                        link(v.scalar_tensor_tensor(oraw[:, t, :], oraw[:, t, :], rso[:, t:t + 1], npost, ALU.mult, ALU.mult))
                        v.tensor_tensor(xres[:, t, :], xres[:, t, :], oraw[:, t, :], ALU.add).then_inc(s_norm, 1)

            def turn(name, c, g):
                n = TURNS.index(("turn", name, c, g))
                dve.wait_ge(s_round, n + 1)
                hi, lo = ACTS[FILLS[name]]
                ps = bank[TILE_RING.slot(g)][:, :]
                if name in TURN_SCALE:
                    ins = v.scalar_tensor_tensor(lo[:, c, :], ps, V(TURN_SCALE[name], c), f32(hi[:, c, :]),
                                                 ALU.mult, ALU.subtract)
                else:
                    ins = v.tensor_tensor(lo[:, c, :], ps, f32(hi[:, c, :]), ALU.subtract)
                ins.then_inc(s_split, 1)
                dve.wait_ge(s_split, SPLITS.index(("turn", name, c, g)) + 1)
                dve.sem_inc(s_end["V"], 1)

            def small_gates(g):
                dve.wait_ge(s_shi, 2)
                v.tensor_tensor(swlo[:, :], swraw[:, :], f32(swhi[:, :]), ALU.subtract).then_inc(s_slo, 1)
                link(v.tensor_tensor(lbs, V("lower", 0, 4), V("lower", 4, 4), ALU.subtract))
                dve.sem_inc(s_hlb, 1)
                dve.wait_ge(s_hlb, 2)
                link(v.tensor_scalar(lbn, lbs, -1.0, 1.0, ALU.mult, ALU.add))

            def compress():
                dve.wait_ge(s_norm, NORMED["qk"])
                link(v.memset(hid, 0.0))
                dve.wait_ge(s_hid, 1)
                v.tensor_copy(posb, bank[4][:, P:P + 2]).then_inc(s_hc_pos, 1)
                dve.wait_ge(s_gelu, 4)
                for g in range(NG):
                    v.tensor_copy(hid4[:, g, :, :], hid[:, 1, g, :].unsqueeze(1).to_broadcast([P, 4, 32])).then_inc(s_hid4, 1)
                norm("kc")
                dve.wait_ge(s_hid, 3)
                for g in range(NG):
                    link(v.tensor_tensor(vcd[:, g, :, :], bank[7][:, HD * g:HD * g + HD].unsqueeze(1).to_broadcast([P, 4, HD]),
                                         heads4.unsqueeze(2).to_broadcast([P, 4, HD]), ALU.mult))
                dve.sem_inc(s_vcd, 1)

            def cmp(qt):
                s3 = cs_[qt % 2]
                n3 = s3[:, :, 0:NCMP]
                mx, sm = cmx[:, 8 * (qt % 2):8 * (qt % 2) + 8], csum[:, 8 * (qt % 2):8 * (qt % 2) + 8]
                gate = gl[:, 24 * qt:24 * qt + 24].rearrange("p (a b) -> p b a", b=3)[:, 0, :]
                if qt >= 2:
                    dve.wait_ge(s_ctr, qt - 1)
                link(v.memset(s3, NEG))
                dve.wait_ge(s_cqk, qt + 1)
                for g in range(NG):
                    link(v.tensor_tensor(n3[:, 4 * g:4 * g + 4, :],
                                         bank[4 + 3 * g][:, 0:P].rearrange("p (a b) -> p a b", b=32)[:, :, 0:NCMP],
                                         cmask[:, qt, 0:NCMP].unsqueeze(1).to_broadcast([P, 4, NCMP]), ALU.add))
                link(v.tensor_reduce(mx, n3, AX.X, ALU.max))
                link(v.tensor_tensor(n3, n3, mx.unsqueeze(2).to_broadcast([P, NH, NCMP]), ALU.subtract))
                dve.sem_inc(s_cs, 1)
                dve.wait_ge(s_ce, qt + 1)
                link(v.tensor_reduce(sm, n3, AX.X, ALU.add))
                link(v.reciprocal(sm, sm))
                if qt == 0:
                    dve.wait_ge(s_end["S"], GATES_READ)
                link(v.tensor_tensor(sm, sm, gate, ALU.mult))
                link(v.tensor_scalar(sm, sm, cmask[:, qt, 31:32], None, ALU.mult))
                v.tensor_tensor(s3, s3, sm.unsqueeze(2).to_broadcast([P, NH, 32]), ALU.mult).then_inc(s_cp, 1)
                dve.wait_ge(s_cpv, qt + 1)
                v.tensor_copy(mixt[:, qt, 0:512], bank[6][:, :]).then_inc(s_cm, 1)

            def nsa(u):
                if u < UNITS:
                    kend = P * (u // 16 + 1)
                    dve.wait_ge(s_nqk, u + 1)
                    link(v.tensor_reduce(nmx[:, u:u + 1], bank[BANK_LOGITS + u % 2][:, 0:kend], AX.X, ALU.max))
                    v.tensor_scalar(nmx[:, u:u + 1], nmx[:, u:u + 1], -SCALE, None, ALU.mult).then_inc(s_nmx, 1)
                o = u - 2
                if 0 <= o < UNITS and o % 8 == 7:
                    qt, b = o // 16, o // 8 % 2
                    f = f8[:, 0:8]
                    gate = gl[:, 24 * qt:24 * qt + 24].rearrange("p (a b) -> p b a", b=3)[:, 1 + b, :]
                    h64 = lambda ap: ap.rearrange("p (a b) -> p a b", b=HD)
                    dve.wait_ge(s_npv, o + 1)
                    link(v.reciprocal(f, nsum[:, o - 7:o + 1]))
                    link(v.tensor_tensor(f, f, gate, ALU.mult))
                    link(v.tensor_tensor(h64(ntmp), h64(bank[BANK_O][:, :]), f.unsqueeze(2).to_broadcast([P, NH, HD]), ALU.mult))
                    link(v.tensor_tensor(mixt[:, qt, 0:512], mixt[:, qt, 0:512], ntmp, ALU.add))
                    dve.sem_inc(s_nm, 1)

            def hgrn(h):
                hq_, hk_, pre, suf = hset[h % 2]
                at = hat[h % 2]
                if h == 0:
                    dve.wait_ge(s_hc, 32)
                    link(v.tensor_copy(halves, halves_f))
                if h >= 2:
                    dve.wait_ge(s_ho, h - 1)

                def read(n):
                    m = (LEVELS + 1) * h + n
                    dve.wait_ge(s_hprod, m + 1)
                    ps = bank[4 + m % 2]
                    if n == 0:
                        r = lambda ap: ap.rearrange("p (a b) -> p a b", b=P)
                        ins = v.tensor_tensor(r(at[:, 0:512]), r(ps[:, :]), ident.unsqueeze(1).to_broadcast([P, NT, P]), ALU.mult)
                    elif n <= 7:
                        w = 2 ** (n - 1)
                        up = lambda ap: ap.rearrange("p (a b c) -> p a b c", b=2, c=w)[:, :, 1, :]
                        ins = v.copy_predicated(up(at[:, 0:512]), halves[:, 256 * (n - 1):256 * n].rearrange("p (a b) -> p a b", b=w),
                                                up(ps[:, :]))
                    elif n == 8:
                        ins = v.tensor_copy(at[:, 512:768], ps[:, 0:256])
                    else:
                        ins = v.tensor_copy(at[:, 768:1280], ps[:, :])
                    link(ins)
                    dve.sem_inc(s_hread, 1)

                dve.sem_inc(s_hlev, 1)
                for n in range(1, LEVELS + 1):
                    m = (LEVELS + 1) * h + n
                    w = 2 ** (n - 1)
                    q_, k_ = hqk[m % 2]
                    two = lambda ap: ap.rearrange("p (a b c) -> p a b c", b=2, c=w)
                    if m >= 2:
                        dve.wait_ge(s_hprod, m - 1)
                    v.tensor_tensor(two(q_)[:, :, 1, :], two(hq_)[:, :, 1, :], two(pre)[:, :, 1, :], ALU.mult)
                    link(v.tensor_tensor(k_, hk_, suf, ALU.mult))
                    dve.sem_inc(s_hlev, 1)
                    if n < LEVELS:
                        last_of = lambda i: two(pre)[:, :, i, w - 1:w].to_broadcast([P, T // (2 * w), w])
                        link(v.tensor_tensor(two(suf)[:, :, 0, :], two(suf)[:, :, 0, :], last_of(1), ALU.mult))
                        link(v.tensor_tensor(two(pre)[:, :, 1, :], two(pre)[:, :, 1, :], last_of(0), ALU.mult))
                    read(n - 1)
                read(LEVELS)

            def small_dt(g):
                dve.wait_ge(s_shi, 1)
                v.tensor_tensor(swlo[:, 0:NK * SH], swraw[:, 0:NK * SH], f32(swhi[:, 0:NK * SH]), ALU.subtract).then_inc(s_slo, 1)
                dve.wait_ge(s_tile, g + 1)
                ps = bank[TILE_RING.slot(g)]
                link(v.tensor_tensor(t64[0].rearrange("p (a b) -> p a b", b=SH), ps[:, 0:64].rearrange("p (a b) -> p a b", b=SH),
                                     V("dt_bias", 0, SH).unsqueeze(1).to_broadcast([P, NT, SH]), ALU.add))
                dve.sem_inc(s_end["V"], 1)
                link(v.tensor_scalar(t64[1], t64[0], -1.0, None, ALU.mult))
                link(v.tensor_tensor(t64[1], t64[1], t64[0], ALU.min))
                dve.sem_inc(s_dte, 1)
                dve.wait_ge(s_ex, 1)
                link(v.tensor_scalar(t64[1], t64[1], 1.0, None, ALU.add))
                dve.sem_inc(s_dte, 1)
                link(v.tensor_scalar(t64[0], t64[0], 0.0, None, ALU.max))
                dve.wait_ge(s_ex, 3)
                link(v.tensor_tensor(dt_, t64[0], t64[1], ALU.add))
                v.scalar_tensor_tensor(adt.rearrange("p (a b) -> p a b", b=SH), dt_.rearrange("p (a b) -> p a b", b=SH),
                                       -1.0, aexp.unsqueeze(1).to_broadcast([P, NT, SH]), ALU.mult, ALU.mult).then_inc(s_dt, 1)

            def ssd_decay():
                dve.wait_ge(s_aux, AUX.at["decay"] + 1)
                ps = bank[4 + AUX.slot("decay")]
                v.tensor_copy(t64[0], ps[:, 0:64])
                link(v.tensor_copy(t64[1], ps[:, 64:128]))
                v.tensor_scalar(acs_n, t64[0], -1.0, None, ALU.mult)
                link(v.tensor_tensor(t64[2], t64[1], t64[0], ALU.subtract))
                dve.sem_inc(s_auxend["V"], 1)
                dve.sem_inc(s_dte, 1)
                dve.wait_ge(s_ex, 4)
                link(v.tensor_tensor(dtend, dtend, dt_, ALU.mult))
                dve.sem_inc(s_dt, 1)

            def ssd(c, part):
                if part == 0:
                    key = ("scores", c)
                    dve.wait_ge(s_aux, AUX.at[key] + 1)
                    link(v.tensor_copy(sc, bank[4 + AUX.slot(key)][:, 0:2 * P].rearrange("p (a b) -> p a b", b=P)))
                    dve.sem_inc(s_auxend["V"], 1)
                if part < 4:
                    dve.wait_ge(s_auxend["S"], AUX.ends[AUX.at[("decay", c, part)]][1])
                    e = ee[:, part % 2, :, :]
                    v.tensor_tensor(e, e, sc[:, part // 2, :].unsqueeze(1).to_broadcast([P, 4, P]), ALU.mult).then_inc(s_attn, 1)
                if part == 4:
                    bc = lambda t, g: t[:, SH * c + 8 * g:SH * c + 8 * g + 8].unsqueeze(2).to_broadcast([P, 8, HD])
                    h8 = lambda ap: ap.rearrange("p (a b) -> p a b", b=HD)
                    if c > 0:
                        for g in range(2):
                            key = ("y_off", c, g)
                            dve.wait_ge(s_aux, AUX.at[key] + 1)
                            link(v.tensor_tensor(h8(ytmp[:, g, :]), h8(bank[4 + AUX.slot(key)][:, :]), bc(ecs, g), ALU.mult))
                            dve.sem_inc(s_auxend["V"], 1)
                    dve.wait_ge(s_yd, 4 * c + 4)
                    dve.wait_ge(s_xd, 2 * c + 2)
                    for g in range(2):
                        y, x = ytmp[:, g, :], xs[:, c, 512 * g:512 * g + 512]
                        if c > 0:
                            link(v.tensor_tensor(y, y, bank[6 + g][:, :], ALU.add))
                            link(v.tensor_tensor(y, y, x, ALU.add))
                        else:
                            link(v.tensor_tensor(y, bank[6 + g][:, :], x, ALU.add))
                        ins = v.tensor_tensor(zt[:, c, 512 * g:512 * g + 512], zt[:, c, 512 * g:512 * g + 512], y, ALU.mult)
                    ins.then_inc(s_y, 1)
                    if c < NT - 1:
                        for g in range(2):
                            key = ("state", c, g)
                            if c > 0:
                                link(v.tensor_tensor(h8(state[:, g, :]), h8(state[:, g, :]), bc(edec, g), ALU.mult))
                            dve.wait_ge(s_aux, AUX.at[key] + 1)
                            ps = bank[4 + AUX.slot(key)][:, :]
                            if c > 0:
                                ins = v.tensor_tensor(state[:, g, :], state[:, g, :], ps, ALU.add)
                            else:
                                ins = v.tensor_copy(state[:, g, :], ps)
                            ins.then_inc(s_st, 1)
                            dve.wait_ge(s_st, 2 * c + g + 1)
                            dve.sem_inc(s_auxend["V"], 1)

            def stick(u):
                if u < SH * NT:
                    kend = P * (u % NT + 1)
                    f0 = 516 * (u % 2)
                    if u == 0:
                        for i in range(2):
                            v.memset(sb_fail[:, 516 * i + 512:516 * i + 513], 1.0)
                        v.memset(zeros, 0.0).then_inc(s_zero, 1)
                        dve.wait_ge(s_zero, 1)
                    dve.wait_ge(s_sig, u + 1)
                    if u >= 2:
                        dve.wait_ge(s_tr, u - 1)
                    w = sb_w[:, u % 2, 0:kend]
                    fail = sb_fail[:, f0 + 513 - kend:f0 + 513]
                    v.tensor_tensor_scan(w[:, ::-1], fail[:, ::-1], zeros[:, 0:kend], 1.0, ALU.mult, ALU.add).then_inc(s_scan, 1)
                if 2 <= u:
                    o = u - 2
                    h, qt = divmod(o, NT)
                    rows = slice(HD * (h % 2), HD * (h % 2) + HD)
                    dve.wait_ge(s_pv, o + 1)
                    v.tensor_copy(qf[rows, h // 2, P * qt:P * qt + P], bank[BANK_O][rows, P * (o % 4):P * (o % 4) + P]).then_inc(s_o, 1)

            rest_of_weights(0)
            for s in STEPS:
                if s[0] == "norm":
                    norm(s[1])
                if s[0] == "turn":
                    turn(*s[1:])
                if s[0] == "gemm":
                    rest_of_weights(s[1] + 1)
                    for g in BLOCKS[s[1]]["closes"]:
                        tile(g)
                if s[0] == "small":
                    (small_dt if s[1] == "dt" else small_gates)(s[2])
                if s[0] == "compress":
                    compress()
                if s[0] == "cmp":
                    cmp(s[1])
                if s[0] == "nsa":
                    nsa(s[1])
                if s[0] == "hgrn":
                    hgrn(s[1])
                if s[0] == "ssd_decay":
                    ssd_decay()
                if s[0] == "ssd":
                    ssd(s[1], s[2])
                if s[0] == "sb":
                    stick(s[1])
                if s[0] == "merge":
                    c = s[1]
                    dve.wait_ge(s_tround, PRODUCTS.index(s) + 1)
                    v.tensor_tensor(a_lo[:, c, :], mg[:, c, :], f32(a_hi[:, c, :]), ALU.subtract).then_inc(s_split, 1)

        @block.gpsimd
        def _(pool):
            g_ = nc.gpsimd
            h16 = lambda ap: ap.rearrange("p (a b) -> p a b", b=HD)
            for s in STEPS:
                if s[0] == "ssd" and s[2] == 0:
                    c = s[1]
                    bc = lambda t: t[:, SH * c:SH * c + SH].unsqueeze(2).to_broadcast([P, SH, HD])
                    if c == 0:
                        pool.wait_ge(s_dt, 2)
                        pool.wait_ge(s_auxend["S"], 10)
                    if c >= 2:
                        pool.wait_ge(s_yd, 4 * c - 4)
                    g_.tensor_tensor(h16(xdt[:, c % 2, :]), h16(xs[:, c, :]), bc(dt_), ALU.mult).then_inc(s_xd, 1)
                    if 1 <= c:
                        pool.wait_ge(s_st, 2 * c)
                    if c < NT - 1:
                        g_.tensor_tensor(h16(xdd), h16(xs[:, c, :]), bc(dtend), ALU.mult).then_inc(s_pc, 1)
                        pool.wait_ge(s_pc, c + 1)
                    pool.wait_ge(s_xd, 2 * c + 1)
                    g_.tensor_tensor(h16(xs[:, c, :]), h16(xs[:, c, :]), V("d_skip", 0, SH).unsqueeze(2).to_broadcast([P, SH, HD]),
                                     ALU.mult).then_inc(s_xd, 1)
                if s[0] == "sb" and s[1] < SH * NT:
                    u = s[1]
                    kend = P * (u % NT + 1)
                    pool.wait_ge(s_scan, u + 1)
                    w = sb_w[:, u % 2, 0:kend]
                    g_.tensor_tensor(w, w, sb_sig[:, u % 2, 0:kend], ALU.mult).then_inc(s_wgt, 1)


def lay_out(x, norm_pre, w_in, b_gate, conv_w, conv_b, dt_bias, a_log, d_skip, ssd_norm, w_ssd_proj, w_sb_proj,
            w_out, norm_post, norm_mix_2, w_in_2, q_norm_2, k_norm_2, cmp_pos_k_2, cmp_pos_v_2, cmp_k_w1_2, cmp_k_w2_2,
            cmp_v_w1_2, cmp_v_w2_2, hgrn_lb_logits_2, hgrn_o_norm_2, w_out_2, norm_ffn_2, w_gate_up_2, w_down_2):
    w = {"w_in": (w_in[0],), "gate_ssd": (w_in[0], w_ssd_proj[0]), "gate_sb": (w_in[0], w_sb_proj[0]), "w_out": (w_out[0],),
         "w_in_2": (w_in_2[0],), "w_out_2": (w_out_2[0],), "w_gate_up": (w_gate_up_2[0],), "w_down": (w_down_2[0],)}
    blk = np.zeros((NB, P, BLK), w_in.dtype)
    for n, b in enumerate(BLOCKS):
        src = w[b["w"]]
        parts = []
        for i, (c0, cn) in enumerate(b["spans"]):
            m = src[min(i, len(src) - 1)]
            parts.append(m[P * b["k0"]:P * (b["k0"] + b["kn"]), c0:c0 + cn].reshape(b["kn"], P, cn))
        joined = np.concatenate(parts, axis=2).transpose(1, 0, 2).reshape(P, -1)
        blk[n, :, :joined.shape[1]] = joined
    cols = lambda a: a.reshape(-1, P).T
    rows = lambda a: np.broadcast_to(a.reshape(1, -1), (P, a.size))
    vec = np.empty((P, VEC.width), x.dtype)
    conv = conv_w[0].reshape(TAPS, XC, P).transpose(2, 1, 0).reshape(P, XC * TAPS)
    for name, v in dict(norm_pre=cols(norm_pre[0]), b_gate=cols(b_gate[0]), conv_w=conv, conv_b=cols(conv_b[0]),
                        ssd_norm=cols(ssd_norm[0]), dt_bias=rows(dt_bias[0]), a_log=rows(a_log[0]),
                        d_skip=rows(d_skip[0]), norm_mix=cols(norm_mix_2[0]), norm_ffn=cols(norm_ffn_2[0]),
                        q_norm=np.tile(q_norm_2[0].reshape(HD, 1), (2, 1)), k_norm=np.tile(k_norm_2[0].T, (2, 1)),
                        lower=np.concatenate([cols(hgrn_lb_logits_2[0]), cols(hgrn_lb_logits_2[1])], axis=1)).items():
        vec[:, VEC.at(name)] = v
    cst = np.empty((P, CST.width), np.float32)
    i, j = np.arange(P)[:, None], np.arange(P)[None, :]
    cst[:, CST.at("ident")] = i == j
    cst[:, CST.at("tri")] = i <= j
    cst[:, CST.at("ones")] = 1.0
    bf = mybir.dt.np(BF16)
    cstb = np.empty((P, CSTB.width), bf)
    cstb[:, CSTB.at("ident")] = i == j
    cstb[:, CSTB.at("strict")] = np.where(j < i, 0.0, NEG)
    cstb[:, CSTB.at("after")] = np.where(i <= j, 0.0, NEG)
    small = lambda m, c0, n: m[:, c0:c0 + n].reshape(NK, P, n).transpose(1, 0, 2).reshape(P, NK * n)
    both = lambda m: np.tile(m, (2, 1))
    w1 = lambda m: both(m[0].reshape(CL, HD, P).transpose(1, 0, 2).reshape(HD, CL * P))
    cst2 = np.zeros((P, CST2.width), x.dtype)
    cst2[:, CST2.at("w2")] = np.concatenate([cmp_k_w2_2[0], cmp_v_w2_2[0]], axis=1)
    cst2[:, CST2.at("pos")] = both(np.concatenate([cmp_pos_k_2[0].T, cmp_pos_v_2[0].T], axis=1))
    cst2[:, CST2.at("heads")] = i // 32 == np.arange(4)[None, :]
    upto = np.where(j <= i, 0.0, NEG).astype(bf)
    token = np.arange(T).reshape(NT, P).T[:, :, None]
    ends = (CS * np.arange(32) + CL - 1)[None, None, :]
    cmask = np.where(ends <= token, 0.0, NEG).astype(np.float32)
    cmask[:, :, 31] = (token >= CL - 1)[:, :, 0]
    halves = np.zeros((P, 7, 256), np.float32)
    t = np.arange(T)
    for n in range(7):
        up = t[(t >> n) & 1 == 1]
        s = np.arange(P)[:, None]
        halves[:, n, :] = (s >> (n + 1) == (up % P)[None, :] >> (n + 1)) & ((s >> n) & 1 == 0)
    return {"x": x[0], "wblk": blk, "vec": vec, "cst": cst, "cstb": cstb, "w_dt": small(w_in[0], DT0, SH),
            "w_gates": small(w_in_2[0], GL0, 24), "norm_post": rows(norm_post[0]), "w1k": w1(cmp_k_w1_2),
            "w1v": w1(cmp_v_w1_2), "cst2": cst2, "upto": upto, "cmask": cmask.reshape(P, P),
            "halves": halves.reshape(P, 7 * 256), "onorm": rows(hgrn_o_norm_2[0])}


def kernel(**inputs):
    import concourse.bacc as bacc
    from concourse.bass_utils import run_bass_kernel_spmd

    nc = bacc.Bacc("TRN2", target_bir_lowering=False, num_devices=1)
    arrays = {name: np.ascontiguousarray(a) for name, a in lay_out(**inputs).items()}
    dram = {name: nc.dram_tensor("in_" + name, a.shape, mybir.dt.from_np(a.dtype), kind="ExternalInput").ap()
            for name, a in arrays.items()}
    out = nc.dram_tensor("out", (T, D), F32, kind="ExternalOutput").ap()
    emit(nc, dram, out)
    r = run_bass_kernel_spmd(nc, [{"in_" + name: a for name, a in arrays.items()}], core_ids=[0])
    return r.results[0]["out"].reshape(1, T, D)
```

```python
from contextlib import ExitStack

import numpy as np

import concourse.bass as bass
from concourse import mybir

ALU = mybir.AluOpType
ACT = mybir.ActivationFunctionType
AX = mybir.AxisListType
F32 = mybir.dt.float32
F32R = mybir.dt.float32r
BF16 = mybir.dt.bfloat16
U8 = mybir.dt.uint8

P = 128
T = 512
D = 1024
NT = T // P
NK = D // P
EPS = 1e-6
NEG = -1e30
HD = 64
SCALE = HD ** -0.5

Z0, XBC0 = 0, 1024
DT0 = XBC0 + 1536
Q0 = DT0 + 16
K0, V0, ZS0, G0 = Q0 + 1024, Q0 + 2048, Q0 + 3072, Q0 + 4096
SH = 16
XC = 12
TAPS = 4
KC0 = 512
KS0, GL0, HQ0, HF0, HI0, HG0 = 768, 1280, 1304, 1816, 2328, 2840
NH = 8
NG = 2
NCMP = 31
CL, CS = 32, 16
HH = 4
DFF = 2816
FFP = ((0, 8), (8, 16), (16, 22))
LEVELS = 9
SLICES = 8
SB_LAG = 2
UNITS = NH * NT
BLK = 2048



def weave(*streams):
    keyed = [((i + 0.5) / len(s), n, i, x) for n, s in enumerate(streams) for i, x in enumerate(s)]
    return [x for *_, x in sorted(keyed, key=lambda k: k[:3])]


def plan():
    blocks, tiles, steps = [], [], []

    def tile(kind, i):
        tiles.append((kind, i))
        return len(tiles) - 1

    def feature(w, spans, kinds, srcs):
        gs = [tile(k, i) for k, i in kinds]
        n = len(blocks)
        parts = [(j, k) for j in range(2) for k in range(NK)]
        blocks.append(dict(w=w, form="feature", spans=spans, k0=0, kn=NK, tiles=gs, srcs=srcs, parts=parts, kb=0,
                           total=NK, closing=True))
        return [("gemm", n, s) for s in range(SLICES)]

    def token(w, col, kind, half, src, k0=0, kn=NK):
        gs = [tile(kind, (t, half)) for t in range(NT)]
        a = kn // 2
        out = []
        for j in range(2):
            n = len(blocks)
            parts = [(t, k) for t in range(NT) for k in range(a)]
            blocks.append(dict(w=w, form="token", spans=[(col, 512)], k0=k0 + j * a, kn=a, tiles=gs, srcs=[src] * 4,
                               parts=parts, kb=j * a, total=kn, closing=j == 1))
            out += [("gemm", n, s) for s in range(SLICES)]
        return out

    def turn(name, t, half):
        return ("turn", name, t, half, tile("turn", (name, t, half)))

    def normed(name, halves=(0, 1)):
        return [[("norm", name, t)] + [turn(name, t, h) for h in halves] for t in range(NT)]

    for t in range(NT):
        steps.append(("norm", "x", t))
    for t in range(NT):
        steps.extend(turn("x", t, h) for h in range(2))
    steps.append(("small", "dt", tile("dt", 0)))
    for j in range(XC // 2):
        steps += feature("w_in", [(XBC0 + 256 * j, 256)], [("xbc", 2 * j), ("xbc", 2 * j + 1)], "AA")
        if j == 1:
            steps.append(("ssd_decay",))
        if j >= 1:
            steps.extend([("xturn", 2 * j - 2), ("xturn", 2 * j - 1)])
    kq = []
    for name, c0 in (("k", K0), ("q", Q0)):
        for j in range(4):
            kq += feature("w_in", [(c0 + 256 * j, 256)], [(name, 2 * j), (name, 2 * j + 1)], "AA")
    steps += weave([("ssd", c, part) for c in range(NT) for part in range(5)], kq)
    for half in range(2):
        steps += token("w_in", Z0 + 512 * half, "z", half, "A")
    vs = token("w_in", V0, "v", 0, "A") + token("w_in", V0 + 512, "v", 1, "A")
    ys = normed("y")
    steps += weave(sum(ys, []), vs[:24]) + vs[24:]
    gs = []
    for c in range(NK):
        gs += feature("gate_ssd", [(G0 + P * c, P), (P * c, P)], [("gate", c), ("y_ssd", c)], "AB")
    steps += weave([("sb", u) for u in range(SH * NT)], gs)
    steps += [("sb", SH * NT + i) for i in range(SB_LAG + 1)]
    for j in range(4):
        steps += feature("w_in", [(ZS0 + 256 * j, 256)], [("z_sb", 2 * j), ("z_sb", 2 * j + 1)], "AA")
    for c in range(NK):
        steps += feature("gate_sb", [(G0 + D + P * c, P), (P * c, P)], [("gate2", c), ("y_sb", c)], "AB")
    for c in range(NK):
        steps.append(("merge", c))

    def residual(name, blocks_, before):
        nonlocal steps
        steps += blocks_[:-8]
        ns = normed(name)
        for s in range(8):
            steps.append(blocks_[s - 8])
            if s % 2:
                steps += [(b, before, s // 2) for b in ("norm",) if before]
                steps.append(ns[s // 2][0])
                if s >= 5:
                    steps += ns[s // 2 - 2][1:]
        steps += ns[2][1:] + ns[3][1:]

    residual("mix", token("w_out", 0, "out1", 0, "A") + token("w_out", 512, "out1", 1, "A"), "out1")

    steps += feature("w_in_2", [(KC0, 256)], [("kcv", 0), ("kcv", 1)], "AA")
    steps.append(("pos",))
    kv = token("w_in_2", KS0, "kv", 0, "A")
    qn = token("w_in_2", 0, "qn", 0, "A")
    steps += kv + qn[:8]
    for s in range(8):
        steps.append(qn[8 + s])
        if s % 2:
            steps.append(("norm", "qk", s // 2))
    steps.append(("small", "gates", tile("gates", 0)))
    head = lambda h: feature("w_in_2", [(HQ0 + P * h, P), (HF0 + P * h, P)], [("hq", h), ("hf", h)], "AA")
    steps += weave([("compress", i) for i in range(4)] + [("qkturn", i, tile("turn_qk", i)) for i in range(6)], head(0))
    steps += weave([("cmp", qt, i) for qt in range(NT) for i in range(3)], token("w_in_2", HI0, "hi", 0, "A"))
    hs = []
    for h in range(HH):
        levels = [("level", h, n, tile("level", (h, n))) for n in range(LEVELS + 1)] + [("hout", h, tile("hout", h))]
        hs += weave(levels, head(h + 1)) if h + 1 < HH else levels
    steps += weave([("nsa", u) for u in range(UNITS + 2)], hs)
    hg = token("w_in_2", HG0, "hg", 0, "A")
    steps += hg[:8]
    hn = normed("hgrn", (1,))
    for s in range(8):
        steps.append(hg[8 + s])
        if s % 2:
            steps.append(hn[s // 2][0])
            if s >= 5:
                steps += hn[s // 2 - 2][1:]
    steps += hn[2][1:] + hn[3][1:]
    residual("ffn", token("w_out_2", 0, "out2", 0, "B") + token("w_out_2", 512, "out2", 1, "B"), None)
    for a, e in FFP:
        for c in range(a, e):
            steps += feature("w_gate_up", [(P * c, P), (DFF + P * c, P)], [("ff_gate", (c, c - a)), ("ff_up", (c, c - a))], "AA")
        for half in range(2):
            steps += token("w_down", 512 * half, "down", (a, half), "B", k0=a, kn=e - a)
    return blocks, tiles, steps


def sliced(b, s):
    n = len(b["parts"])
    return b["parts"][s * n // SLICES:(s + 1) * n // SLICES]


def opened(b, s):
    return [b["tiles"][j] for j, k in sliced(b, s) if k == 0 and b["kb"] == 0]


def closed(b, s):
    return [b["tiles"][j] for j, k in sliced(b, s) if k == b["kn"] - 1 and b["closing"]]


BLOCKS, TILES, STEPS = plan()
NB = len(BLOCKS)

READER = {"turn": "V", "xbc": "S", "dt": "V", "z": "V", "k": "S", "q": "S", "v": "S", "gate": "S", "y_ssd": "V",
          "z_sb": "V", "gate2": "S", "y_sb": "V", "out1": "S", "kv": "S", "qn": "S", "kcv": "S", "gates": "S",
          "turn_qk": "S", "hi": "S", "hg": "V", "hq": "V", "hf": "V", "level": "V", "hout": "S", "out2": "V",
          "ff_gate": "V", "ff_up": "V", "down": "V"}


class Ring:

    def __init__(self, size):
        self.size, self.ends, self.count, self.at = size, [], {"V": 0, "S": 0}, {}

    def use(self, key, reader):
        self.count[reader] += 1
        self.at[key] = len(self.ends)
        self.ends.append((reader, self.count[reader]))

    def slot(self, key):
        return self.at[key] % self.size

    def before(self, key):
        i = self.at[key] - self.size
        return self.ends[i] if i >= 0 else None


def plan_tiles():
    begun, done, ended = [], [], []
    for s in STEPS:
        if s[0] == "gemm":
            begun += opened(BLOCKS[s[1]], s[2])
            done += closed(BLOCKS[s[1]], s[2])
            ended += closed(BLOCKS[s[1]], s[2])
        elif s[0] in ("turn", "small", "qkturn", "level", "hout"):
            begun.append(s[-1])
            done.append(s[-1])
            if s[0] == "level":
                if s[2] > 0:
                    ended.append(level_tile(s[1], s[2] - 1))
            elif s[0] == "hout":
                ended += [level_tile(s[1], LEVELS), s[-1]]
            else:
                ended.append(s[-1])
    count, end = {"V": 0, "S": 0}, {}
    for g in ended:
        who = READER[TILES[g][0]]
        count[who] += 1
        end[g] = (who, count[who])
    bank, before = {}, {}
    groups = {"turn": (4, 5, 6, 7), "level": (2, 3), "hout": (2, 3), "turn_qk": (2, 3), "hq": (0, 1), "hf": (0, 1)}
    uses, last = {}, {}
    for g in begun:
        banks = groups.get(TILES[g][0], (0, 1, 2, 3))
        i = uses[banks] = uses.get(banks, -1) + 1
        bank[g] = banks[i % len(banks)]
        before[g] = last.get(bank[g])
        last[bank[g]] = g
    return bank, before, {g: i + 1 for i, g in enumerate(done)}, end


def level_tile(h, n):
    return TILES.index(("level", (h, n)))


BANK, BEFORE, DONE, END = plan_tiles()


def plan_aux():
    ring = Ring(2)
    for s in STEPS:
        if s[0] == "xturn":
            ring.use(s, "S")
        if s[0] == "ssd_decay":
            ring.use("decay", "V")
        if s[0] == "ssd":
            _, c, part = s
            if part == 0:
                ring.use(("scores", c), "V")
            if part < 4:
                ring.use(("decay", c, part), "S")
            if part == 4:
                for g in range(2):
                    if c > 0:
                        ring.use(("y_off", c, g), "V")
                for g in range(2):
                    if c < NT - 1:
                        ring.use(("state", c, g), "V")
    return ring


AUX = plan_aux()
SIGMOID = {"z", "gate", "z_sb", "gate2", "hg", "hq", "hf", "ff_gate"}
CONSUMER = {"z": 0, "gate": 1, "z_sb": 0, "gate2": 1, "hg": 0, "hq": 0, "hf": 0, "ff_gate": 1}
SIG_TILES = sorted((g for g, (kind, _) in enumerate(TILES) if kind in SIGMOID), key=DONE.get)
FILLS = {"x": "A", "y": "B", "mix": "A", "hgrn": "B", "ffn": "A"}
ROWS = {"x": "norm_pre", "y": "ssd_norm", "mix": "norm_mix", "ffn": "norm_ffn"}
SQUARED = ("x", "y", "mix", "ffn")
SPLIT_TILES = {"z_sb": "B", "ff_up": "B"}
NORMS = [s[1:] for s in STEPS if s[0] == "norm"] 
NORMS.insert(max(i for i, x in enumerate(NORMS) if x[0] == "qk") + 1, ("kc", 0))


def plan_splits():
    order, need, last = [], {}, {}

    def done(key, dst, chunks, tokens=range(NT)):
        order.append(key)
        for k in chunks:
            for t in tokens:
                last[dst, t, k] = len(order)

    for s in STEPS:
        if s[0] == "turn":
            done(s, FILLS[s[1]], range(4 * s[3], 4 * s[3] + 4), [s[2]])
        if s[0] == "merge":
            done(s, "A", [s[1]])
        if s[0] == "nsa" and s[1] >= 2 and (s[1] - 2) % NH == NH - 1:
            done(s, "B", range(4), [(s[1] - 2) // NH])
        if s[0] == "small":
            need[s[:2]] = max(v for (x, _, _), v in last.items() if x == "A")
        if s[0] == "gemm":
            b = BLOCKS[s[1]]
            for j, k in sliced(b, s[2]):
                ts = [j] if b["form"] == "token" else range(NT)
                need[s[1], j, k] = max(last[b["srcs"][j], t, b["kb"] + k] for t in ts)
            for g in closed(b, s[2]):
                kind, i = TILES[g]
                if kind in SPLIT_TILES:
                    done(("tile", g), SPLIT_TILES[kind], [i if kind == "z_sb" else i[1]])
    return order, need


SPLITS, SPLIT_NEED = plan_splits()
PRODUCTS = [s for s in SPLITS if s[0] in ("tile", "merge")]


class Columns:

    def __init__(self, spans):
        self.spans, self.width = {}, 0
        for name, n in spans:
            self.spans[name] = slice(self.width, self.width + n)
            self.width += n

    def at(self, name):
        return self.spans[name]


CST = Columns([("ident", P), ("tri", P), ("ones", P)])
CSTB = Columns([("ident", P), ("strict", P), ("after", P)])
VEC = Columns([("b_gate", 16), ("conv_w", 48), ("conv_b", 12), ("dt_bias", 16), ("a_log", 16), ("d_skip", 16),
               ("q_norm", 1), ("k_norm", 3), ("lower", 8)])
CST2 = Columns([("w2", 2 * HD), ("pos", CL), ("heads", 4), ("one", 64)])
CMASK0 = 572
HALVES = Columns([(f"level{i}", 256) for i in range(7)])
ARENA = 22528
STAT = 700
BANK_LOGITS, BANK_WT, BANK_O = 4, 6, 7


LATE = min(n for n, b in enumerate(BLOCKS) if TILES[b["tiles"][0]][0] == "z_sb") + 1
LAST_DOWN = len(TILES) - 8
MERGE_AFTER = max(n for n, b in enumerate(BLOCKS) if b["w"] == "gate_sb")
TURNS = [s for s in SPLITS if s[0] in ("turn", "nsa")]


def block_of(kind):
    return min(n for n, b in enumerate(BLOCKS) if TILES[b["tiles"][0]][0] == kind)


def end_of(kind, i=None):
    ends = [END[g] for g, (k, j) in enumerate(TILES) if k == kind and i in (None, j)]
    return max(ends)


T_READY = [sum(s[0] == "tile" for s in PRODUCTS[:p + 1]) for p in range(len(PRODUCTS))]


def emit(nc, dram, spill, out):
    ctx = ExitStack()
    with ctx:
        def sb(name, shape, dt=F32):
            return ctx.enter_context(nc.sbuf_tensor(name, shape, dt))

        def sem(name):
            return ctx.enter_context(nc.semaphore(name))

        wraw = [sb(f"wraw{i}", [P, BLK]) for i in range(2)]
        whi = [sb(f"whi{i}", [P, BLK], F32R) for i in range(2)]
        wlo = [sb(f"wlo{i}", [P, BLK], F32R) for i in range(2)]
        swraw = sb("swraw", [P, NK * 24])
        swhi = sb("swhi", [P, NK * 24], F32R)
        swlo = sb("swlo", [P, NK * 24], F32R)
        a_hi, a_lo = sb("a_hi", [P, NK, T], F32R), sb("a_lo", [P, NK, T], F32R)
        b_hi, b_lo = sb("b_hi", [P, NK, T], F32R), sb("b_lo", [P, NK, T], F32R)
        ACTS = {"A": (a_hi, a_lo), "B": (b_hi, b_lo)}
        cst = sb("cst", [P, CST.width])
        cstb = sb("cstb", [P, CSTB.width], BF16)
        vec = sb("vec", [P, VEC.width])
        zerob = sb("zerob", [P, 2], BF16)
        stat = sb("stat", [P, STAT])
        arena = sb("arena", [P, ARENA])

        def mem(kb, shape):
            n = int(np.prod(shape))
            v = arena[:, int(kb * 256):int(kb * 256) + n]
            assert kb * 256 + n <= ARENA, (kb, shape)
            if len(shape) == 2:
                v = v.rearrange("p (a b) -> p a b", b=shape[1])
            if len(shape) == 3:
                v = v.rearrange("p (a b c) -> p a b c", b=shape[1], c=shape[2])
            return v

        used = [0]

        def small(n):
            used[0] += n
            assert used[0] <= STAT
            return stat[:, used[0] - n:used[0]]

        bank = [ctx.enter_context(nc.psum_tensor(f"bank{i}", [P, 512], F32)) for i in range(8)]

        ident = cst[:, CST.at("ident")]
        tri = cst[:, CST.at("tri")]
        ones = cst[:, CST.at("ones")]
        w2 = cst[:, P:P + 2 * HD].rearrange("p (a b) -> p a b", b=HD)
        pos = cst[:, P + 2 * HD:P + 2 * HD + CL].rearrange("p (a b) -> p a b", b=CL // 2)
        heads4 = cst[:, P + 2 * HD + CL:P + 2 * HD + CL + 4]
        one = cst[:, P + 2 * HD + CL + 4:P + 2 * HD + CL + 68]
        identb = cstb[:, CSTB.at("ident")]
        strict = cstb[:, CSTB.at("strict")]
        after = cstb[:, CSTB.at("after")]

        def V(name, i=0, n=1):
            a = VEC.at(name).start
            return vec[:, a + i:a + i + n]

        xt = mem(72, [NT, D])
        xs = mem(16, [NT, D])
        bct = mem(32, [4, T])
        btok = mem(40, [NT, 256])
        state = mem(44, [2, 512])
        xdt = mem(48, [2, D])
        xdd = mem(56, [D])
        sc = mem(60, [2, P])
        ee = mem(61, [2, 4, P])
        ytmp = mem(65, [2, 512])
        kf = mem(72, [NK, T])
        qf = mem(0, [NK, T])
        vt = mem(32, [NT, D])
        junks = {"x": mem(0, [NT, D]), "y": mem(52, [NT, D])}
        rows = {"x": mem(64, [D]), "y": mem(48, [D]), "mix": mem(80, [D]), "ffn": mem(0, [D])}
        craw = mem(0, [2, T])
        cacc = mem(48, [2, T])
        csig = mem(52, [2, T])
        cx = mem(56, [2, T])
        sgt = mem(68, [2, T])
        sb_sig = mem(48, [2, T])
        sb_fail = mem(52, [2 * 516])
        sb_w = mem(57, [3, T])
        sb_wT = mem(63, [2, T])
        zeros = mem(67.5, [1])
        tt = mem(48, [2, T])
        mg = mem(16, [NK, T])
        oraw = mem(0, [NT, D])
        xres = mem(32, [NT, D])
        npost = mem(52, [D])

        xn = mem(16, [NT, D])
        x2 = mem(72, [NT, D])
        vst = mem(0, [NT, 256])
        kst = mem(4, [NT, 256])
        qt_ = mem(8, [NT, 512])
        kcf = mem(48, [2, T])
        kc2 = mem(24, [2, 2, T])
        w1 = [mem(56, [CL // 2, P]), mem(72, [CL // 2, P])]
        qn_ = mem(32, [NT, 4, P])
        qT = mem(40, [4, T])
        kT = mem(64, [2, T])
        sq_ = mem(52, [512])
        cs_ = [mem(8 + i, [NH, 32]) for i in range(2)]
        cpT = mem(10, [NT, 2, P])
        vcd = mem(14, [2, 4, HD])
        hid = mem(52, [2, 2, 32])
        hid4 = mem(52.5, [2, 4, 32])
        kcn = mem(53.5, [P])
        kcT = mem(54, [32])
        nsq = mem(54.25, [P])
        posr = mem(55, [2 * P])
        np_ = mem(24, [2, 2, T])
        npT = mem(56, [4, T])
        mixt = mem(32, [NT, 512])
        hit = mem(16, [NT, 512])
        hgt = mem(24, [NT, 512])
        hset = [[mem(kb, [T]) for kb in kbs] for kbs in ((72, 74, 76, 78), (4, 6, 8, 78))]
        hqk = [[mem(80 + 4 * i + 2 * j, [T]) for j in range(2)] for i in range(2)]
        hat = mem(48, [1280])
        halves = mem(53, [7 * 64]).bitcast(U8)
        halves_f = mem(80, [7 * 256])
        hsq = mem(4, [512])

        sso = small(8)
        nss1 = {"out1": small(4), "mix": small(4), "ffn": small(4)}
        first = used[0]
        dt_ = small(64)
        adt = small(64)
        acs_n = small(64)
        ecs = small(64)
        edec = small(64)
        dtend = small(64)
        t64 = [small(64) for _ in range(3)]
        aexp = small(16)
        nss = {"x": small(4), "y": small(8)}
        nss.update(nss1)
        used[0] = first
        nmx, nsum = small(64), small(64)
        onorm = small(P)
        gl = small(96)
        nss.update({"qk": small(48), "kc": small(2), "hgrn": small(16)})
        cmx, csum = small(16), small(16)
        lbs, lbn = small(4), small(4)
        f2 = small(4)
        cmask = stat[:, CMASK0:CMASK0 + P].rearrange("p (a b) -> p a b", b=32)
        assert used[0] <= CMASK0

        s_w = [sem(f"s_w{i}") for i in range(2)]
        s_sw = sem("s_small_weights")
        s_cst = sem("s_constants")
        s_x = [sem(f"s_x{t}") for t in range(NT)]
        s_row = {name: sem("s_row_" + name) for name in ROWS}
        s_yz, s_spill, s_back = sem("s_gated"), sem("s_residual_stored"), sem("s_residual_back")
        s_kc2, s_pos, s_posr = sem("s_kc_spread"), sem("s_positions_hidden"), sem("s_positions_read")
        s_hi, s_lo = sem("s_weights_hi"), sem("s_weights_lo")
        s_shi, s_slo = sem("s_small_hi"), sem("s_small_lo")
        s_blk, s_tile = sem("s_block_used"), sem("s_tile_summed")
        s_small = sem("s_small_used")
        s_end = {"V": sem("s_tile_read_v"), "S": sem("s_tile_read_s")}
        s_split = sem("s_chunk_split")
        s_round = sem("s_chunk_rounded")
        s_sg = sem("s_sigmoid")
        s_conv, s_csig, s_cx, s_xt = sem("s_conv"), sem("s_conv_sigmoid"), sem("s_conv_silu"), sem("s_x_turned")
        s_aux = sem("s_aux_summed")
        s_auxend = {"V": sem("s_aux_read_v"), "S": sem("s_aux_read_s")}
        s_ss, s_rec, s_rt, s_norm = sem("s_squares"), sem("s_mean"), sem("s_root"), sem("s_normed")
        s_dt, s_dte, s_ex = sem("s_dt"), sem("s_dt_exp"), sem("s_decays")
        s_xd = sem("s_x_dt")
        s_attn, s_yd, s_y, s_st = sem("s_ssd_attn"), sem("s_y_diag"), sem("s_y_read"), sem("s_state")
        s_qk, s_sig, s_scan, s_wgt = sem("s_logits"), sem("s_sb_sigmoids"), sem("s_sb_products"), sem("s_sb_weights")
        s_tr, s_wT, s_pv, s_o = sem("s_sb_turned"), sem("s_sb_wT"), sem("s_sb_summed"), sem("s_sb_out")
        s_t, s_tround, s_mg = sem("s_product"), sem("s_product_rounded"), sem("s_merged")
        s_res, s_zero = sem("s_residual"), sem("s_zero")
        s_vc, s_ac, s_pc = sem("s_vector_chain"), sem("s_scalar_chain"), sem("s_pool_chain")
        s_out = sem("s_stored")
        s_hid4, s_hidz = sem("s_hidden_repeated"), sem("s_hidden_zero")
        s_late, s_hc = sem("s_late_constants"), sem("s_hgrn_constants")
        s_hid, s_gelu, s_kc, s_kct, s_kcr, s_vcd = (sem("s_hidden"), sem("s_gelu"), sem("s_kc"), sem("s_kc_turned"),
                                                    sem("s_kc_read"), sem("s_vc_ready"))
        s_cqk, s_cs, s_ce, s_cp, s_ctr, s_cpt = (
            sem("s_cmp_logits"), sem("s_cmp_shifted"), sem("s_cmp_exp"), sem("s_cmp_weights"), sem("s_cmp_turned"),
            sem("s_cmp_wT"))
        s_nqk, s_nmx, s_np, s_nw, s_ntr, s_npt, s_npv, s_nm = (
            sem("s_nsa_logits"), sem("s_nsa_max"), sem("s_nsa_exp"), sem("s_nsa_weights"), sem("s_nsa_turned"),
            sem("s_nsa_wT"), sem("s_nsa_summed"), sem("s_nsa_out"))
        s_hlb, s_hlev = sem("s_lower"), sem("s_hgrn_operands")

        f32 = lambda ap: ap.bitcast(F32)

        def width(n):
            return BLOCKS[n]["kn"] * sum(c for _, c in BLOCKS[n]["spans"])

        def used_by_pe(n):
            if BLOCKS[n]["closing"]:
                return s_tile, DONE[BLOCKS[n]["tiles"][-1]]
            return s_blk, sum(not b["closing"] for b in BLOCKS[:n + 1])

        def ended(g):
            who, n = END[g]
            return s_end[who], n

        def sigmoid_ready(g):
            if READER[TILES[g][0]] == "S":
                return ended(g)
            return s_sg, sum(READER[TILES[x][0]] == "V" for x in SIG_TILES[:SIG_TILES.index(g) + 1])

        def end_sem(kind):
            who, n = end_of(kind)
            return s_end[who], n

        def norm_no(name, t):
            return NORMS.index((name, t)) + 1

        def norm_cols(name, t):
            n = {"y": 2, "qk": 12, "kc": 2, "hgrn": 4}.get(name, 1)
            return n * t, n

        def tile_of(kind, i):
            return TILES.index((kind, i))

        block = ctx.enter_context(nc.Block())

        @block.sync
        def _(sp):
            by_token = lambda ap: ap.rearrange("(a p) d -> p a d", p=P)
            for t in range(NT):
                sp.dma_start(xt[:, t, :], by_token(dram["x"])[:, t, :]).then_inc(s_x[t], 16)
            sp.dma_start(rows["x"], dram["norm_pre"]).then_inc(s_row["x"], 16)
            sp.dma_start(cst[:, :], dram["cst"]).then_inc(s_cst, 16)
            sp.dma_start(swraw[:, 0:NK * SH], dram["w_dt"]).then_inc(s_sw, 16)
            sp.dma_start(vec[:, :], dram["vec"]).then_inc(s_cst, 16)
            sp.dma_start(cstb[:, :], dram["cstb"]).then_inc(s_cst, 16)
            for n in range(NB):
                if n >= 2:
                    sp.wait_ge(s_lo, n - 1)
                cols = width(n)
                sp.dma_start(wraw[n % 2][:, 0:cols], dram["wblk"][n][:, 0:cols]).then_inc(s_w[n % 2], 16)
                if n == block_of("z") + 3:
                    sp.wait_ge(s_yd, 4 * NT)
                    sp.wait_ge(s_xd, 2 * NT)
                    sp.dma_start(rows["y"], dram["ssd_norm"]).then_inc(s_row["y"], 16)
                if n == LATE:
                    sp.wait_ge(s_pv, SH * NT)
                    sp.dma_start(xres, by_token(dram["x"])).then_inc(s_res, 16)
                    sp.dma_start(npost, dram["norm_post"]).then_inc(s_res, 16)
                    sp.dma_start(rows["mix"], dram["norm_mix"]).then_inc(s_row["mix"], 16)
                    sp.dma_start(w1[0].rearrange("p a b -> p (a b)"), dram["w1k"]).then_inc(s_late, 16)
                    sp.dma_start(w1[1].rearrange("p a b -> p (a b)"), dram["w1v"]).then_inc(s_late, 16)
                    sp.dma_start(cst[:, P:P + CST2.width], dram["cst2"]).then_inc(s_late, 16)
                    sp.dma_start(cstb[:, CSTB.at("after")], dram["upto"]).then_inc(s_late, 16)
                    sp.dma_start(stat[:, CMASK0:CMASK0 + P], dram["cmask"]).then_inc(s_late, 16)
                    sp.dma_start(swraw[:, :], dram["w_gates"]).then_inc(s_sw, 16)
                if n == block_of("kv") + 1:
                    for t in range(NT):
                        sp.wait_ge(s_norm, norm_no("out1", t))
                        sp.dma_start(by_token(spill)[:, t, :], xres[:, t, :]).then_inc(s_spill, 16)
                    sp.wait_ge(s_norm, norm_no("mix", NT - 1))
                    sp.dma_start(halves_f, dram["halves"]).then_inc(s_hc, 16)
                    sp.dma_start(onorm, dram["onorm"]).then_inc(s_hc, 16)
                if n == block_of("out2"):
                    sp.wait_ge(*ended(tile_of("hout", HH - 1)))
                    sp.wait_ge(s_split, SPLITS.index(("nsa", UNITS + 1)) + 1)
                    sp.wait_ge(s_spill, 16 * NT)
                    sp.dma_start(x2, by_token(spill)).then_inc(s_back, 16)
                    sp.dma_start(rows["ffn"], dram["norm_ffn"]).then_inc(s_row["ffn"], 16)
            for half in range(2):
                for t in range(NT):
                    sp.wait_ge(*ended(LAST_DOWN + 4 * half + t))
                    cols = slice(512 * half, 512 * half + 512)
                    sp.dma_start(by_token(out)[:, t, cols], x2[:, t, cols]).then_inc(s_out, 16)
            sp.wait_ge(s_out, 16 * 2 * NT)

        @block.tensor
        def _(pe):
            def mm(o, lhsT, rhs, start, stop, **kw):
                return nc.tensor.matmul(o, lhsT, rhs, start=start, stop=stop, **kw)

            def free_bank(g):
                if BEFORE[g] is not None:
                    pe.wait_ge(*ended(BEFORE[g]))

            def free_aux(key):
                if AUX.before(key):
                    who, n = AUX.before(key)
                    pe.wait_ge(s_auxend[who], n)
                return bank[4 + AUX.slot(key)]

            split = [0]

            def need_split(n):
                if n > split[0]:
                    pe.wait_ge(s_split, n)
                    split[0] = n

            def gemm(n, s):
                b, slot = BLOCKS[n], n % 2
                if s == 0:
                    pe.wait_ge(s_hi, n + 1)
                    pe.wait_ge(s_lo, n + 1)
                for j, k in sliced(b, s):
                    g = b["tiles"][j]
                    xh, xl = ACTS[b["srcs"][j]]
                    ps = bank[BANK[g]]
                    if g in opened(b, s) and k == 0:
                        free_bank(g)
                    need_split(SPLIT_NEED[n, j, k])
                    kk = b["kb"] + k
                    if b["form"] == "feature":
                        w = slice(256 * k + P * j, 256 * k + P * j + P)
                        pairs = [(whi[slot][:, w], xh[:, k, :]), (whi[slot][:, w], xl[:, k, :]),
                                 (wlo[slot][:, w], xh[:, k, :])]
                    else:
                        w, ts = slice(512 * k, 512 * k + 512), slice(P * j, P * j + P)
                        pairs = [(xh[:, kk, ts], whi[slot][:, w]), (xh[:, kk, ts], wlo[slot][:, w]),
                                 (xl[:, kk, ts], whi[slot][:, w])]
                    for i, (l, r) in enumerate(pairs):
                        last = mm(ps[:, :], l, r, kk == 0 and i == 0, kk == b["total"] - 1 and i == 2)
                    if k == b["kn"] - 1 and b["closing"]:
                        last.then_inc(s_tile, 1)
                if s == SLICES - 1 and not b["closing"]:
                    last.then_inc(s_blk, 1)

            def turn(name, t, half, g):
                src = {"x": xt, "y": xs, "mix": xn, "hgrn": mixt, "ffn": xn}[name]
                if (name, t, half) == ("x", 0, 0):
                    pe.wait_ge(s_cst, 48)
                pe.wait_ge(s_norm, norm_no(name, t))
                free_bank(g)
                c0 = 512 * half if name != "hgrn" else 0
                for i in range(4):
                    last = nc.tensor.transpose(bank[BANK[g]][:, P * i:P * i + P], src[:, t, c0 + P * i:c0 + P * i + P], ident)
                last.then_inc(s_tile, 1)

            def small_block(kind, g, cols):
                pe.wait_ge(s_slo, 1 if kind == "dt" else 2)
                need_split(SPLIT_NEED["small", kind])
                free_bank(g)
                ps = bank[BANK[g]]
                for t in range(NT):
                    for k in range(NK):
                        xh, xl = a_hi[:, k, P * t:P * t + P], a_lo[:, k, P * t:P * t + P]
                        h, l = swhi[:, cols * k:cols * k + cols], swlo[:, cols * k:cols * k + cols]
                        for i, (a, w) in enumerate(((xh, h), (xh, l), (xl, h))):
                            last = mm(ps[:, cols * t:cols * t + cols], a, w, k == 0 and i == 0, k == NK - 1 and i == 2)
                last.then_inc(s_tile, 1)

            def qkturn(i, g):
                pe.wait_ge(s_norm, norm_no("qk", NT - 1))
                free_bank(g)
                for t in range(NT):
                    src = qn_[:, t, i, :] if i < 4 else kst[:, t, P * (i - 4):P * (i - 4) + P]
                    last = nc.tensor.transpose(bank[BANK[g]][:, P * t:P * t + P], src, ident)
                last.then_inc(s_tile, 1)

            def positions():
                pe.wait_ge(s_late, 80)
                for b in range(2):
                    for j in range(CL // 2):
                        last = mm(bank[5][0:1, P * b:P * b + P], pos[:, b, j:j + 1], w1[b][:, j, :], j == 0, j == CL // 2 - 1)
                last.then_inc(s_pos, 1)

            def compress(i):
                if i == 0:
                    pe.wait_ge(s_kc2, 64)
                    pe.wait_ge(s_posr, 1)
                    for b in range(2):
                        o = bank[4][:, 64 * b:64 * b + 64].rearrange("p (a b) -> p a b", b=32)[:, :, 0:NCMP]
                        for j in range(CL // 2):
                            mm(o, w1[b][:, j, :], kc2[:, b, :, 2 * j:2 * j + CS * (NCMP - 1) + 1:CS], j == 0, False)
                        last = mm(o, posr[0:1, P * b:P * b + P], one[0:1, 0:2 * NCMP].rearrange("p (a b) -> p a b", b=NCMP),
                                  False, True)
                    last.then_inc(s_hid, 1)
                if i == 1:
                    pe.wait_ge(s_gelu, 2)
                    for g in range(NG):
                        last = mm(bank[6][0:32, HD * g:HD * g + HD], hid[:, 0, g, :], w2[:, 0, :], True, True)
                    last.then_inc(s_hid, 1)
                if i == 2:
                    pe.wait_ge(s_hid4, NG)
                    for g in range(NG):
                        last = mm(bank[7][:, HD * g:HD * g + HD], hid4[:, g, :, :].rearrange("p a b -> p (a b)"),
                                  w2[:, 1, :], True, True)
                    last.then_inc(s_hid, 1)
                if i == 3:
                    pe.wait_ge(s_norm, norm_no("kc", 0))
                    nc.tensor.transpose(bank[4][:, 0:32], kcn[0:32, :], ident[0:32, 0:32]).then_inc(s_kct, 1)

            def cmp(qt, i):
                if i == 0:
                    pe.wait_ge(s_kcr, 1)
                    if qt == 0:
                        pe.wait_ge(s_vcd, 1)
                        pe.wait_ge(*ended(tile_of("turn_qk", 5)))
                    if qt >= 1:
                        pe.wait_ge(s_cs, qt)
                    for h in range(NH):
                        g, r = divmod(h, 4)
                        rows_ = slice(HD * g, HD * g + HD)
                        last = mm(bank[4 + 3 * g][:, 32 * r:32 * r + NCMP], qT[rows_, r, P * qt:P * qt + P],
                                  kcT[rows_, 0:NCMP], True, True)
                    last.then_inc(s_cqk, 1)
                if i == 2:
                    pe.wait_ge(s_cp, qt + 1)
                    if qt >= 1:
                        pe.wait_ge(s_cpt, qt)
                    for g in range(NG):
                        last = nc.tensor.transpose(bank[5][:, P * g:P * g + P],
                                                   cs_[qt % 2][:, 4 * g:4 * g + 4, :].rearrange("p a b -> p (a b)"), ident)
                    last.then_inc(s_ctr, 1)

            def nsa(u):
                def turned(v, b):
                    kend = P * (v // NH + 1)
                    pe.wait_ge(s_nw, v + 1)
                    if 2 * v + b >= 1:
                        pe.wait_ge(s_npt, 2 * v + b)
                    for kb in range(kend // P):
                        last = nc.tensor.transpose(bank[BANK_WT][:, P * kb:P * kb + P], np_[:, v % 2, b, P * kb:P * kb + P], ident)
                    last.then_inc(s_ntr, 1)

                def summed(v, b):
                    qt, h = divmod(v, NH)
                    out_ = bank[BANK_O]
                    if h == 0 and b == 0:
                        if qt == 0:
                            pe.wait_ge(s_cpt, NT)
                            pe.wait_ge(s_zero, 2)
                        else:
                            pe.wait_ge(s_nm, qt)
                        mm(out_[:, :], identb, zerob[:, 0:1].to_broadcast([P, 512]), True, False, skip_group_check=True)
                        for c in range(4):
                            mm(out_[:, P * c:P * c + P], vcd[:, c // 2, 2 * (c % 2):2 * (c % 2) + 2, :].rearrange("p a b -> p (a b)"),
                               cpT[:, qt, c // 2, :], False, False, skip_group_check=True)
                    pe.wait_ge(s_npt, 2 * v + b + 1)
                    o = out_[HD * (h % 2):HD * (h % 2) + HD, P * (h // 2):P * (h // 2) + P]
                    for kb in range(qt + 1):
                        end = kb == qt and b == 1 and h == NH - 1
                        last = mm(o, vst[:, kb, P * b + HD * (h // 4):P * b + HD * (h // 4) + HD],
                                  npT[:, (2 * v + b) % 4, P * kb:P * kb + P], False, end, skip_group_check=True)
                    last.then_inc(s_npv, 1)

                if 0 <= u - 1 < UNITS:
                    turned(u - 1, 0)
                if u < UNITS:
                    qt, h = divmod(u, NH)
                    g, r = divmod(h, 4)
                    rows_, kend = slice(HD * g, HD * g + HD), P * (qt + 1)
                    if u == 0:
                        pe.wait_ge(s_cs, NT)
                        pe.wait_ge(s_cpt, NT)
                    if u >= 1:
                        pe.wait_ge(s_np, 2 * u)
                    for b in range(2):
                        ps = bank[BANK_LOGITS + b]
                        mm(ps[:, 0:kend], qT[rows_, r, P * qt:P * qt + P], kT[rows_, b, 0:kend], True, False)
                        mm(ps[:, kend - P:kend], identb, after, False, True).then_inc(s_nqk, 1)
                if 0 <= u - 2 < UNITS:
                    summed(u - 2, 1)
                if 0 <= u - 1 < UNITS:
                    turned(u - 1, 1)
                    summed(u - 1, 0)

            def level(h, n, g):
                q_, k_ = hqk[n % 2] if n else hset[h % 2][:2]
                pe.wait_ge(s_hlev, (LEVELS + 1) * h + n + 1)
                free_bank(g)
                ps, w = bank[BANK[g]], 2 ** (n - 1) if n else 0
                if w < P:
                    up = lambda ap: ap.rearrange("p (a b c) -> p a b c", b=2, c=w)[:, :, 1, :] if w else ap
                    for t in range(NT):
                        ts = slice(P * t, P * t + P)
                        last = mm(up(ps[:, ts]), k_[:, ts], up(q_[:, ts]), True, True)
                elif w == P:
                    for i in range(2):
                        last = mm(ps[:, P * i:P * i + P], k_[:, 2 * P * i:2 * P * i + P],
                                  q_[:, 2 * P * i + P:2 * P * i + 2 * P], True, True)
                else:
                    for i in range(2):
                        last = mm(ps[:, 256 * i:256 * i + 256], k_[:, P * i:P * i + P], q_[:, 256:512], True, True)
                last.then_inc(s_tile, 1)

            def hout(h, g):
                pe.wait_ge(*ended(level_tile(h, LEVELS)))
                pe.wait_ge(*ended(tile_of("hi", (NT - 1, 0))))
                free_bank(g)
                for t in range(NT):
                    for s_ in range(t + 1):
                        if s_ == t:
                            lhs = hat[:, P * t:P * t + P]
                        elif t >= 2 and s_ < 2:
                            lhs = hat[:, 768 + 256 * s_ + P * (t - 2):768 + 256 * s_ + P * (t - 2) + P]
                        else:
                            lhs = hat[:, 512 + P * (t // 2):512 + P * (t // 2) + P]
                        last = mm(bank[BANK[g]][:, P * t:P * t + P], lhs, hit[:, s_, P * h:P * h + P], s_ == 0, s_ == t)
                last.then_inc(s_tile, 1)

            def xturn(c):
                pe.wait_ge(s_cx, c + 1)
                ps = free_aux(("xturn", c))
                src = cx[:, c % 2, :] if c < 8 else bct[:, c - 8, :]
                for t in range(NT):
                    last = nc.tensor.transpose(ps[:, P * t:P * t + P], src[:, P * t:P * t + P], ident)
                last.then_inc(s_aux, 1)

            def ssd_decay():
                pe.wait_ge(s_dt, 1)
                ps = free_aux("decay")
                mm(ps[:, 0:64], tri, adt, True, True)
                mm(ps[:, 64:128], ones, adt, True, True).then_inc(s_aux, 1)

            def ssd(c, part):
                ts = slice(P * c, P * c + P)

                def y_diag(j):
                    pe.wait_ge(s_attn, 4 * c + j + 1)
                    if j == 0:
                        pe.wait_ge(s_xd, 2 * c + 1)
                        if c >= 1:
                            pe.wait_ge(s_y, c)
                    for i in range(4):
                        h = 4 * j + i
                        last = mm(bank[6 + j // 2][:, (h % 8) * HD:(h % 8) * HD + HD], ee[:, j % 2, i, :],
                                  xdt[:, c % 2, h * HD:h * HD + HD], True, True)
                    last.then_inc(s_yd, 1)

                if part == 0:
                    pe.wait_ge(s_cx, XC)
                    ps = free_aux(("scores", c))
                    for g in range(2):
                        last = mm(ps[:, P * g:P * g + P], bct[:, g, ts], bct[:, 2 + g, ts], True, True)
                    last.then_inc(s_aux, 1)
                if part < 4:
                    pe.wait_ge(s_dt, 1)
                    ps = free_aux(("decay", c, part))
                    mm(ps[:, :], identb, after.unsqueeze(1).to_broadcast([P, 4, P]), True, False)
                    for i in range(4):
                        col = SH * c + 4 * part + i
                        last = mm(ps[:, P * i:P * i + P], adt[:, col:col + 1].to_broadcast([P, P]), tri, False, i == 3)
                    last.then_inc(s_aux, 1)
                    if part >= 1:
                        y_diag(part - 1)
                if part == 4:
                    if c > 0:
                        pe.wait_ge(s_st, 2 * c)
                        for g in range(2):
                            ps = free_aux(("y_off", c, g))
                            mm(ps[:, :], bct[:, 2 + g, ts], state[:, g, :], True, True).then_inc(s_aux, 1)
                    y_diag(3)
                    if c < NT - 1:
                        pe.wait_ge(s_xd, 2 * c + 2)
                        for g in range(2):
                            ps = free_aux(("state", c, g))
                            mm(ps[:, :], btok[:, c, P * g:P * g + P], xdd[:, 512 * g:512 * g + 512], True, True)\
                                .then_inc(s_aux, 1)

            def stick(u):
                if u < SH * NT:
                    h, qt = divmod(u, NT)
                    rows, kend = slice(HD * (h % 2), HD * (h % 2) + HD), P * (qt + 1)
                    if u >= 2:
                        pe.wait_ge(s_sig, u - 1)
                    ps = bank[BANK_LOGITS + u % 2]
                    if u == 0:
                        pe.wait_ge(*end_sem("v"))
                        need_split(max(SPLITS.index(x) for x in SPLITS if x[:2] == ("turn", "y")) + 1)
                    mm(ps[:, 0:kend], qf[rows, h // 2, P * qt:P * qt + P], kf[rows, h // 2, 0:kend], True, False)
                    mm(ps[:, kend - P:kend], identb, strict, False, True).then_inc(s_qk, 1)
                v = u - SB_LAG
                if 0 <= v < SH * NT:
                    pe.wait_ge(s_wgt, v + 1)
                    if v >= 1:
                        pe.wait_ge(s_wT, v)
                    for kb in range(v % NT + 1):
                        last = nc.tensor.transpose(bank[BANK_WT][:, P * kb:P * kb + P], sb_w[:, v % 3, P * kb:P * kb + P], ident)
                    last.then_inc(s_tr, 1)
                v = u - SB_LAG - 1
                if 0 <= v < SH * NT:
                    h, qt = divmod(v, NT)
                    rows = slice(HD * (h % 2), HD * (h % 2) + HD)
                    pe.wait_ge(s_wT, v + 1)
                    if v >= 1:
                        pe.wait_ge(s_o, v)
                    for kb in range(qt + 1):
                        last = mm(bank[BANK_O][rows, P * (v % 4):P * (v % 4) + P], vt[:, kb, h * HD:h * HD + HD],
                                  sb_wT[:, v % 2, P * kb:P * kb + P], kb == 0, kb == qt)
                    last.then_inc(s_pv, 1)

            for s in STEPS:
                if s[0] == "gemm":
                    gemm(*s[1:])
                if s[0] == "turn":
                    turn(*s[1:])
                if s[0] == "small":
                    small_block(s[1], s[2], SH if s[1] == "dt" else 24)
                if s[0] == "qkturn":
                    qkturn(*s[1:])
                if s[0] == "pos":
                    positions()
                if s[0] == "compress":
                    compress(s[1])
                if s[0] == "cmp":
                    cmp(*s[1:])
                if s[0] == "nsa":
                    nsa(s[1])
                if s[0] == "level":
                    level(*s[1:])
                if s[0] == "hout":
                    hout(*s[1:])
                if s[0] == "xturn":
                    xturn(s[1])
                if s[0] == "ssd_decay":
                    ssd_decay()
                if s[0] == "ssd":
                    ssd(s[1], s[2])
                if s[0] == "sb":
                    stick(s[1])

        @block.scalar
        def _(act):
            A = nc.scalar.activation
            chain = [0]

            def link(ins):
                chain[0] += 1
                ins.then_inc(s_ac, 1)
                act.wait_ge(s_ac, chain[0])

            def round_weights(n):
                if n >= NB:
                    return
                act.wait_ge(s_w[n % 2], 16 * (n // 2 + 1))
                if n >= 2:
                    act.wait_ge(*used_by_pe(n - 2))
                cols = width(n)
                A(whi[n % 2][:, 0:cols], wraw[n % 2][:, 0:cols], ACT.Copy).then_inc(s_hi, 1)

            def round_small(kind):
                cols = NK * (SH if kind == "dt" else 24)
                act.wait_ge(s_sw, 16 if kind == "dt" else 32)
                if kind == "gates":
                    act.wait_ge(s_tile, DONE[tile_of("dt", 0)])
                A(swhi[:, 0:cols], swraw[:, 0:cols], ACT.Copy).then_inc(s_shi, 1)

            def sigmoid(g, kind, i):
                k = SIG_TILES.index(g)
                if k >= 2:
                    o = SIG_TILES[k - 2]
                    act.wait_ge(*ended(o + CONSUMER[TILES[o][0]]))
                bias = 0.0
                if kind in ("gate", "gate2"):
                    bias = V("b_gate", i + (8 if kind == "gate2" else 0))
                ins = A(sgt[:, k % 2, :], bank[BANK[g]][:, :], ACT.Sigmoid, bias=bias)
                ins.then_inc(s_end["S"] if READER[kind] == "S" else s_sg, 1)

            def conv_sigmoid(i):
                act.wait_ge(s_conv, i + 1)
                if i >= 2:
                    act.wait_ge(s_cx, i - 1)
                A(csig[:, i % 2, :], cacc[:, i % 2, :], ACT.Sigmoid).then_inc(s_csig, 1)

            def tile(g):
                kind, i = TILES[g]
                ps = bank[BANK[g]]
                if kind in ("dt", "y_ssd", "y_sb", "out2", "down"):
                    return
                act.wait_ge(s_tile, DONE[g])
                if kind == "xbc":
                    if i >= 2:
                        act.wait_ge(s_conv, i - 1)
                    A(craw[:, i % 2, :], ps[:, :], ACT.Copy).then_inc(s_end["S"], 1)
                    if i >= 1:
                        conv_sigmoid(i - 1)
                    if i == XC - 1:
                        conv_sigmoid(i)
                if kind in SIGMOID:
                    if kind == "z" and i == (0, 0):
                        act.wait_ge(s_y, NT)
                    sigmoid(g, kind, i)
                if kind in ("z_sb", "ff_up"):
                    p = PRODUCTS.index(("tile", g))
                    act.wait_ge(s_t, T_READY[p])
                    c = i if kind == "z_sb" else i[1]
                    A(b_hi[:, c, :], tt[:, p % 2, :], ACT.Copy).then_inc(s_tround, 1)
                if kind == "kv":
                    src = ps[:, :].rearrange("p (a b c) -> p a b c", b=2, c=P)
                    pair = lambda ap: ap.rearrange("p (a b) -> p a b", b=P)
                    A(pair(kst[:, i[0], :]), src[:, :, 0, :], ACT.Copy)
                    A(pair(vst[:, i[0], :]), src[:, :, 1, :], ACT.Copy).then_inc(s_end["S"], 1)
                if kind == "qn":
                    A(qt_[:, i[0], :], ps[:, :], ACT.Copy).then_inc(s_end["S"], 1)
                if kind == "kcv":
                    A(kcf[:, i, :], ps[:, :], ACT.Copy).then_inc(s_end["S"], 1)
                    if i == 1:
                        act.wait_ge(*ended(g))
                        for g_ in range(NG):
                            for later in range(2):
                                act.dma_start(kc2[HD * later:HD * later + HD, :, g_, 0:T - later],
                                              kcf[HD * g_:HD * g_ + HD, :, later:T]).then_inc(s_kc2, 16)
                if kind == "hi":
                    A(hit[:, i[0], :], ps[:, :], ACT.Copy).then_inc(s_end["S"], 1)
                if kind == "k":
                    A(kf[:, i, :], ps[:, :], ACT.Copy).then_inc(s_end["S"], 1)
                if kind == "q":
                    A(qf[:, i, :], ps[:, :], ACT.Copy).then_inc(s_end["S"], 1)
                if kind == "v":
                    t, half = i
                    A(vt[:, t, 512 * half:512 * half + 512], ps[:, :], ACT.Copy).then_inc(s_end["S"], 1)
                if kind == "out1":
                    t, half = i
                    A(oraw[:, t, 512 * half:512 * half + 512], ps[:, :], ACT.Copy)
                    if i == (0, 0):
                        act.wait_ge(s_mg, NK)
                    link(A(sgt[:, 0, :], ps[:, :], ACT.Square, accum_out=sso[:, 2 * t + half:2 * t + half + 1]))
                    act.sem_inc(s_end["S"], 1)

            def root(name, t):
                act.wait_ge(s_rec, norm_no(name, t))
                a, n = norm_cols(name, t)
                r = nss[name][0:32 if name == "kc" else P, a:a + n]
                A(r, r, ACT.Sqrt).then_inc(s_rt, 1)

            def norm(name, t):
                if name == "x":
                    act.wait_ge(s_x[t], 16)
                if name == "y":
                    act.wait_ge(s_yz, NT + t + 1)
                if name == "mix":
                    act.wait_ge(s_norm, norm_no("out1", t))
                if name == "ffn":
                    act.wait_ge(*ended(tile_of("out2", (t, 1))))
                src, junk = {"x": (xt, junks["x"]), "y": (xs, junks["y"]), "mix": (xres, xn), "ffn": (x2, xn)}.get(name, (0, 0))
                if name == "y":
                    for g in range(2):
                        cols = slice(512 * g, 512 * g + 512)
                        last = A(junk[:, t, cols], src[:, t, cols], ACT.Square, accum_out=nss[name][:, 2 * t + g:2 * t + g + 1])
                    last.then_inc(s_ss, 1)
                elif name in SQUARED:
                    A(junk[:, t, :], src[:, t, :], ACT.Square, accum_out=nss[name][:, t:t + 1]).then_inc(s_ss, 1)
                root(name, t)

            def turn(name, t, half, g):
                act.wait_ge(s_tile, DONE[g])
                A(ACTS[FILLS[name]][0][:, 4 * half:4 * half + 4, P * t:P * t + P],
                  bank[BANK[g]][:, :].rearrange("p (a b) -> p a b", b=P), ACT.Copy).then_inc(s_round, 1)

            def stick(u):
                if u < SH * NT:
                    kend = P * (u % NT + 1)
                    act.wait_ge(s_qk, u + 1)
                    if u >= 2:
                        act.wait_ge(s_wgt, u - 1)
                    ps = bank[BANK_LOGITS + u % 2]
                    f0 = 516 * (u % 2)
                    if u < 2:
                        act.wait_ge(s_zero, 1)
                    A(sb_sig[:, u % 2, 0:kend], ps[:, 0:kend], ACT.Sigmoid, scale=SCALE)
                    A(sb_fail[:, f0 + 512 - kend:f0 + 512], ps[:, 0:kend], ACT.Sigmoid, scale=-SCALE).then_inc(s_sig, 1)
                v = u - SB_LAG
                if 0 <= v < SH * NT:
                    kend = P * (v % NT + 1)
                    act.wait_ge(s_tr, v + 1)
                    if v >= 2:
                        act.wait_ge(s_pv, v - 1)
                    A(sb_wT[:, v % 2, 0:kend], bank[BANK_WT][:, 0:kend], ACT.Copy).then_inc(s_wT, 1)

            def small_dt():
                act.wait_ge(s_dte, 1)
                A(t64[1], t64[1], ACT.Exp).then_inc(s_ex, 1)
                A(aexp, V("a_log", 0, SH), ACT.Exp).then_inc(s_ex, 1)
                act.wait_ge(s_dte, 2)
                A(t64[1], t64[1], ACT.Ln).then_inc(s_ex, 1)

            def small_gates(g):
                act.wait_ge(s_tile, DONE[g])
                A(gl, bank[BANK[g]][:, 0:96], ACT.Sigmoid).then_inc(s_end["S"], 1)
                act.wait_ge(s_hlb, 1)
                A(lbs, lbs, ACT.Sigmoid).then_inc(s_hlb, 1)

            def compress(i):
                if i == 0:
                    act.wait_ge(s_hidz, 1)
                    act.wait_ge(s_hid, 1)
                    for b in range(2):
                        A(hid[:, b, :, 0:NCMP], bank[4][:, 64 * b:64 * b + 64].rearrange("p (a b) -> p a b", b=32)[:, :, 0:NCMP],
                          ACT.Gelu_apprx_tanh).then_inc(s_gelu, 1)
                if i == 1:
                    root("kc", 0)
                if i == 3:
                    act.wait_ge(s_kct, 1)
                    A(kcT, bank[4][:, 0:32], ACT.Copy, scale=V("k_norm", 0)).then_inc(s_kcr, 1)

            def cmp(qt, i):
                if i == 0:
                    act.wait_ge(s_cs, qt + 1)
                    A(cs_[qt % 2][:, :, :], cs_[qt % 2][:, :, :], ACT.Exp, scale=SCALE).then_inc(s_ce, 1)
                if i == 2:
                    act.wait_ge(s_ctr, qt + 1)
                    A(cpT[:, qt, :, :], bank[5][:, 0:256].rearrange("p (a b) -> p a b", b=P), ACT.Copy).then_inc(s_cpt, 1)

            def nsa(u):
                def read_turned(v, b):
                    kend = P * (v // NH + 1)
                    act.wait_ge(s_ntr, 2 * v + b + 1)
                    if v >= 2:
                        act.wait_ge(s_npv, 2 * v + b - 3)
                    A(npT[:, (2 * v + b) % 4, 0:kend], bank[BANK_WT][:, 0:kend], ACT.Copy).then_inc(s_npt, 1)

                if 0 <= u - 1 < UNITS:
                    read_turned(u - 1, 0)
                if u < UNITS:
                    kend = P * (u // NH + 1)
                    act.wait_ge(s_nmx, u + 1)
                    if u >= 2:
                        act.wait_ge(s_ntr, 2 * (u - 1))
                    for b in range(2):
                        A(np_[:, u % 2, b, 0:kend], bank[BANK_LOGITS + b][:, 0:kend], ACT.Exp, scale=SCALE,
                          bias=nmx[:, 2 * u + b:2 * u + b + 1], accum_out=nsum[:, 2 * u + b:2 * u + b + 1]).then_inc(s_np, 1)
                if u >= 2 and (u - 2) % NH == NH - 1:
                    qt = (u - 2) // NH
                    act.wait_ge(s_npv, 2 * (u - 1))
                    A(b_hi[:, 0:4, P * qt:P * qt + P], bank[BANK_O][:, :].rearrange("p (a b) -> p a b", b=P), ACT.Copy)\
                        .then_inc(s_round, 1)
                if 0 <= u - 1 < UNITS:
                    read_turned(u - 1, 1)

            for n, s in enumerate(STEPS):
                if n == NT:
                    round_small("dt")
                    round_weights(0)
                if s[0] == "small":
                    small_dt() if s[1] == "dt" else small_gates(s[2])
                if s[0] == "pos":
                    round_small("gates")
                    act.wait_ge(s_pos, 1)
                    A(posr[0:1, :], bank[5][0:1, 0:2 * P], ACT.Copy).then_inc(s_posr, 1)
                if s[0] == "qkturn":
                    i, g = s[1:]
                    act.wait_ge(s_tile, DONE[g])
                    dst = qT[:, i, :] if i < 4 else kT[:, i - 4, :]
                    A(dst, bank[BANK[g]][:, :], ACT.Copy,
                      scale=V("q_norm") if i < 4 else V("k_norm", i - 3)).then_inc(s_end["S"], 1)
                if s[0] == "compress":
                    compress(s[1])
                if s[0] == "cmp":
                    cmp(*s[1:])
                if s[0] == "nsa":
                    nsa(s[1])
                if s[0] == "hout":
                    h, g = s[1:]
                    act.wait_ge(s_tile, DONE[g])
                    A(mixt[:, :, P * h:P * h + P], bank[BANK[g]][:, :].rearrange("p (a b) -> p a b", b=P), ACT.Copy)\
                        .then_inc(s_end["S"], 1)
                if s[0] == "norm":
                    norm(*s[1:])
                if s[0] == "turn":
                    turn(*s[1:])
                if s[0] == "gemm":
                    if s[2] == 0:
                        round_weights(s[1] + 1)
                    for g in closed(BLOCKS[s[1]], s[2]):
                        tile(g)
                if s[0] == "xturn":
                    c = s[1]
                    act.wait_ge(s_aux, AUX.at[("xturn", c)] + 1)
                    dst = xs[:, :, P * c:P * c + P] if c < 8 else btok[:, :, P * (c - 8):P * (c - 8) + P]
                    A(dst, bank[4 + AUX.slot(("xturn", c))][:, :].rearrange("p (a b) -> p a b", b=P), ACT.Copy)\
                        .then_inc(s_auxend["S"], 1)
                if s[0] == "ssd_decay":
                    act.wait_ge(s_dte, 3)
                    A(ecs, t64[0], ACT.Exp)
                    A(edec, t64[1], ACT.Exp)
                    A(dtend, t64[2], ACT.Exp).then_inc(s_ex, 1)
                if s[0] == "ssd" and s[2] < 4:
                    _, c, j = s
                    key = ("decay", c, j)
                    act.wait_ge(s_aux, AUX.at[key] + 1)
                    n_ = 4 * c + j
                    if n_ >= 2:
                        act.wait_ge(s_yd, n_ - 1)
                    for i in range(4):
                        col = SH * c + 4 * j + i
                        last = A(ee[:, j % 2, i, :], bank[4 + AUX.slot(key)][:, P * i:P * i + P], ACT.Exp,
                                 bias=acs_n[:, col:col + 1])
                    last.then_inc(s_auxend["S"], 1)
                if s[0] == "sb":
                    stick(s[1])
                if s[0] == "merge":
                    c = s[1]
                    if c == 0:
                        act.wait_ge(*used_by_pe(MERGE_AFTER))
                        act.wait_ge(s_mg, NK)
                    A(a_hi[:, c, :], mg[:, c, :], ACT.Copy).then_inc(s_tround, 1)

        @block.vector
        def _(dve):
            v = nc.vector
            chain = [0]
            h64 = lambda ap: ap.rearrange("p (a b) -> p a b", b=HD)

            def link(ins):
                chain[0] += 1
                ins.then_inc(s_vc, 1)
                dve.wait_ge(s_vc, chain[0])

            def rest_of_weights(n):
                if n >= NB:
                    return
                dve.wait_ge(s_hi, n + 1)
                cols = width(n)
                v.tensor_tensor(wlo[n % 2][:, 0:cols], wraw[n % 2][:, 0:cols], f32(whi[n % 2][:, 0:cols]),
                                ALU.subtract).then_inc(s_lo, 1)

            def rest_of_small(kind):
                dve.wait_ge(s_shi, 1 if kind == "dt" else 2)
                cols = NK * (SH if kind == "dt" else 24)
                v.tensor_tensor(swlo[:, 0:cols], swraw[:, 0:cols], f32(swhi[:, 0:cols]), ALU.subtract).then_inc(s_slo, 1)

            def conv(i, g):
                dve.wait_ge(*ended(g))
                if i == 0:
                    dve.wait_ge(s_cst, 48)
                if i >= 2:
                    dve.wait_ge(s_cx, i - 1)
                acc, x_ = cacc[:, i % 2, :], craw[:, i % 2, :]
                link(v.tensor_scalar(acc, x_, V("conv_w", 4 * i + 3), V("conv_b", i), ALU.mult, ALU.add))
                for j in (1, 2, 3):
                    ins = v.scalar_tensor_tensor(acc[:, j:T], x_[:, 0:T - j], V("conv_w", 4 * i + 3 - j),
                                                 acc[:, j:T], ALU.mult, ALU.add)
                    if j < 3:
                        link(ins)
                ins.then_inc(s_conv, 1)

            def silu(i):
                dve.wait_ge(s_csig, i + 1)
                if 2 <= i < 8:
                    dve.wait_ge(s_aux, AUX.at[("xturn", i - 2)] + 1)
                dst = cx[:, i % 2, :] if i < 8 else bct[:, i - 8, :]
                v.tensor_tensor(dst, cacc[:, i % 2, :], csig[:, i % 2, :], ALU.mult).then_inc(s_cx, 1)

            def tile(g):
                kind, i = TILES[g]
                ps = bank[BANK[g]]
                if kind == "xbc":
                    conv(i, g)
                    if i >= 1:
                        silu(i - 1)
                    if i == XC - 1:
                        silu(i)
                if kind == "z":
                    t, half = i
                    sg = sgt[:, SIG_TILES.index(g) % 2, :]
                    y = xs[:, t, 512 * half:512 * half + 512]
                    dve.wait_ge(*sigmoid_ready(g))
                    link(v.tensor_tensor(sg, ps[:, :], sg, ALU.mult))
                    v.tensor_tensor(y, y, sg, ALU.mult).then_inc(s_yz, 1)
                    dve.wait_ge(s_yz, 4 * half + t + 1)
                    dve.sem_inc(s_end["V"], 1)
                if kind in ("y_ssd", "y_sb"):
                    dve.wait_ge(s_tile, DONE[g])
                    k = SIG_TILES.index(g - 1)
                    dve.wait_ge(*sigmoid_ready(g - 1))
                    sg = sgt[:, k % 2, :]
                    if kind == "y_ssd":
                        v.tensor_tensor(mg[:, i, :], ps[:, :], sg, ALU.mult).then_inc(s_end["V"], 1)
                    else:
                        link(v.tensor_tensor(sg, ps[:, :], sg, ALU.mult))
                        v.tensor_tensor(mg[:, i, :], mg[:, i, :], sg, ALU.add).then_inc(s_mg, 1)
                        dve.wait_ge(s_mg, i + 1)
                        dve.sem_inc(s_end["V"], 1)
                if kind == "hg":
                    o = hgt[:, i[0], :].rearrange("p (a b) -> p a b", b=P)
                    dve.wait_ge(*sigmoid_ready(g))
                    link(v.tensor_tensor(hgt[:, i[0], :], ps[:, :], sgt[:, SIG_TILES.index(g) % 2, :], ALU.mult))
                    dve.sem_inc(s_end["V"], 1)
                    link(v.tensor_tensor(o, o, onorm.unsqueeze(1).to_broadcast([P, 4, P]), ALU.mult))
                if kind == "hq":
                    dve.wait_ge(*sigmoid_ready(g))
                    if i == 0:
                        dve.wait_ge(s_hid, 1)
                    if i == 1:
                        dve.wait_ge(s_ctr, NT)
                    v.tensor_tensor(hset[i % 2][0], ps[:, :], sgt[:, SIG_TILES.index(g) % 2, :], ALU.mult)\
                        .then_inc(s_end["V"], 1)
                if kind == "hf":
                    dve.wait_ge(*sigmoid_ready(g))
                    _, hk_, pre, suf = hset[i % 2]
                    link(v.tensor_scalar(pre, sgt[:, SIG_TILES.index(g) % 2, :], lbn[:, i:i + 1], lbs[:, i:i + 1],
                                         ALU.mult, ALU.add))
                    dve.sem_inc(s_end["V"], 1)
                    v.tensor_scalar(hk_, pre, -1.0, 1.0, ALU.mult, ALU.add).then_inc(s_hlev, 1)
                if kind in ("out2", "down"):
                    t, half = i if kind == "out2" else (i[0], i[1][1])
                    dve.wait_ge(s_tile, DONE[g])
                    if kind == "out2":
                        dve.wait_ge(s_back, 16)
                    x = x2[:, t, 512 * half:512 * half + 512]
                    v.tensor_tensor(x, x, ps[:, :], ALU.add).then_inc(s_end["V"], 1)
                if kind == "ff_gate":
                    dve.wait_ge(*sigmoid_ready(g))
                    sg = sgt[:, SIG_TILES.index(g) % 2, :]
                    link(v.tensor_tensor(sg, sg, ps[:, :], ALU.mult))
                    dve.sem_inc(s_end["V"], 1)
                if kind == "ff_up":
                    p = PRODUCTS.index(("tile", g))
                    dve.wait_ge(s_tile, DONE[g])
                    sg = sgt[:, SIG_TILES.index(g - 1) % 2, :]
                    v.tensor_tensor(tt[:, p % 2, :], sg, ps[:, :], ALU.mult).then_inc(s_t, 1)
                    dve.wait_ge(s_t, T_READY[p])
                    dve.sem_inc(s_end["V"], 1)
                    dve.wait_ge(s_tround, p + 1)
                    v.tensor_tensor(b_lo[:, i[1], :], tt[:, p % 2, :], f32(b_hi[:, i[1], :]), ALU.subtract).then_inc(s_split, 1)
                if kind == "z_sb":
                    k = SIG_TILES.index(g)
                    p = PRODUCTS.index(("tile", g))
                    dve.wait_ge(*sigmoid_ready(g))
                    if i == 0:
                        dve.wait_ge(s_tr, SH * NT)
                        dve.wait_ge(s_o, SH * NT)
                    link(v.tensor_tensor(sgt[:, k % 2, :], ps[:, :], sgt[:, k % 2, :], ALU.mult))
                    v.tensor_tensor(tt[:, p % 2, :], qf[:, i, :], sgt[:, k % 2, :], ALU.mult).then_inc(s_t, 1)
                    dve.wait_ge(s_t, T_READY[p])
                    dve.sem_inc(s_end["V"], 1)
                    dve.wait_ge(s_tround, p + 1)
                    v.tensor_tensor(b_lo[:, i, :], tt[:, p % 2, :], f32(b_hi[:, i, :]), ALU.subtract).then_inc(s_split, 1)

            def norm(name, t):
                a, n = norm_cols(name, t)
                r = nss[name][0:32 if name == "kc" else P, a:a + n]
                w = {"y": 512, "qk": HD, "kc": HD, "hgrn": P}.get(name, D)
                ts = slice(P * t, P * t + P)
                if name == "out1":
                    dve.wait_ge(*ended(tile_of("out1", (t, 1))))
                    link(v.tensor_tensor(r, sso[:, 2 * t:2 * t + 1], sso[:, 2 * t + 1:2 * t + 2], ALU.add))
                elif name in SQUARED:
                    dve.wait_ge(s_ss, sum(x[0] in SQUARED for x in NORMS[:norm_no(name, t)]))
                elif name == "qk":
                    if t == 0:
                        dve.wait_ge(s_spill, 16 * NT)
                    dve.wait_ge(*ended(tile_of("kv", (t, 0))))
                    dve.wait_ge(*ended(tile_of("qn", (t, 0))))
                    link(v.tensor_tensor(sq_, qt_[:, t, :], qt_[:, t, :], ALU.mult))
                    link(v.tensor_reduce(r[:, 0:8], h64(sq_), AX.X, ALU.add))
                    link(v.tensor_tensor(sq_[:, 0:256], kst[:, t, :], kst[:, t, :], ALU.mult))
                    link(v.tensor_reduce(r[:, 8:12], h64(sq_[:, 0:256]), AX.X, ALU.add))
                elif name == "kc":
                    dve.wait_ge(s_hid, 2)
                    link(v.tensor_copy(kcn[0:32, :], bank[6][0:32, 0:P]))
                    link(v.tensor_tensor(nsq[0:32, :], kcn[0:32, :], kcn[0:32, :], ALU.mult))
                    link(v.tensor_reduce(r, h64(nsq[0:32, :]), AX.X, ALU.add))
                else:
                    dve.wait_ge(*ended(tile_of("hout", HH - 1)))
                    link(v.tensor_tensor(hsq, mixt[:, t, :], mixt[:, t, :], ALU.mult))
                    link(v.tensor_reduce(r, hsq.rearrange("p (a b) -> p a b", b=P), AX.X, ALU.add))
                link(v.tensor_scalar(r, r, 1.0 / w, EPS, ALU.mult, ALU.add))
                v.reciprocal(r, r).then_inc(s_rec, 1)
                dve.wait_ge(s_rt, norm_no(name, t))
                if name in ROWS:
                    dve.wait_ge(s_row[name], 16)
                if name == "x":
                    last = v.scalar_tensor_tensor(xt[:, t, :], xt[:, t, :], r, rows["x"], ALU.mult, ALU.mult)
                if name == "y":
                    for g in range(2):
                        y = xs[:, t, 512 * g:512 * g + 512]
                        last = v.scalar_tensor_tensor(y, y, r[:, g:g + 1], rows["y"][:, 512 * g:512 * g + 512], ALU.mult, ALU.mult)
                if name in ("mix", "ffn"):
                    src = {"mix": xres, "ffn": x2}[name]
                    last = v.scalar_tensor_tensor(xn[:, t, :], src[:, t, :], r, rows[name], ALU.mult, ALU.mult)
                if name == "qk":
                    for g in range(NG):
                        v.tensor_tensor(qn_[:, t, :, HD * g:HD * g + HD], h64(qt_[:, t, 256 * g:256 * g + 256]),
                                        r[:, 4 * g:4 * g + 4].unsqueeze(2).to_broadcast([P, 4, HD]), ALU.mult)
                    k = h64(kst[:, t, :])
                    last = v.tensor_tensor(k, k, r[:, 8:12].unsqueeze(2).to_broadcast([P, 4, HD]), ALU.mult)
                if name == "kc":
                    k = h64(kcn[0:32, :])
                    last = v.tensor_tensor(k, k, r.unsqueeze(2).to_broadcast([32, 2, HD]), ALU.mult)
                if name == "hgrn":
                    o = mixt[:, t, :].rearrange("p (a b) -> p a b", b=P)
                    link(v.tensor_tensor(o, o, r.unsqueeze(2).to_broadcast([P, 4, P]), ALU.mult))
                    last = v.tensor_tensor(mixt[:, t, :], mixt[:, t, :], hgt[:, t, :], ALU.mult)
                if name == "out1":
                    dve.wait_ge(s_res, 32)
                    link(v.scalar_tensor_tensor(oraw[:, t, :], oraw[:, t, :], r, npost, ALU.mult, ALU.mult))
                    last = v.tensor_tensor(xres[:, t, :], xres[:, t, :], oraw[:, t, :], ALU.add)
                last.then_inc(s_norm, 1)

            def split_turned(s, dst, chunks, t, bank_):
                ts = slice(P * t, P * t + P)
                hi, lo = ACTS[dst]
                dve.wait_ge(s_round, TURNS.index(s) + 1)
                v.tensor_tensor(lo[:, chunks, ts], bank_[:, :].rearrange("p (a b) -> p a b", b=P), f32(hi[:, chunks, ts]),
                                ALU.subtract).then_inc(s_split, 1)
                dve.wait_ge(s_split, SPLITS.index(s) + 1)

            def small_gates():
                dve.wait_ge(s_hlb, 2)
                link(v.tensor_scalar(lbn, lbs, -1.0, 1.0, ALU.mult, ALU.add))

            def compress(i):
                if i == 0:
                    v.memset(hid, 0.0).then_inc(s_hidz, 1)
                    dve.wait_ge(s_gelu, 2)
                    for g in range(NG):
                        v.tensor_copy(hid4[:, g, :, :], hid[:, 1, g, :].unsqueeze(1).to_broadcast([P, 4, 32])).then_inc(s_hid4, 1)
                if i == 1:
                    norm("kc", 0)
                if i == 2:
                    dve.wait_ge(s_hid, 3)
                    for g in range(NG):
                        last = v.tensor_tensor(vcd[:, g, :, :], bank[7][:, HD * g:HD * g + HD].unsqueeze(1).to_broadcast([P, 4, HD]),
                                               heads4.unsqueeze(2).to_broadcast([P, 4, HD]), ALU.mult)
                    last.then_inc(s_vcd, 1)

            def cmp(qt, i):
                s3 = cs_[qt % 2]
                n3 = s3[:, :, 0:NCMP]
                mx, sm = cmx[:, 8 * (qt % 2):8 * (qt % 2) + 8], csum[:, 8 * (qt % 2):8 * (qt % 2) + 8]
                gate = gl[:, 24 * qt:24 * qt + 24].rearrange("p (a b) -> p b a", b=3)[:, 0, :]
                if i == 0:
                    if qt >= 2:
                        dve.wait_ge(s_ctr, qt - 1)
                    link(v.memset(s3, NEG))
                    dve.wait_ge(s_cqk, qt + 1)
                    for g in range(NG):
                        link(v.tensor_tensor(n3[:, 4 * g:4 * g + 4, :],
                                             bank[4 + 3 * g][:, 0:P].rearrange("p (a b) -> p a b", b=32)[:, :, 0:NCMP],
                                             cmask[:, qt, 0:NCMP].unsqueeze(1).to_broadcast([P, 4, NCMP]), ALU.add))
                    link(v.tensor_reduce(mx, n3, AX.X, ALU.max))
                    v.tensor_tensor(n3, n3, mx.unsqueeze(2).to_broadcast([P, NH, NCMP]), ALU.subtract).then_inc(s_cs, 1)
                if i == 1:
                    dve.wait_ge(s_ce, qt + 1)
                    link(v.tensor_reduce(sm, n3, AX.X, ALU.add))
                    link(v.reciprocal(sm, sm))
                    if qt == 0:
                        dve.wait_ge(*end_sem("gates"))
                    link(v.tensor_tensor(sm, sm, gate, ALU.mult))
                    link(v.tensor_scalar(sm, sm, cmask[:, qt, 31:32], None, ALU.mult))
                    v.tensor_tensor(s3, s3, sm.unsqueeze(2).to_broadcast([P, NH, 32]), ALU.mult).then_inc(s_cp, 1)

            def nsa(u):
                w = u - 1
                if 0 <= w < UNITS:
                    qt, h = divmod(w, NH)
                    f = f2[:, 2 * (w % 2):2 * (w % 2) + 2]
                    dve.wait_ge(s_np, 2 * w + 2)
                    link(v.reciprocal(f, nsum[:, 2 * w:2 * w + 2]))
                    link(v.tensor_tensor(f, f, gl[:, 24 * qt + 3 * h + 1:24 * qt + 3 * h + 3], ALU.mult))
                    for b in range(2):
                        p_ = np_[:, w % 2, b, 0:P * (qt + 1)]
                        last = v.tensor_scalar(p_, p_, f[:, b:b + 1], None, ALU.mult)
                    last.then_inc(s_nw, 1)
                if u < UNITS:
                    kend = P * (u // NH + 1)
                    dve.wait_ge(s_nqk, 2 * u + 2)
                    m = nmx[:, 2 * u:2 * u + 2]
                    for b in range(2):
                        last = v.tensor_reduce(m[:, b:b + 1], bank[BANK_LOGITS + b][:, 0:kend], AX.X, ALU.max)
                    link(last)
                    v.tensor_scalar(m, m, -SCALE, None, ALU.mult).then_inc(s_nmx, 1)
                if u >= 2 and (u - 2) % NH == NH - 1:
                    split_turned(("nsa", u), "B", slice(0, 4), (u - 2) // NH, bank[BANK_O])
                    dve.sem_inc(s_nm, 1)

            def level(h, n):
                hq_, hk_, pre, suf = hset[h % 2]
                if (h, n) == (0, 0):
                    dve.wait_ge(s_hc, 32)
                    link(v.tensor_copy(halves, halves_f))
                if n > 0:
                    dve.wait_ge(s_tile, DONE[level_tile(h, n - 1)])
                m = n + 1
                if m <= LEVELS:
                    w = 2 ** n
                    q_, k_ = hqk[m % 2]
                    two = lambda ap: ap.rearrange("p (a b c) -> p a b c", b=2, c=w)
                    if m == 1:
                        link(v.memset(suf, 1.0))
                        dve.wait_ge(s_hlev, (LEVELS + 1) * h + 1)
                    v.tensor_tensor(two(q_)[:, :, 1, :], two(hq_)[:, :, 1, :], two(pre)[:, :, 1, :], ALU.mult)
                    v.tensor_tensor(k_, hk_, suf, ALU.mult).then_inc(s_hlev, 1)
                    if m < LEVELS:
                        dve.wait_ge(s_hlev, (LEVELS + 1) * h + m + 1)
                        last_of = lambda i: two(pre)[:, :, i, w - 1:w].to_broadcast([P, T // (2 * w), w])
                        link(v.tensor_tensor(two(suf)[:, :, 0, :], two(suf)[:, :, 0, :], last_of(1), ALU.mult))
                        link(v.tensor_tensor(two(pre)[:, :, 1, :], two(pre)[:, :, 1, :], last_of(0), ALU.mult))
                if n > 0:
                    read(h, n - 1)

            def read(h, n):
                g = level_tile(h, n)
                dve.wait_ge(s_tile, DONE[g])
                ps = bank[BANK[g]]
                if n == 0:
                    if h > 0:
                        dve.wait_ge(s_tile, DONE[tile_of("hout", h - 1)])
                    r = lambda ap: ap.rearrange("p (a b) -> p a b", b=P)
                    ins = v.tensor_tensor(r(hat[:, 0:512]), r(ps[:, :]), ident.unsqueeze(1).to_broadcast([P, NT, P]), ALU.mult)
                elif n <= 7:
                    w = 2 ** (n - 1)
                    up = lambda ap: ap.rearrange("p (a b c) -> p a b c", b=2, c=w)[:, :, 1, :]
                    ins = v.copy_predicated(up(hat[:, 0:512]), halves[:, 256 * (n - 1):256 * n].rearrange("p (a b) -> p a b", b=w),
                                            up(ps[:, :]))
                elif n == 8:
                    ins = v.tensor_copy(hat[:, 512:768], ps[:, 0:256])
                else:
                    ins = v.tensor_copy(hat[:, 768:1280], ps[:, :])
                link(ins)
                dve.sem_inc(s_end["V"], 1)

            def small_dt(g):
                dve.wait_ge(s_tile, DONE[g])
                ps = bank[BANK[g]]
                link(v.tensor_tensor(t64[0].rearrange("p (a b) -> p a b", b=SH), ps[:, 0:64].rearrange("p (a b) -> p a b", b=SH),
                                     V("dt_bias", 0, SH).unsqueeze(1).to_broadcast([P, NT, SH]), ALU.add))
                dve.sem_inc(s_end["V"], 1)
                link(v.tensor_scalar(t64[1], t64[0], -1.0, None, ALU.mult))
                link(v.tensor_tensor(t64[1], t64[1], t64[0], ALU.min))
                dve.sem_inc(s_dte, 1)
                dve.wait_ge(s_ex, 1)
                link(v.tensor_scalar(t64[1], t64[1], 1.0, None, ALU.add))
                dve.sem_inc(s_dte, 1)
                link(v.tensor_scalar(t64[0], t64[0], 0.0, None, ALU.max))
                dve.wait_ge(s_ex, 3)
                link(v.tensor_tensor(dt_, t64[0], t64[1], ALU.add))
                v.scalar_tensor_tensor(adt.rearrange("p (a b) -> p a b", b=SH), dt_.rearrange("p (a b) -> p a b", b=SH),
                                       -1.0, aexp.unsqueeze(1).to_broadcast([P, NT, SH]), ALU.mult, ALU.mult).then_inc(s_dt, 1)

            def ssd_decay():
                dve.wait_ge(s_aux, AUX.at["decay"] + 1)
                ps = bank[4 + AUX.slot("decay")]
                v.tensor_copy(t64[0], ps[:, 0:64])
                link(v.tensor_copy(t64[1], ps[:, 64:128]))
                v.tensor_scalar(acs_n, t64[0], -1.0, None, ALU.mult)
                link(v.tensor_tensor(t64[2], t64[1], t64[0], ALU.subtract))
                dve.sem_inc(s_auxend["V"], 1)
                dve.sem_inc(s_dte, 1)
                dve.wait_ge(s_ex, 4)
                link(v.tensor_tensor(dtend, dtend, dt_, ALU.mult))
                dve.sem_inc(s_dt, 1)

            def ssd(c, part):
                if part == 0:
                    key = ("scores", c)
                    dve.wait_ge(s_aux, AUX.at[key] + 1)
                    link(v.tensor_copy(sc, bank[4 + AUX.slot(key)][:, 0:2 * P].rearrange("p (a b) -> p a b", b=P)))
                    dve.sem_inc(s_auxend["V"], 1)
                if part < 4:
                    dve.wait_ge(s_auxend["S"], AUX.ends[AUX.at[("decay", c, part)]][1])
                    e = ee[:, part % 2, :, :]
                    v.tensor_tensor(e, e, sc[:, part // 2, :].unsqueeze(1).to_broadcast([P, 4, P]), ALU.mult).then_inc(s_attn, 1)
                if part == 4:
                    bc = lambda t, g: t[:, SH * c + 8 * g:SH * c + 8 * g + 8].unsqueeze(2).to_broadcast([P, 8, HD])
                    if c > 0:
                        for g in range(2):
                            key = ("y_off", c, g)
                            dve.wait_ge(s_aux, AUX.at[key] + 1)
                            link(v.tensor_tensor(h64(ytmp[:, g, :]), h64(bank[4 + AUX.slot(key)][:, :]), bc(ecs, g), ALU.mult))
                            dve.sem_inc(s_auxend["V"], 1)
                    dve.wait_ge(s_yd, 4 * c + 4)
                    dve.wait_ge(s_xd, 2 * c + 2)
                    for g in range(2):
                        y, x = ytmp[:, g, :], xs[:, c, 512 * g:512 * g + 512]
                        if c > 0:
                            link(v.tensor_tensor(y, y, bank[6 + g][:, :], ALU.add))
                            ins = v.tensor_tensor(x, x, y, ALU.add)
                        else:
                            ins = v.tensor_tensor(x, bank[6 + g][:, :], x, ALU.add)
                    ins.then_inc(s_y, 1)
                    if c < NT - 1:
                        for g in range(2):
                            key = ("state", c, g)
                            if c > 0:
                                link(v.tensor_tensor(h64(state[:, g, :]), h64(state[:, g, :]), bc(edec, g), ALU.mult))
                            dve.wait_ge(s_aux, AUX.at[key] + 1)
                            ps = bank[4 + AUX.slot(key)][:, :]
                            if c > 0:
                                ins = v.tensor_tensor(state[:, g, :], state[:, g, :], ps, ALU.add)
                            else:
                                ins = v.tensor_copy(state[:, g, :], ps)
                            ins.then_inc(s_st, 1)
                            dve.wait_ge(s_st, 2 * c + g + 1)
                            dve.sem_inc(s_auxend["V"], 1)

            def stick(u):
                if u < SH * NT:
                    kend = P * (u % NT + 1)
                    f0 = 516 * (u % 2)
                    if u == 0:
                        for i in range(2):
                            v.memset(sb_fail[:, 516 * i + 512:516 * i + 513], 1.0)
                        v.memset(zeros, 0.0).then_inc(s_zero, 1)
                        dve.wait_ge(s_zero, 1)
                        v.memset(zerob[:, :], 0.0).then_inc(s_zero, 1)
                    dve.wait_ge(s_sig, u + 1)
                    if u >= 3:
                        dve.wait_ge(s_tr, u - 2)
                    w = sb_w[:, u % 3, 0:kend]
                    fail = sb_fail[:, f0 + 513 - kend:f0 + 513]
                    v.tensor_tensor_scan(w[:, ::-1], fail[:, ::-1], zeros.to_broadcast([P, kend]), 1.0, ALU.mult, ALU.add)\
                        .then_inc(s_scan, 1)
                o = u - SB_LAG - 1
                if 0 <= o:
                    h, qt = divmod(o, NT)
                    rows_ = slice(HD * (h % 2), HD * (h % 2) + HD)
                    dve.wait_ge(s_pv, o + 1)
                    v.tensor_copy(qf[rows_, h // 2, P * qt:P * qt + P], bank[BANK_O][rows_, P * (o % 4):P * (o % 4) + P]).then_inc(s_o, 1)

            for n, s in enumerate(STEPS):
                if n == NT:
                    rest_of_small("dt")
                    rest_of_weights(0)
                if s[0] == "norm":
                    norm(*s[1:])
                if s[0] == "turn":
                    split_turned(s, FILLS[s[1]], slice(4 * s[3], 4 * s[3] + 4), s[2], bank[BANK[s[4]]])
                    dve.sem_inc(s_end["V"], 1)
                if s[0] == "gemm":
                    if s[2] == 2:
                        rest_of_weights(s[1] + 1)
                    for g in closed(BLOCKS[s[1]], s[2]):
                        tile(g)
                if s[0] == "pos":
                    v.tensor_tensor(lbs, V("lower", 0, 4), V("lower", 4, 4), ALU.subtract).then_inc(s_hlb, 1)
                    rest_of_small("gates")
                if s[0] == "small":
                    small_dt(s[2]) if s[1] == "dt" else small_gates()
                if s[0] == "compress":
                    compress(s[1])
                if s[0] == "cmp":
                    cmp(*s[1:])
                if s[0] == "nsa":
                    nsa(s[1])
                if s[0] == "level":
                    level(s[1], s[2])
                if s[0] == "hout":
                    read(s[1], LEVELS)
                if s[0] == "ssd_decay":
                    ssd_decay()
                if s[0] == "ssd":
                    ssd(s[1], s[2])
                if s[0] == "sb":
                    stick(s[1])
                if s[0] == "merge":
                    c = s[1]
                    dve.wait_ge(s_tround, PRODUCTS.index(s) + 1)
                    v.tensor_tensor(a_lo[:, c, :], mg[:, c, :], f32(a_hi[:, c, :]), ALU.subtract).then_inc(s_split, 1)

        @block.gpsimd
        def _(pool):
            g_ = nc.gpsimd
            h16 = lambda ap: ap.rearrange("p (a b) -> p a b", b=HD)
            for s in STEPS:
                if s[0] == "ssd" and s[2] == 0:
                    c = s[1]
                    bc = lambda t: t[:, SH * c:SH * c + SH].unsqueeze(2).to_broadcast([P, SH, HD])
                    if c == 0:
                        pool.wait_ge(s_dt, 2)
                        pool.wait_ge(s_auxend["S"], 10)
                        pool.wait_ge(s_cx, XC)
                    if c >= 2:
                        pool.wait_ge(s_yd, 4 * c - 4)
                    g_.tensor_tensor(h16(xdt[:, c % 2, :]), h16(xs[:, c, :]), bc(dt_), ALU.mult).then_inc(s_xd, 1)
                    if 1 <= c:
                        pool.wait_ge(s_st, 2 * c)
                    if c < NT - 1:
                        g_.tensor_tensor(h16(xdd), h16(xs[:, c, :]), bc(dtend), ALU.mult).then_inc(s_pc, 1)
                        pool.wait_ge(s_pc, c + 1)
                    pool.wait_ge(s_xd, 2 * c + 1)
                    g_.tensor_tensor(h16(xs[:, c, :]), h16(xs[:, c, :]), V("d_skip", 0, SH).unsqueeze(2).to_broadcast([P, SH, HD]),
                                     ALU.mult).then_inc(s_xd, 1)
                if s[0] == "sb" and s[1] < SH * NT:
                    u = s[1]
                    kend = P * (u % NT + 1)
                    pool.wait_ge(s_scan, u + 1)
                    w = sb_w[:, u % 3, 0:kend]
                    g_.tensor_tensor(w, w, sb_sig[:, u % 2, 0:kend], ALU.mult).then_inc(s_wgt, 1)


def lay_out(x, norm_pre, w_in, b_gate, conv_w, conv_b, dt_bias, a_log, d_skip, ssd_norm, w_ssd_proj, w_sb_proj,
            w_out, norm_post, norm_mix_2, w_in_2, q_norm_2, k_norm_2, cmp_pos_k_2, cmp_pos_v_2, cmp_k_w1_2, cmp_k_w2_2,
            cmp_v_w1_2, cmp_v_w2_2, hgrn_lb_logits_2, hgrn_o_norm_2, w_out_2, norm_ffn_2, w_gate_up_2, w_down_2):
    w = {"w_in": (w_in[0],), "gate_ssd": (w_in[0], w_ssd_proj[0]), "gate_sb": (w_in[0], w_sb_proj[0]), "w_out": (w_out[0],),
         "w_in_2": (w_in_2[0],), "w_out_2": (w_out_2[0],), "w_gate_up": (w_gate_up_2[0],), "w_down": (w_down_2[0],)}
    blk = np.zeros((NB, P, BLK), w_in.dtype)
    for n, b in enumerate(BLOCKS):
        src = w[b["w"]]
        parts = []
        for i, (c0, cn) in enumerate(b["spans"]):
            m = src[min(i, len(src) - 1)]
            parts.append(m[P * b["k0"]:P * (b["k0"] + b["kn"]), c0:c0 + cn].reshape(b["kn"], P, cn))
        joined = np.concatenate(parts, axis=2).transpose(1, 0, 2).reshape(P, -1)
        blk[n, :, :joined.shape[1]] = joined
    cols = lambda a: a.reshape(-1, P).T
    rows = lambda a: np.broadcast_to(a.reshape(1, -1), (P, a.size))
    vec = np.empty((P, VEC.width), x.dtype)
    conv = conv_w[0].reshape(TAPS, XC, P).transpose(2, 1, 0).reshape(P, XC * TAPS)
    for name, v in dict(b_gate=cols(b_gate[0]), conv_w=conv, conv_b=cols(conv_b[0]),
                        dt_bias=rows(dt_bias[0]), a_log=rows(a_log[0]),
                        d_skip=rows(d_skip[0]),
                        q_norm=np.tile(q_norm_2[0].reshape(HD, 1), (2, 1)), k_norm=np.tile(k_norm_2[0].T, (2, 1)),
                        lower=np.concatenate([cols(hgrn_lb_logits_2[0]), cols(hgrn_lb_logits_2[1])], axis=1)).items():
        vec[:, VEC.at(name)] = v
    cst = np.empty((P, CST.width), np.float32)
    i, j = np.arange(P)[:, None], np.arange(P)[None, :]
    cst[:, CST.at("ident")] = i == j
    cst[:, CST.at("tri")] = i <= j
    cst[:, CST.at("ones")] = 1.0
    bf = mybir.dt.np(BF16)
    cstb = np.empty((P, CSTB.width), bf)
    cstb[:, CSTB.at("ident")] = i == j
    cstb[:, CSTB.at("strict")] = np.where(j < i, 0.0, NEG)
    cstb[:, CSTB.at("after")] = np.where(i <= j, 0.0, NEG)
    small = lambda m, c0, n: m[:, c0:c0 + n].reshape(NK, P, n).transpose(1, 0, 2).reshape(P, NK * n)
    w1 = lambda m: m[0].reshape(CL // 2, P, P).transpose(1, 0, 2).reshape(P, CL // 2 * P)
    cst2 = np.zeros((P, CST2.width), x.dtype)
    cst2[:, CST2.at("w2")] = np.concatenate([cmp_k_w2_2[0], cmp_v_w2_2[0]], axis=1)
    cst2[:, CST2.at("pos")] = np.concatenate([m[0].reshape(CL // 2, P).T for m in (cmp_pos_k_2, cmp_pos_v_2)], axis=1)
    cst2[:, CST2.at("one")] = 1.0
    cst2[:, CST2.at("heads")] = i // 32 == np.arange(4)[None, :]
    upto = np.where(j <= i, 0.0, NEG).astype(bf)
    token = np.arange(T).reshape(NT, P).T[:, :, None]
    ends = (CS * np.arange(32) + CL - 1)[None, None, :]
    cmask = np.where(ends <= token, 0.0, NEG).astype(np.float32)
    cmask[:, :, 31] = (token >= CL - 1)[:, :, 0]
    halves = np.zeros((P, 7, 256), np.float32)
    t = np.arange(T)
    for n in range(7):
        up = t[(t >> n) & 1 == 1]
        s = np.arange(P)[:, None]
        halves[:, n, :] = (s >> (n + 1) == (up % P)[None, :] >> (n + 1)) & ((s >> n) & 1 == 0)
    return {"x": x[0], "wblk": blk, "vec": vec, "cst": cst, "cstb": cstb, "w_dt": small(w_in[0], DT0, SH),
            "w_gates": small(w_in_2[0], GL0, 24), "norm_post": rows(norm_post[0]), "w1k": w1(cmp_k_w1_2),
            "w1v": w1(cmp_v_w1_2), "cst2": cst2, "upto": upto, "cmask": cmask.reshape(P, P),
            "halves": halves.reshape(P, 7 * 256), "onorm": rows(hgrn_o_norm_2[0]), "norm_pre": rows(norm_pre[0]),
            "ssd_norm": rows(ssd_norm[0]), "norm_mix": rows(norm_mix_2[0]), "norm_ffn": rows(norm_ffn_2[0])}


def kernel(**inputs):
    import concourse.bacc as bacc
    from concourse.bass_utils import run_bass_kernel_spmd

    nc = bacc.Bacc("TRN2", target_bir_lowering=False, num_devices=1)
    arrays = {name: np.ascontiguousarray(a) for name, a in lay_out(**inputs).items()}
    dram = {name: nc.dram_tensor("in_" + name, a.shape, mybir.dt.from_np(a.dtype), kind="ExternalInput").ap()
            for name, a in arrays.items()}
    out = nc.dram_tensor("out", (T, D), F32, kind="ExternalOutput").ap()
    spill = nc.dram_tensor("spill", (T, D), F32).ap()
    emit(nc, dram, spill, out)
    r = run_bass_kernel_spmd(nc, [{"in_" + name: a for name, a in arrays.items()}], core_ids=[0])
    return r.results[0]["out"].reshape(1, T, D)
```

```python
from contextlib import ExitStack

import numpy as np

import concourse.bass as bass
from concourse import mybir

ALU = mybir.AluOpType
ACT = mybir.ActivationFunctionType
AX = mybir.AxisListType
F32 = mybir.dt.float32
F32R = mybir.dt.float32r
BF16 = mybir.dt.bfloat16
U8 = mybir.dt.uint8

P = 128
T = 512
D = 1024
NT = T // P
NK = D // P
EPS = 1e-6
NEG = -1e30
HD = 64
SCALE = HD ** -0.5

Z0, XBC0 = 0, 1024
DT0 = XBC0 + 1536
Q0 = DT0 + 16
K0, V0, ZS0, G0 = Q0 + 1024, Q0 + 2048, Q0 + 3072, Q0 + 4096
SH = 16
XC = 12
TAPS = 4
KC0 = 512
KS0, GL0, HQ0, HF0, HI0, HG0 = 768, 1280, 1304, 1816, 2328, 2840
NH = 8
NG = 2
NCMP = 31
CL, CS = 32, 16
HH = 4
DFF = 2816
FFP = ((0, 8), (8, 16), (16, 22))
LEVELS = 9
SLICES = 8
SB_LAG = 2
NSA_LAG = 2
UNITS = NH * NT
BLK = 2048



def weave(*streams, weights=None):
    ends = [np.arange(1, len(s) + 1) for s in streams]
    if weights:
        ends[0] = np.cumsum(weights)
    keyed = [((ends[n][i] - 0.5) / ends[n][-1], n, i, x) for n, s in enumerate(streams) for i, x in enumerate(s)]
    return [x for *_, x in sorted(keyed, key=lambda k: k[:3])]


def plan():
    blocks, tiles, steps = [], [], []

    def tile(kind, i):
        tiles.append((kind, i))
        return len(tiles) - 1

    def feature(w, spans, kinds, srcs):
        gs = [tile(k, i) for k, i in kinds]
        n = len(blocks)
        parts = [(j, k) for j in range(2) for k in range(NK)]
        blocks.append(dict(w=w, form="feature", spans=spans, k0=0, kn=NK, tiles=gs, srcs=srcs, parts=parts, kb=0,
                           total=NK, closing=True))
        return [("gemm", n, s) for s in range(SLICES)]

    def token(w, col, kind, half, src, k0=0, kn=NK):
        gs = [tile(kind, (t, half)) for t in range(NT)]
        a = kn // 2
        out = []
        for j in range(2):
            n = len(blocks)
            parts = [(t, k) for t in range(NT) for k in range(a)]
            blocks.append(dict(w=w, form="token", spans=[(col, 512)], k0=k0 + j * a, kn=a, tiles=gs, srcs=[src] * 4,
                               parts=parts, kb=j * a, total=kn, closing=j == 1))
            out += [("gemm", n, s) for s in range(SLICES)]
        return out

    def turn(name, t, half):
        return ("turn", name, t, half, tile("turn", (name, t, half)))

    def normed(names, halves=(0, 1), gap=2):
        done = []
        stages = [(what, name) for name in names for what in ("norm", "apply")] + ([("turn", names[-1])] if halves else [])
        for row in range(gap * (NT - 1) + len(stages)):
            done.append([])
            for t in range(NT):
                if 0 <= row - gap * t < len(stages):
                    what, name = stages[row - gap * t]
                    done[-1] += [turn(name, t, h) for h in halves] if what == "turn" else [(what, name, t)]
        return done

    def last_block(steps_, rows_):
        out = [steps_[0]]
        for i, row in enumerate(rows_):
            out += steps_[i + 1:i + 2] + row
        return out + steps_[len(rows_) + 1:]

    for row in normed(["x"], gap=1):
        steps += row[::-1] if row[-1][0] != "turn" else row
    steps.append(("small", "dt", tile("dt_t", 0)))
    for j in range(XC // 2):
        block_ = feature("w_in", [(XBC0 + 256 * j, 256)], [("xbc", 2 * j), ("xbc", 2 * j + 1)], "AA")
        if j == 1:
            block_ = weave(block_, [("dt", i) for i in range(3)])
        steps += block_
        if j == 0:
            steps.append(("smallturn", "dt", tile("dt", 0)))
        if j == 2:
            steps.append(("ssd_decay",))
        if j >= 1:
            steps.extend([("xturn", 2 * j - 2), ("xturn", 2 * j - 1)])
    kq = []
    for name, c0 in (("k", K0), ("q", Q0)):
        for j in range(4):
            kq += feature("w_in", [(c0 + 256 * j, 256)], [(name, 2 * j), (name, 2 * j + 1)], "AA")
    steps += weave([("ssd", c, part) for c in range(NT) for part in range(5)], kq)
    for half in range(2):
        steps += token("w_in", Z0 + 512 * half, "z", half, "A")
    vs = token("w_in", V0, "v", 0, "A") + token("w_in", V0 + 512, "v", 1, "A")
    ys = normed(["y"])
    steps += weave(sum(ys, []), vs[:24]) + vs[24:]
    gs = []
    for c in range(NK):
        gs += feature("gate_ssd", [(G0 + P * c, P), (P * c, P)], [("gate", c), ("y_ssd", c)], "AB")
    steps += weave([("sb", u) for u in range(SH * NT)], gs)
    steps += [("sb", SH * NT + i) for i in range(SB_LAG + 1)]
    for j in range(4):
        steps += feature("w_in", [(ZS0 + 256 * j, 256)], [("z_sb", 2 * j), ("z_sb", 2 * j + 1)], "AA")
    for c in range(NK):
        steps += feature("gate_sb", [(G0 + D + P * c, P), (P * c, P)], [("gate2", c), ("y_sb", c)], "AB")
    for c in range(NK):
        steps.append(("merge", c))

    out1 = token("w_out", 0, "out1", 0, "A") + token("w_out", 512, "out1", 1, "A")
    kv = token("w_in_2", KS0, "kv", 0, "A")
    rows_ = normed(["out1", "mix"])
    steps += out1[:-8] + last_block(out1[-8:], rows_[:7])
    steps += kv[:2] + [("positions",)] + rows_[7] + kv[2:4] + rows_[8] + kv[4:5] + rows_[9] + kv[5:6] + rows_[10] + kv[6:]

    steps += feature("w_in_2", [(KC0, 256)], [("kcv", 0), ("kcv", 1)], "AA")
    steps.append(("pos",))
    qn = token("w_in_2", 0, "qn", 0, "A")
    steps += qn[:8] + last_block(qn[8:], normed(["qk"], ()))
    steps.append(("small", "gates", tile("gates_t", 0)))
    head = lambda h: feature("w_in_2", [(HQ0 + P * h, P), (HF0 + P * h, P)], [("hq", h), ("hf", h)], "AA")
    steps += weave([("compress", i) for i in range(4)] + [("qkturn", i, tile("turn_qk", i)) for i in range(6)], head(0))
    steps.append(("smallturn", "gates", tile("gates", 0)))
    steps += weave([("cmp", qt, i) for qt in range(NT) for i in range(3)], token("w_in_2", HI0, "hi", 0, "A"))
    hs = []
    for h in range(HH):
        levels = [("level", h, n, tile("level", (h, n))) for n in range(LEVELS + 1)] + [("hout", h, tile("hout", h))]
        hs += weave(levels, head(h + 1)) if h + 1 < HH else levels
    units = range(UNITS + NSA_LAG + 1)
    steps += weave([("nsa", u) for u in units], hs, weights=[2 + min(u, UNITS - 1) // NH for u in units])
    hg = token("w_in_2", HG0, "hg", 0, "A")
    steps += weave(hg[:8], sum(normed(["hgrn"], (), 1), []))
    out2 = token("w_out_2", 0, "out2", 0, "B") + token("w_out_2", 512, "out2", 1, "B")
    steps += hg[8:-1] + [turn("hgrn", 0, 1)] + hg[-1:] + out2[:1] + [turn("hgrn", 1, 1)] + out2[1:3]
    steps += [turn("hgrn", 2, 1)] + out2[3:5] + [turn("hgrn", 3, 1)] + out2[5:-8] + last_block(out2[-8:], normed(["ffn"]))
    for a, e in FFP:
        for c in range(a, e):
            steps += feature("w_gate_up", [(P * c, P), (DFF + P * c, P)], [("ff_gate", (c, c - a)), ("ff_up", (c, c - a))], "AA")
        for half in range(2):
            steps += token("w_down", 512 * half, "down", (a, half), "B", k0=a, kn=e - a)
    return blocks, tiles, steps


def sliced(b, s):
    n = len(b["parts"])
    return b["parts"][s * n // SLICES:(s + 1) * n // SLICES]


def opened(b, s):
    return [b["tiles"][j] for j, k in sliced(b, s) if k == 0 and b["kb"] == 0]


def closed(b, s):
    return [b["tiles"][j] for j, k in sliced(b, s) if k == b["kn"] - 1 and b["closing"]]


BLOCKS, TILES, STEPS = plan()
NB = len(BLOCKS)

READER = {"dt_t": "S", "gates_t": "S", "xbc": "S", "dt": "V", "z": "V", "k": "S", "q": "S", "v": "S", "gate": "S", "y_ssd": "V",
          "z_sb": "V", "gate2": "S", "y_sb": "V", "out1": "S", "kv": "S", "qn": "S", "kcv": "S", "gates": "S",
          "turn_qk": "S", "hi": "S", "hg": "V", "hq": "V", "hf": "V", "level": "V", "hout": "S", "out2": "V",
          "ff_gate": "V", "ff_up": "V", "down": "V"}


class Ring:

    def __init__(self, size):
        self.size, self.ends, self.count, self.at = size, [], {"V": 0, "S": 0}, {}

    def use(self, key, reader):
        self.count[reader] += 1
        self.at[key] = len(self.ends)
        self.ends.append((reader, self.count[reader]))

    def slot(self, key):
        return self.at[key] % self.size

    def before(self, key):
        i = self.at[key] - self.size
        return self.ends[i] if i >= 0 else None


def plan_tiles():
    begun, done, ended, end = [], [], [], {}
    for s in STEPS:
        if s[0] == "gemm":
            begun += opened(BLOCKS[s[1]], s[2])
            done += closed(BLOCKS[s[1]], s[2])
            ended += closed(BLOCKS[s[1]], s[2])
        elif s[0] in ("turn", "small", "smallturn", "qkturn", "level", "hout"):
            begun.append(s[-1])
            done.append(s[-1])
            if s[0] == "level":
                if s[2] > 0:
                    ended.append(level_tile(s[1], s[2] - 1))
            elif s[0] == "hout":
                ended += [level_tile(s[1], LEVELS), s[-1]]
            elif s[0] == "turn":
                end[s[-1]] = ("split", s)
            else:
                ended.append(s[-1])
    count = {"V": 0, "S": 0}
    for g in ended:
        who = READER[TILES[g][0]]
        count[who] += 1
        end[g] = (who, count[who])
    bank, before = {}, {}
    groups = {"turn": (4, 6, 7), "dt": (7,), "level": (2, 3), "hout": (2, 3), "turn_qk": (2, 3), "hq": (0, 1), "hf": (0, 1)}
    uses, last = {}, {}
    for g in begun:
        banks = groups.get(TILES[g][0], (0, 1, 2, 3))
        i = uses[banks] = uses.get(banks, -1) + 1
        bank[g] = banks[i % len(banks)]
        before[g] = last.get(bank[g])
        last[bank[g]] = g
    return bank, before, {g: i + 1 for i, g in enumerate(done)}, end


def level_tile(h, n):
    return TILES.index(("level", (h, n)))


BANK, BEFORE, DONE, END = plan_tiles()


def plan_aux():
    ring = Ring(2)
    for s in STEPS:
        if s[0] == "xturn":
            ring.use(s, "S")
        if s[0] == "ssd_decay":
            ring.use("decay", "V")
        if s[0] == "ssd":
            _, c, part = s
            if part == 0:
                ring.use(("scores", c), "V")
            if part < 4:
                ring.use(("decay", c, part), "S")
            if part == 4:
                for g in range(2):
                    if c > 0:
                        ring.use(("y_off", c, g), "V")
                for g in range(2):
                    if c < NT - 1:
                        ring.use(("state", c, g), "V")
    return ring


AUX = plan_aux()
SIGMOID = {"z", "gate", "z_sb", "gate2", "hg", "hq", "hf", "ff_gate"}
CONSUMER = {"z": 0, "gate": 1, "z_sb": 0, "gate2": 1, "hg": 0, "hq": 0, "hf": 0, "ff_gate": 1}
SIG_TILES = sorted((g for g, (kind, _) in enumerate(TILES) if kind in SIGMOID), key=DONE.get)
FILLS = {"x": "A", "y": "B", "mix": "A", "hgrn": "B", "ffn": "A"}
ROWS = {"x": "norm_pre", "y": "ssd_norm", "mix": "norm_mix", "ffn": "norm_ffn"}
SQUARED = ("x", "y", "mix", "ffn")
SPLIT_TILES = {"z_sb": "B", "ff_up": "B"}
NORMS = [s[1:] for s in STEPS if s[0] == "norm"]
APPLIED = [s[1:] for s in STEPS if s[0] == "apply"]
for order in (NORMS, APPLIED):
    order.insert(max(i for i, x in enumerate(order) if x[0] == "qk") + 1, ("kc", 0))


def plan_splits():
    order, need, last = [], {}, {}

    def done(key, dst, chunks, tokens=range(NT)):
        order.append(key)
        for k in chunks:
            for t in tokens:
                last[dst, t, k] = len(order)

    for s in STEPS:
        if s[0] == "turn":
            done(s, FILLS[s[1]], range(4 * s[3], 4 * s[3] + 4), [s[2]])
        if s[0] == "merge":
            done(s, "A", [s[1]])
        if s[0] == "nsa" and s[1] > NSA_LAG and (s[1] - NSA_LAG - 1) % NH == NH - 1:
            done(s, "B", range(4), [(s[1] - NSA_LAG - 1) // NH])
        if s[0] == "small":
            need[s[:2]] = max(v for (x, _, _), v in last.items() if x == "A")
        if s[0] == "gemm":
            b = BLOCKS[s[1]]
            for j, k in sliced(b, s[2]):
                ts = [j] if b["form"] == "token" else range(NT)
                need[s[1], j, k] = max(last[b["srcs"][j], t, b["kb"] + k] for t in ts)
            for g in closed(b, s[2]):
                kind, i = TILES[g]
                if kind in SPLIT_TILES:
                    done(("tile", g), SPLIT_TILES[kind], [i if kind == "z_sb" else i[1]])
    return order, need


SPLITS, SPLIT_NEED = plan_splits()
PRODUCTS = [s for s in SPLITS if s[0] in ("tile", "merge")]


class Columns:

    def __init__(self, spans):
        self.spans, self.width = {}, 0
        for name, n in spans:
            self.spans[name] = slice(self.width, self.width + n)
            self.width += n

    def at(self, name):
        return self.spans[name]


CST = Columns([("ident", P), ("tri", P), ("ones", P)])
CSTB = Columns([("ident", P), ("strict", P), ("after", P)])
VEC = Columns([("b_gate", 16), ("conv_w", 48), ("conv_b", 12), ("dt_bias", 16), ("a_log", 16), ("d_skip", 16),
               ("q_norm", 1), ("k_norm", 3), ("lower", 8)])
CST2 = Columns([("w2", 2 * HD), ("pos", CL), ("heads", 4), ("one", 64)])
CMASK0 = 572
ARENA = 22528
STAT = 700
BANK_LOGITS, BANK_WT, BANK_O = 4, 6, 7


LATE = min(n for n, b in enumerate(BLOCKS) if TILES[b["tiles"][0]][0] == "z_sb") + 1
LAST_DOWN = len(TILES) - 8
MERGE_AFTER = max(n for n, b in enumerate(BLOCKS) if b["w"] == "gate_sb")
TURNS = [s for s in SPLITS if s[0] in ("turn", "nsa")]


def block_of(kind):
    return min(n for n, b in enumerate(BLOCKS) if TILES[b["tiles"][0]][0] == kind)


def end_of(kind, i=None):
    ends = [END[g] for g, (k, j) in enumerate(TILES) if k == kind and i in (None, j)]
    return max(ends)


T_READY = [sum(s[0] == "tile" for s in PRODUCTS[:p + 1]) for p in range(len(PRODUCTS))]


def emit(nc, dram, spill, out):
    ctx = ExitStack()
    with ctx:
        def sb(name, shape, dt=F32):
            return ctx.enter_context(nc.sbuf_tensor(name, shape, dt))

        def sem(name):
            return ctx.enter_context(nc.semaphore(name))

        wraw = [sb(f"wraw{i}", [P, BLK]) for i in range(2)]
        whi = [sb(f"whi{i}", [P, BLK], F32R) for i in range(2)]
        wlo = [sb(f"wlo{i}", [P, BLK], F32R) for i in range(2)]
        swraw = sb("swraw", [P, NK * 24])
        swhi = sb("swhi", [P, NK * 24], F32R)
        swlo = sb("swlo", [P, NK * 24], F32R)
        a_hi, a_lo = sb("a_hi", [P, NK, T], F32R), sb("a_lo", [P, NK, T], F32R)
        b_hi, b_lo = sb("b_hi", [P, NK, T], F32R), sb("b_lo", [P, NK, T], F32R)
        ACTS = {"A": (a_hi, a_lo), "B": (b_hi, b_lo)}
        cst = sb("cst", [P, CST.width])
        cstb = sb("cstb", [P, CSTB.width], BF16)
        vec = sb("vec", [P, VEC.width])
        zerob = sb("zerob", [P, 2], BF16)
        stat = sb("stat", [P, STAT])
        arena = sb("arena", [P, ARENA])

        def mem(kb, shape):
            n = int(np.prod(shape))
            v = arena[:, int(kb * 256):int(kb * 256) + n]
            assert kb * 256 + n <= ARENA, (kb, shape)
            if len(shape) == 2:
                v = v.rearrange("p (a b) -> p a b", b=shape[1])
            if len(shape) == 3:
                v = v.rearrange("p (a b c) -> p a b c", b=shape[1], c=shape[2])
            return v

        used = [0]

        def small(n):
            used[0] += n
            assert used[0] <= STAT
            return stat[:, used[0] - n:used[0]]

        bank = [ctx.enter_context(nc.psum_tensor(f"bank{i}", [P, 512], F32)) for i in range(8)]

        ident = cst[:, CST.at("ident")]
        tri = cst[:, CST.at("tri")]
        ones = cst[:, CST.at("ones")]
        w2 = cst[:, P:P + 2 * HD].rearrange("p (a b) -> p a b", b=HD)
        pos = cst[:, P + 2 * HD:P + 2 * HD + CL].rearrange("p (a b) -> p a b", b=CL // 2)
        heads4 = cst[:, P + 2 * HD + CL:P + 2 * HD + CL + 4]
        one = cst[:, P + 2 * HD + CL + 4:P + 2 * HD + CL + 68]
        identb = cstb[:, CSTB.at("ident")]
        strict = cstb[:, CSTB.at("strict")]
        after = cstb[:, CSTB.at("after")]

        def V(name, i=0, n=1):
            a = VEC.at(name).start
            return vec[:, a + i:a + i + n]

        xt = mem(72, [NT, D])
        xs = mem(16, [NT, D])
        bct = mem(32, [4, T])
        btok = mem(40, [NT, 256])
        state = mem(44, [2, 512])
        xdt = mem(48, [2, D])
        xdd = mem(56, [D])
        sc = mem(60, [2, P])
        ee = mem(61, [2, 4, P])
        ytmp = mem(65, [2, 512])
        kf = mem(72, [NK, T])
        qf = mem(0, [NK, T])
        vt = mem(32, [NT, D])
        junks = {"x": mem(0, [NT, D]), "y": mem(52, [NT, D])}
        rows = {"x": mem(64, [D]), "y": mem(48, [D]), "mix": mem(80, [D]), "ffn": mem(0, [D])}
        craw = mem(0, [2, T])
        cacc = mem(48, [2, T])
        csig = mem(52, [2, T])
        cx = mem(56, [2, T])
        sgt = mem(68, [2, T])
        adt_hi, adt_lo = b_hi[:, 4, 0:64], b_lo[:, 4, 0:64]
        ones_r = b_hi[:, 5, 0:P]
        sb_sig = mem(48, [2, T])
        sb_fail = mem(52, [2 * 516])
        sb_w = mem(57, [3, T])
        sb_wT = mem(63, [2, T])
        zeros = mem(67.5, [1])
        small_t = {"dt": mem(12, [T]), "gates": mem(10, [T])}
        tt = mem(48, [2, T])
        mg = mem(16, [NK, T])
        oraw = mem(0, [NT, D])
        xres = mem(32, [NT, D])
        npost = mem(52, [D])

        xn = mem(16, [NT, D])
        x2 = mem(72, [NT, D])
        vst = mem(0, [NT, 256])
        kst = mem(4, [NT, 256])
        qt_ = mem(8, [NT, 512])
        kcf = mem(48, [2, T])
        kc2 = mem(24, [2, 2, T])
        w1 = [mem(56, [CL // 2, P]), mem(72, [CL // 2, P])]
        qn_ = mem(32, [NT, 4, P])
        qT = mem(40, [4, T])
        kT = mem(64, [2, T])
        sq_ = mem(52, [512])
        cs_ = [mem(8 + i, [NH, 32]) for i in range(2)]
        cpT = mem(10, [NT, 2, P])
        vcd = mem(14, [2, 4, HD])
        hid = mem(52, [2, 2, 32])
        hid4 = mem(52.5, [2, 4, 32])
        kcn = mem(53.5, [P])
        kcT = mem(54, [32])
        nsq = mem(54.25, [P])
        posr = mem(55, [2 * P])
        np_ = [mem(kb, [2, T]) for kb in (24, 28, 60)]
        npT = mem(56, [2, T])
        mixt = mem(32, [NT, 512])
        hit = mem(16, [NT, 512])
        hgt = mem(24, [NT, 512])
        hset = [[mem(kb, [T]) for kb in kbs] for kbs in ((72, 74, 76, 78), (4, 6, 8, 78))]
        hqk = [[mem(kb, [T]) for kb in kbs] for kbs in ((80, 86), (84, 82))]
        hat = mem(48, [1280])
        halves = mem(53, [6 * 64]).bitcast(U8)
        halves_f = mem(80, [6 * 256])
        hsq = mem(4, [512])

        sso = small(8)
        nss1 = {"out1": small(4), "mix": small(4), "ffn": small(4)}
        first = used[0]
        dt_ = small(64)
        adt = small(64)
        acs_n = small(64)
        ecs = small(64)
        edec = small(64)
        dtend = small(64)
        t64 = [small(64) for _ in range(3)]
        aexp = small(16)
        nss = {"x": small(4), "y": small(8)}
        nss.update(nss1)
        used[0] = first
        nmx, nsum = small(64), small(64)
        onorm = small(P)
        gl = small(96)
        nss.update({"qk": small(48), "kc": small(2), "hgrn": small(16)})
        cmx, csum = small(16), small(16)
        lbs, lbn = small(4), small(4)
        f2 = small(4)
        cmask = stat[:, CMASK0:CMASK0 + P].rearrange("p (a b) -> p a b", b=32)
        assert used[0] <= CMASK0

        s_w = [sem(f"s_w{i}") for i in range(2)]
        s_sw = sem("s_small_weights")
        s_cst, s_ident = sem("s_constants"), sem("s_identity")
        s_tri, s_hg = sem("s_decays_spread"), sem("s_hgrn_gated")
        s_x = [sem(f"s_x{t}") for t in range(NT)]
        s_row = {name: sem("s_row_" + name) for name in ROWS}
        s_yz, s_spill, s_back = sem("s_gated"), sem("s_residual_stored"), sem("s_residual_back")
        s_kc2, s_pos, s_posr = sem("s_kc_spread"), sem("s_positions_hidden"), sem("s_positions_read")
        s_hi, s_lo = sem("s_weights_hi"), sem("s_weights_lo")
        s_shi, s_slo = sem("s_small_hi"), sem("s_small_lo")
        s_blk, s_tile = sem("s_block_used"), sem("s_tile_summed")
        s_end = {"V": sem("s_tile_read_v"), "S": sem("s_tile_read_s")}
        s_split = sem("s_chunk_split")
        s_round = sem("s_chunk_rounded")
        s_sg = sem("s_sigmoid")
        s_conv, s_csig, s_cx = sem("s_conv"), sem("s_conv_sigmoid"), sem("s_conv_silu")
        s_aux = sem("s_aux_summed")
        s_auxend = {"V": sem("s_aux_read_v"), "S": sem("s_aux_read_s")}
        s_ss, s_rec, s_rt, s_norm = sem("s_squares"), sem("s_mean"), sem("s_root"), sem("s_normed")
        s_dt, s_dte, s_ex = sem("s_dt"), sem("s_dt_exp"), sem("s_decays")
        s_xd = sem("s_x_dt")
        s_attn, s_yd, s_y, s_st = sem("s_ssd_attn"), sem("s_y_diag"), sem("s_y_read"), sem("s_state")
        s_qk, s_sig, s_scan, s_wgt = sem("s_logits"), sem("s_sb_sigmoids"), sem("s_sb_products"), sem("s_sb_weights")
        s_tr, s_wT, s_pv, s_o = sem("s_sb_turned"), sem("s_sb_wT"), sem("s_sb_summed"), sem("s_sb_out")
        s_t, s_tround, s_mg = sem("s_product"), sem("s_product_rounded"), sem("s_merged")
        s_res, s_zero = sem("s_residual"), sem("s_zero")
        s_vc, s_ac, s_pc = sem("s_vector_chain"), sem("s_scalar_chain"), sem("s_pool_chain")
        s_out = sem("s_stored")
        s_hid4, s_hidz = sem("s_hidden_repeated"), sem("s_hidden_zero")
        s_late, s_hc = sem("s_late_constants"), sem("s_hgrn_constants")
        s_hid, s_gelu, s_kc, s_kct, s_kcr, s_vcd = (sem("s_hidden"), sem("s_gelu"), sem("s_kc"), sem("s_kc_turned"),
                                                    sem("s_kc_read"), sem("s_vc_ready"))
        s_cqk, s_cs, s_ce, s_cp, s_ctr, s_cpt = (
            sem("s_cmp_logits"), sem("s_cmp_shifted"), sem("s_cmp_exp"), sem("s_cmp_weights"), sem("s_cmp_turned"),
            sem("s_cmp_wT"))
        s_nqk, s_nmx, s_np, s_nw, s_ntr, s_npt, s_npv, s_nm = (
            sem("s_nsa_logits"), sem("s_nsa_max"), sem("s_nsa_exp"), sem("s_nsa_weights"), sem("s_nsa_turned"),
            sem("s_nsa_wT"), sem("s_nsa_summed"), sem("s_nsa_out"))
        s_nf = sem("s_nsa_factors")
        s_hlb, s_hlev = sem("s_lower"), sem("s_hgrn_operands")

        f32 = lambda ap: ap.bitcast(F32)

        def nsa_logits(u, b):
            kend = P * (u // NH + 1)
            if kend <= 256:
                return bank[BANK_LOGITS + u % 2][:, kend * b:kend * b + kend]
            return bank[BANK_LOGITS + b][:, 0:kend]

        def width(n):
            return BLOCKS[n]["kn"] * sum(c for _, c in BLOCKS[n]["spans"])

        def used_by_pe(n):
            if BLOCKS[n]["closing"]:
                return s_tile, DONE[BLOCKS[n]["tiles"][-1]]
            return s_blk, sum(not b["closing"] for b in BLOCKS[:n + 1])

        def ended(g):
            who, n = END[g]
            if who == "split":
                return s_split, SPLITS.index(n) + 1
            return s_end[who], n

        def sigmoid_ready(g):
            if READER[TILES[g][0]] == "S":
                return ended(g)
            return s_sg, sum(READER[TILES[x][0]] == "V" for x in SIG_TILES[:SIG_TILES.index(g) + 1])

        def end_sem(kind):
            who, n = end_of(kind)
            return s_end[who], n

        def norm_no(name, t):
            return APPLIED.index((name, t)) + 1

        def norm_cols(name, t):
            n = {"y": 2, "qk": 12, "kc": 2, "hgrn": 4}.get(name, 1)
            return n * t, n

        def tile_of(kind, i):
            return TILES.index((kind, i))

        block = ctx.enter_context(nc.Block())

        @block.sync
        def _(sp):
            by_token = lambda ap: ap.rearrange("(a p) d -> p a d", p=P)
            for t in range(NT):
                if t == 2:
                    sp.dma_start(cst[:, :], dram["cst"]).then_inc(s_ident, 16)
                    sp.dma_start(rows["x"], dram["norm_pre"]).then_inc(s_row["x"], 16)
                sp.dma_start(xt[:, t, :], by_token(dram["x"])[:, t, :]).then_inc(s_x[t], 16)
            sp.dma_start(swraw[:, 0:NK * SH], dram["w_dt"]).then_inc(s_sw, 16)
            for n in range(NB):
                if n >= 2:
                    sp.wait_ge(s_lo, n - 1)
                cols = width(n)
                sp.dma_start(wraw[n % 2][:, 0:cols], dram["wblk"][n][:, 0:cols]).then_inc(s_w[n % 2], 16)
                if n == 1:
                    sp.dma_start(vec[:, :], dram["vec"]).then_inc(s_cst, 16)
                    sp.dma_start(cstb[:, :], dram["cstb"]).then_inc(s_cst, 16)
                if n == block_of("z") + 3:
                    sp.wait_ge(s_yd, 4 * NT)
                    sp.wait_ge(s_xd, 2 * NT)
                    sp.dma_start(rows["y"], dram["ssd_norm"]).then_inc(s_row["y"], 16)
                if n == LATE:
                    sp.wait_ge(s_pv, SH * NT)
                    sp.dma_start(xres, by_token(dram["x"])).then_inc(s_res, 16)
                    sp.dma_start(npost, dram["norm_post"]).then_inc(s_res, 16)
                if n == LATE + 2:
                    sp.dma_start(rows["mix"], dram["norm_mix"]).then_inc(s_row["mix"], 16)
                    sp.dma_start(w1[0].rearrange("p a b -> p (a b)"), dram["w1k"]).then_inc(s_late, 16)
                if n == LATE + 4:
                    sp.dma_start(w1[1].rearrange("p a b -> p (a b)"), dram["w1v"]).then_inc(s_late, 16)
                    sp.dma_start(cst[:, P:P + CST2.width], dram["cst2"]).then_inc(s_late, 16)
                    sp.dma_start(cstb[:, CSTB.at("after")], dram["upto"]).then_inc(s_late, 16)
                    sp.dma_start(stat[:, CMASK0:CMASK0 + P], dram["cmask"]).then_inc(s_late, 16)
                    sp.dma_start(swraw[:, :], dram["w_gates"]).then_inc(s_sw, 16)
                if n == block_of("kcv") + 1:
                    for t in range(NT):
                        sp.wait_ge(s_norm, norm_no("out1", t))
                        sp.dma_start(by_token(spill)[:, t, :], xres[:, t, :]).then_inc(s_spill, 16)
                    sp.wait_ge(s_norm, norm_no("mix", NT - 1))
                    sp.dma_start(halves_f, dram["halves"]).then_inc(s_hc, 16)
                    sp.dma_start(onorm, dram["onorm"]).then_inc(s_hc, 16)
                if n == block_of("out2"):
                    sp.wait_ge(*ended(tile_of("hout", HH - 1)))
                    sp.wait_ge(s_split, SPLITS.index(("nsa", UNITS + NSA_LAG)) + 1)
                    sp.wait_ge(s_spill, 16 * NT)
                    sp.dma_start(x2, by_token(spill)).then_inc(s_back, 16)
                    sp.dma_start(rows["ffn"], dram["norm_ffn"]).then_inc(s_row["ffn"], 16)
            for half in range(2):
                for t in range(NT):
                    sp.wait_ge(*ended(LAST_DOWN + 4 * half + t))
                    cols = slice(512 * half, 512 * half + 512)
                    sp.dma_start(by_token(out)[:, t, cols], x2[:, t, cols]).then_inc(s_out, 16)
            sp.wait_ge(s_out, 16 * 2 * NT)

        @block.tensor
        def _(pe):
            def mm(o, lhsT, rhs, start, stop, **kw):
                return nc.tensor.matmul(o, lhsT, rhs, start=start, stop=stop, **kw)

            def free_bank(g):
                if BEFORE[g] is not None:
                    pe.wait_ge(*ended(BEFORE[g]))

            def free_aux(key):
                if AUX.before(key):
                    who, n = AUX.before(key)
                    pe.wait_ge(s_auxend[who], n)
                return bank[4 + AUX.slot(key)]

            split = [0]

            def need_split(n):
                if n > split[0]:
                    pe.wait_ge(s_split, n)
                    split[0] = n

            def gemm(n, s):
                b, slot = BLOCKS[n], n % 2
                if s == 0:
                    pe.wait_ge(s_hi, n + 1)
                    pe.wait_ge(s_lo, n + 1)
                for j, k in sliced(b, s):
                    g = b["tiles"][j]
                    xh, xl = ACTS[b["srcs"][j]]
                    ps = bank[BANK[g]]
                    if g in opened(b, s) and k == 0:
                        free_bank(g)
                    need_split(SPLIT_NEED[n, j, k])
                    kk = b["kb"] + k
                    if b["form"] == "feature":
                        w = slice(256 * k + P * j, 256 * k + P * j + P)
                        pairs = [(whi[slot][:, w], xh[:, k, :]), (whi[slot][:, w], xl[:, k, :]),
                                 (wlo[slot][:, w], xh[:, k, :])]
                    else:
                        w, ts = slice(512 * k, 512 * k + 512), slice(P * j, P * j + P)
                        pairs = [(xh[:, kk, ts], whi[slot][:, w]), (xh[:, kk, ts], wlo[slot][:, w]),
                                 (xl[:, kk, ts], whi[slot][:, w])]
                    for i, (l, r) in enumerate(pairs):
                        last = mm(ps[:, :], l, r, kk == 0 and i == 0, kk == b["total"] - 1 and i == 2)
                    if k == b["kn"] - 1 and b["closing"]:
                        last.then_inc(s_tile, 1)
                if s == SLICES - 1 and not b["closing"]:
                    last.then_inc(s_blk, 1)

            def turn(name, t, half, g):
                src = {"x": xt, "y": xs, "mix": xn, "hgrn": mixt, "ffn": xn}[name]
                if (name, t, half) == ("x", 0, 0):
                    pe.wait_ge(s_ident, 16)
                pe.wait_ge(*((s_hg, t + 1) if name == "hgrn" else (s_norm, norm_no(name, t))))
                free_bank(g)
                c0 = 512 * half if name != "hgrn" else 0
                for i in range(4):
                    last = nc.tensor.transpose(bank[BANK[g]][:, P * i:P * i + P], src[:, t, c0 + P * i:c0 + P * i + P], ident)
                last.then_inc(s_tile, 1)

            def small_block(kind, g, cols):
                pe.wait_ge(s_slo, 1 if kind == "dt" else 2)
                need_split(SPLIT_NEED["small", kind])
                free_bank(g)
                ps = bank[BANK[g]][0:cols, :]
                for k in range(NK):
                    h, l = swhi[:, cols * k:cols * k + cols], swlo[:, cols * k:cols * k + cols]
                    for i, (w, a) in enumerate(((h, a_hi), (h, a_lo), (l, a_hi))):
                        last = mm(ps, w, a[:, k, :], k == 0 and i == 0, k == NK - 1 and i == 2)
                last.then_inc(s_tile, 1)

            def small_turn(kind, g, cols):
                pe.wait_ge(*end_sem(kind + "_t"))
                free_bank(g)
                for t in range(NT):
                    last = nc.tensor.transpose(bank[BANK[g]][:, cols * t:cols * t + cols],
                                               small_t[kind][0:cols, P * t:P * t + P], ident[0:cols, 0:cols])
                last.then_inc(s_tile, 1)

            def qkturn(i, g):
                pe.wait_ge(s_norm, norm_no("qk", NT - 1))
                free_bank(g)
                for t in range(NT):
                    src = qn_[:, t, i, :] if i < 4 else kst[:, t, P * (i - 4):P * (i - 4) + P]
                    last = nc.tensor.transpose(bank[BANK[g]][:, P * t:P * t + P], src, ident)
                last.then_inc(s_tile, 1)

            def positions():
                pe.wait_ge(s_late, 80)
                for b in range(2):
                    for j in range(CL // 2):
                        last = mm(bank[5][0:1, P * b:P * b + P], pos[:, b, j:j + 1], w1[b][:, j, :], j == 0, j == CL // 2 - 1)
                last.then_inc(s_pos, 1)

            def compress(i):
                if i == 0:
                    pe.wait_ge(s_kc2, 64)
                    pe.wait_ge(s_posr, 1)
                    for b in range(2):
                        o = bank[4][:, 64 * b:64 * b + 64].rearrange("p (a b) -> p a b", b=32)[:, :, 0:NCMP]
                        for j in range(CL // 2):
                            mm(o, w1[b][:, j, :], kc2[:, b, :, 2 * j:2 * j + CS * (NCMP - 1) + 1:CS], j == 0, False)
                        last = mm(o, posr[0:1, P * b:P * b + P], one[0:1, 0:2 * NCMP].rearrange("p (a b) -> p a b", b=NCMP),
                                  False, True)
                    last.then_inc(s_hid, 1)
                if i == 1:
                    pe.wait_ge(s_gelu, 2)
                    for g in range(NG):
                        last = mm(bank[6][0:32, HD * g:HD * g + HD], hid[:, 0, g, :], w2[:, 0, :], True, True)
                    last.then_inc(s_hid, 1)
                if i == 2:
                    pe.wait_ge(s_hid4, NG)
                    for g in range(NG):
                        last = mm(bank[7][:, HD * g:HD * g + HD], hid4[:, g, :, :].rearrange("p a b -> p (a b)"),
                                  w2[:, 1, :], True, True)
                    last.then_inc(s_hid, 1)
                if i == 3:
                    pe.wait_ge(s_norm, norm_no("kc", 0))
                    nc.tensor.transpose(bank[4][:, 0:32], kcn[0:32, :], ident[0:32, 0:32]).then_inc(s_kct, 1)

            def cmp(qt, i):
                if i == 0:
                    pe.wait_ge(s_kcr, 1)
                    if qt == 0:
                        pe.wait_ge(s_vcd, 1)
                        pe.wait_ge(*ended(tile_of("turn_qk", 5)))
                    if qt >= 1:
                        pe.wait_ge(s_cs, qt)
                    for h in range(NH):
                        g, r = divmod(h, 4)
                        rows_ = slice(HD * g, HD * g + HD)
                        last = mm(bank[4 + 3 * g][:, 32 * r:32 * r + NCMP], qT[rows_, r, P * qt:P * qt + P],
                                  kcT[rows_, 0:NCMP], True, True)
                    last.then_inc(s_cqk, 1)
                if i == 2:
                    pe.wait_ge(s_cp, qt + 1)
                    if qt >= 1:
                        pe.wait_ge(s_cpt, qt)
                    for g in range(NG):
                        last = nc.tensor.transpose(bank[5][:, P * g:P * g + P],
                                                   cs_[qt % 2][:, 4 * g:4 * g + 4, :].rearrange("p a b -> p (a b)"), ident)
                    last.then_inc(s_ctr, 1)

            def nsa(u):
                def turned(v, b):
                    kend = P * (v // NH + 1)
                    if kend <= 256 and b == 0:
                        return
                    pe.wait_ge(s_nw, v + 1)
                    n = 2 * v + b if kend > 256 else 2 * v
                    if n > 0:
                        pe.wait_ge(s_npt, n)
                    both = range(2) if kend <= 256 else (b,)
                    for b_ in both:
                        for kb in range(kend // P):
                            o = kend * b_ + P * kb if kend <= 256 else P * kb
                            last = nc.tensor.transpose(bank[BANK_WT][:, o:o + P], np_[v % 3][:, b_, P * kb:P * kb + P], ident)
                    last.then_inc(s_ntr, len(both))

                def summed(v, b):
                    qt, h = divmod(v, NH)
                    out_ = bank[BANK_O]
                    if h == 0 and b == 0:
                        if qt == 0:
                            pe.wait_ge(s_cpt, NT)
                            pe.wait_ge(s_zero, 2)
                        else:
                            pe.wait_ge(s_nm, qt)
                        mm(out_[:, :], identb, zerob[:, 0:1].to_broadcast([P, 512]), True, False, skip_group_check=True)
                        for c in range(4):
                            mm(out_[:, P * c:P * c + P], vcd[:, c // 2, 2 * (c % 2):2 * (c % 2) + 2, :].rearrange("p a b -> p (a b)"),
                               cpT[:, qt, c // 2, :], False, False, skip_group_check=True)
                    pe.wait_ge(s_npt, 2 * v + b + 1)
                    o = out_[HD * (h % 2):HD * (h % 2) + HD, P * (h // 2):P * (h // 2) + P]
                    for kb in range(qt + 1):
                        end = kb == qt and b == 1 and h == NH - 1
                        last = mm(o, vst[:, kb, P * b + HD * (h // 4):P * b + HD * (h // 4) + HD],
                                  npT[:, b, P * kb:P * kb + P], False, end, skip_group_check=True)
                    last.then_inc(s_npv, 1)

                v, w = u - NSA_LAG, u - NSA_LAG - 1
                if u < UNITS:
                    qt, h = divmod(u, NH)
                    g, r = divmod(h, 4)
                    rows_, kend = slice(HD * g, HD * g + HD), P * (qt + 1)
                    if u == 0:
                        pe.wait_ge(s_cs, NT)
                        pe.wait_ge(s_cpt, NT)
                    n = 2 * u if kend > 256 else 2 * (u - 1)
                    if n > 0:
                        pe.wait_ge(s_np, n)
                    if kend <= 256:
                        ps = bank[BANK_LOGITS + u % 2][:, 0:2 * kend].rearrange("p (a b) -> p a b", b=kend)
                        mm(ps, qT[rows_, r, P * qt:P * qt + P], kT[rows_, :, 0:kend], True, False)
                        mm(ps[:, :, kend - P:kend], identb, after.unsqueeze(1).to_broadcast([P, 2, P]), False, True)                            .then_inc(s_nqk, 2)
                    else:
                        for b in range(2):
                            ps = nsa_logits(u, b)
                            mm(ps, qT[rows_, r, P * qt:P * qt + P], kT[rows_, b, 0:kend], True, False)
                            mm(ps[:, kend - P:kend], identb, after, False, True).then_inc(s_nqk, 1)
                if 0 <= w < UNITS:
                    summed(w, 0)
                if 0 <= v < UNITS:
                    turned(v, 0)
                if 0 <= w < UNITS:
                    summed(w, 1)
                if 0 <= v < UNITS:
                    turned(v, 1)

            def level(h, n, g):
                q_, k_ = hqk[n % 2]
                pe.wait_ge(s_hlev, (LEVELS + 1) * h + n + 1)
                free_bank(g)
                ps, w = bank[BANK[g]], 2 ** (n - 1) if n else 0
                if n == 0:
                    last = mm(ps[:, :], one[:, 0:1].to_broadcast([P, P]), k_, True, True)
                elif n == 1:
                    last = mm(ps[:, 1:T:2], one[:, 0:1].to_broadcast([P, P]), k_[:, 1:T:2], True, True)
                elif w < P:
                    up = lambda ap: ap.rearrange("p (a b c) -> p a b c", b=2, c=w)[:, :, 1, :]
                    rows_ = HD if w == HD else P
                    for t in range(NT):
                        ts = slice(P * t, P * t + P)
                        last = mm(up(ps[0:rows_, ts]), k_[:, P * t:P * t + rows_], up(q_[:, ts]), True, True)
                elif w == P:
                    for i in range(2):
                        last = mm(ps[:, P * i:P * i + P], k_[:, 2 * P * i:2 * P * i + P],
                                  q_[:, 2 * P * i + P:2 * P * i + 2 * P], True, True)
                else:
                    for i in range(2):
                        last = mm(ps[:, 256 * i:256 * i + 256], k_[:, P * i:P * i + P], q_[:, 256:512], True, True)
                last.then_inc(s_tile, 1)

            def hout(h, g):
                pe.wait_ge(*ended(level_tile(h, LEVELS)))
                pe.wait_ge(*ended(tile_of("hi", (NT - 1, 0))))
                free_bank(g)
                for t in range(NT):
                    for s_ in range(t + 1):
                        if s_ == t:
                            lhs = hat[:, P * t:P * t + P]
                        elif t >= 2 and s_ < 2:
                            lhs = hat[:, 768 + 256 * s_ + P * (t - 2):768 + 256 * s_ + P * (t - 2) + P]
                        else:
                            lhs = hat[:, 512 + P * (t // 2):512 + P * (t // 2) + P]
                        last = mm(bank[BANK[g]][:, P * t:P * t + P], lhs, hit[:, s_, P * h:P * h + P], s_ == 0, s_ == t)
                last.then_inc(s_tile, 1)

            def xturn(c):
                pe.wait_ge(s_cx, c + 1)
                ps = free_aux(("xturn", c))
                src = cx[:, c % 2, :] if c < 8 else bct[:, c - 8, :]
                for t in range(NT):
                    last = nc.tensor.transpose(ps[:, P * t:P * t + P], src[:, P * t:P * t + P], ident)
                last.then_inc(s_aux, 1)

            def ssd_decay():
                pe.wait_ge(s_dt, 1)
                ps = free_aux("decay")
                mm(ps[:, 0:64], tri, adt, True, True)
                mm(ps[:, 64:128], ones, adt, True, True).then_inc(s_aux, 1)

            def ssd(c, part):
                ts = slice(P * c, P * c + P)

                def y_diag(j):
                    pe.wait_ge(s_attn, 4 * c + j + 1)
                    if j == 0:
                        pe.wait_ge(s_xd, 2 * c + 1)
                        if c >= 1:
                            pe.wait_ge(s_y, c)
                    for i in range(4):
                        h = 4 * j + i
                        last = mm(bank[6 + j // 2][:, (h % 8) * HD:(h % 8) * HD + HD], ee[:, j % 2, i, :],
                                  xdt[:, c % 2, h * HD:h * HD + HD], True, True)
                    last.then_inc(s_yd, 1)

                if part == 0:
                    pe.wait_ge(s_cx, XC)
                    ps = free_aux(("scores", c))
                    for g in range(2):
                        last = mm(ps[:, P * g:P * g + P], bct[:, g, ts], bct[:, 2 + g, ts], True, True)
                    last.then_inc(s_aux, 1)
                if part < 4:
                    pe.wait_ge(s_cst, 32)
                    ps = free_aux(("decay", c, part))
                    mm(ps[:, :], identb, after.unsqueeze(1).to_broadcast([P, 4, P]), True, False)
                    n = 4 * c + part
                    pe.wait_ge(s_tri, n + 1)
                    mm(ps[:, :], ones_r, b_hi[:, n % 4, :], False, False)
                    mm(ps[:, :], ones_r, b_lo[:, n % 4, :], False, True).then_inc(s_aux, 1)
                    if part >= 1:
                        y_diag(part - 1)
                if part == 4:
                    if c > 0:
                        pe.wait_ge(s_st, 2 * c)
                        for g in range(2):
                            ps = free_aux(("y_off", c, g))
                            mm(ps[:, :], bct[:, 2 + g, ts], state[:, g, :], True, True).then_inc(s_aux, 1)
                    y_diag(3)
                    if c < NT - 1:
                        pe.wait_ge(s_xd, 2 * c + 2)
                        for g in range(2):
                            ps = free_aux(("state", c, g))
                            mm(ps[:, :], btok[:, c, P * g:P * g + P], xdd[:, 512 * g:512 * g + 512], True, True)\
                                .then_inc(s_aux, 1)

            def stick(u):
                if u < SH * NT:
                    h, qt = divmod(u, NT)
                    rows, kend = slice(HD * (h % 2), HD * (h % 2) + HD), P * (qt + 1)
                    if u >= 2:
                        pe.wait_ge(s_sig, u - 1)
                    ps = bank[BANK_LOGITS + u % 2]
                    if u == 0:
                        pe.wait_ge(*end_sem("v"))
                        need_split(max(SPLITS.index(x) for x in SPLITS if x[:2] == ("turn", "y")) + 1)
                    mm(ps[:, 0:kend], qf[rows, h // 2, P * qt:P * qt + P], kf[rows, h // 2, 0:kend], True, False)
                    mm(ps[:, kend - P:kend], identb, strict, False, True).then_inc(s_qk, 1)
                v = u - SB_LAG
                if 0 <= v < SH * NT:
                    pe.wait_ge(s_wgt, v + 1)
                    if v >= 1:
                        pe.wait_ge(s_wT, v)
                    for kb in range(v % NT + 1):
                        last = nc.tensor.transpose(bank[BANK_WT][:, P * kb:P * kb + P], sb_w[:, v % 3, P * kb:P * kb + P], ident)
                    last.then_inc(s_tr, 1)
                v = u - SB_LAG - 1
                if 0 <= v < SH * NT:
                    h, qt = divmod(v, NT)
                    rows = slice(HD * (h % 2), HD * (h % 2) + HD)
                    pe.wait_ge(s_wT, v + 1)
                    if v >= 1:
                        pe.wait_ge(s_o, v)
                    for kb in range(qt + 1):
                        last = mm(bank[BANK_O][rows, P * (v % 4):P * (v % 4) + P], vt[:, kb, h * HD:h * HD + HD],
                                  sb_wT[:, v % 2, P * kb:P * kb + P], kb == 0, kb == qt)
                    last.then_inc(s_pv, 1)

            for s in STEPS:
                if s[0] == "gemm":
                    gemm(*s[1:])
                if s[0] == "turn":
                    turn(*s[1:])
                if s[0] == "small":
                    small_block(s[1], s[2], SH if s[1] == "dt" else 24)
                if s[0] == "smallturn":
                    small_turn(s[1], s[2], SH if s[1] == "dt" else 24)
                if s[0] == "qkturn":
                    qkturn(*s[1:])
                if s[0] == "positions":
                    positions()
                if s[0] == "compress":
                    compress(s[1])
                if s[0] == "cmp":
                    cmp(*s[1:])
                if s[0] == "nsa":
                    nsa(s[1])
                if s[0] == "level":
                    level(*s[1:])
                if s[0] == "hout":
                    hout(*s[1:])
                if s[0] == "xturn":
                    xturn(s[1])
                if s[0] == "ssd_decay":
                    ssd_decay()
                if s[0] == "ssd":
                    ssd(s[1], s[2])
                if s[0] == "sb":
                    stick(s[1])

        @block.scalar
        def _(act):
            A = nc.scalar.activation
            chain = [0]

            def link(ins):
                chain[0] += 1
                ins.then_inc(s_ac, 1)
                act.wait_ge(s_ac, chain[0])

            def round_weights(n):
                if n >= NB:
                    return
                act.wait_ge(s_w[n % 2], 16 * (n // 2 + 1))
                if n >= 2:
                    act.wait_ge(*used_by_pe(n - 2))
                cols = width(n)
                A(whi[n % 2][:, 0:cols], wraw[n % 2][:, 0:cols], ACT.Copy).then_inc(s_hi, 1)

            def round_small(kind):
                cols = NK * (SH if kind == "dt" else 24)
                act.wait_ge(s_sw, 16 if kind == "dt" else 32)
                if kind == "gates":
                    act.wait_ge(s_tile, DONE[tile_of("dt", 0)])
                A(swhi[:, 0:cols], swraw[:, 0:cols], ACT.Copy).then_inc(s_shi, 1)

            def sigmoid(g, kind, i):
                k = SIG_TILES.index(g)
                if k >= 2:
                    o = SIG_TILES[k - 2]
                    act.wait_ge(*ended(o + CONSUMER[TILES[o][0]]))
                bias = 0.0
                if kind in ("gate", "gate2"):
                    bias = V("b_gate", i + (8 if kind == "gate2" else 0))
                ins = A(sgt[:, k % 2, :], bank[BANK[g]][:, :], ACT.Sigmoid, bias=bias)
                ins.then_inc(s_end["S"] if READER[kind] == "S" else s_sg, 1)

            def conv_sigmoid(i):
                act.wait_ge(s_conv, i + 1)
                if i >= 2:
                    act.wait_ge(s_cx, i - 1)
                A(csig[:, i % 2, :], cacc[:, i % 2, :], ACT.Sigmoid).then_inc(s_csig, 1)

            def tile(g):
                kind, i = TILES[g]
                ps = bank[BANK[g]]
                if kind in ("dt", "y_ssd", "y_sb", "out2", "down"):
                    return
                act.wait_ge(s_tile, DONE[g])
                if kind == "xbc":
                    if i >= 2:
                        act.wait_ge(s_conv, i - 1)
                    A(craw[:, i % 2, :], ps[:, :], ACT.Copy).then_inc(s_end["S"], 1)
                    if i >= 1:
                        conv_sigmoid(i - 1)
                    if i == XC - 1:
                        conv_sigmoid(i)
                if kind in SIGMOID:
                    if kind == "z" and i == (0, 0):
                        act.wait_ge(s_y, NT)
                    sigmoid(g, kind, i)
                if kind in ("z_sb", "ff_up"):
                    p = PRODUCTS.index(("tile", g))
                    act.wait_ge(s_t, T_READY[p])
                    c = i if kind == "z_sb" else i[1]
                    A(b_hi[:, c, :], tt[:, p % 2, :], ACT.Copy).then_inc(s_tround, 1)
                if kind == "kv":
                    src = ps[:, :].rearrange("p (a b c) -> p a b c", b=2, c=P)
                    pair = lambda ap: ap.rearrange("p (a b) -> p a b", b=P)
                    A(pair(kst[:, i[0], :]), src[:, :, 0, :], ACT.Copy)
                    A(pair(vst[:, i[0], :]), src[:, :, 1, :], ACT.Copy).then_inc(s_end["S"], 1)
                if kind == "qn":
                    A(qt_[:, i[0], :], ps[:, :], ACT.Copy).then_inc(s_end["S"], 1)
                if kind == "kcv":
                    A(kcf[:, i, :], ps[:, :], ACT.Copy).then_inc(s_end["S"], 1)
                    if i == 1:
                        act.wait_ge(*ended(g))
                        for g_ in range(NG):
                            for later in range(2):
                                act.dma_start(kc2[HD * later:HD * later + HD, :, g_, 0:T - later],
                                              kcf[HD * g_:HD * g_ + HD, :, later:T]).then_inc(s_kc2, 16)
                if kind == "hi":
                    A(hit[:, i[0], :], ps[:, :], ACT.Copy).then_inc(s_end["S"], 1)
                if kind == "k":
                    A(kf[:, i, :], ps[:, :], ACT.Copy).then_inc(s_end["S"], 1)
                if kind == "q":
                    A(qf[:, i, :], ps[:, :], ACT.Copy).then_inc(s_end["S"], 1)
                if kind == "v":
                    t, half = i
                    A(vt[:, t, 512 * half:512 * half + 512], ps[:, :], ACT.Copy).then_inc(s_end["S"], 1)
                if kind == "out1":
                    t, half = i
                    A(oraw[:, t, 512 * half:512 * half + 512], ps[:, :], ACT.Copy)
                    if i == (0, 0):
                        act.wait_ge(s_mg, NK)
                    link(A(sgt[:, 0, :], ps[:, :], ACT.Square, accum_out=sso[:, 2 * t + half:2 * t + half + 1]))
                    act.sem_inc(s_end["S"], 1)

            def root(name, t):
                act.wait_ge(s_rec, NORMS.index((name, t)) + 1)
                a, n = norm_cols(name, t)
                r = nss[name][0:32 if name == "kc" else P, a:a + n]
                A(r, r, ACT.Sqrt).then_inc(s_rt, 1)

            def norm(name, t):
                if name == "x":
                    act.wait_ge(s_x[t], 16)
                if name == "y":
                    act.wait_ge(s_yz, NT + t + 1)
                if name == "mix":
                    act.wait_ge(s_norm, norm_no("out1", t))
                if name == "ffn":
                    act.wait_ge(*ended(tile_of("out2", (t, 1))))
                src, junk = {"x": (xt, junks["x"]), "y": (xs, junks["y"]), "mix": (xres, xn), "ffn": (x2, xn)}.get(name, (0, 0))
                if name == "y":
                    for g in range(2):
                        cols = slice(512 * g, 512 * g + 512)
                        last = A(junk[:, t, cols], src[:, t, cols], ACT.Square, accum_out=nss[name][:, 2 * t + g:2 * t + g + 1])
                    last.then_inc(s_ss, 1)
                elif name in SQUARED:
                    A(junk[:, t, :], src[:, t, :], ACT.Square, accum_out=nss[name][:, t:t + 1]).then_inc(s_ss, 1)

            def turn(name, t, half, g):
                act.wait_ge(s_tile, DONE[g])
                A(ACTS[FILLS[name]][0][:, 4 * half:4 * half + 4, P * t:P * t + P],
                  bank[BANK[g]][:, :].rearrange("p (a b) -> p a b", b=P), ACT.Copy).then_inc(s_round, 1)

            def stick(u):
                if u < SH * NT:
                    kend = P * (u % NT + 1)
                    act.wait_ge(s_qk, u + 1)
                    if u >= 2:
                        act.wait_ge(s_wgt, u - 1)
                    ps = bank[BANK_LOGITS + u % 2]
                    f0 = 516 * (u % 2)
                    if u < 2:
                        act.wait_ge(s_zero, 1)
                    A(sb_sig[:, u % 2, 0:kend], ps[:, 0:kend], ACT.Sigmoid, scale=SCALE)
                    A(sb_fail[:, f0 + 512 - kend:f0 + 512], ps[:, 0:kend], ACT.Sigmoid, scale=-SCALE).then_inc(s_sig, 1)
                v = u - SB_LAG
                if 0 <= v < SH * NT:
                    kend = P * (v % NT + 1)
                    act.wait_ge(s_tr, v + 1)
                    if v >= 2:
                        act.wait_ge(s_pv, v - 1)
                    A(sb_wT[:, v % 2, 0:kend], bank[BANK_WT][:, 0:kend], ACT.Copy).then_inc(s_wT, 1)

            def dt_part(i):
                if i == 1:
                    act.wait_ge(s_dte, 1)
                    A(t64[1], t64[1], ACT.Exp).then_inc(s_ex, 1)
                    A(aexp, V("a_log", 0, SH), ACT.Exp).then_inc(s_ex, 1)
                if i == 2:
                    act.wait_ge(s_dte, 2)
                    A(t64[1], t64[1], ACT.Ln).then_inc(s_ex, 1)

            def small_gates(g):
                act.wait_ge(s_tile, DONE[g])
                A(gl, bank[BANK[g]][:, 0:96], ACT.Sigmoid).then_inc(s_end["S"], 1)

            def compress(i):
                if i == 0:
                    act.wait_ge(s_hidz, 1)
                    act.wait_ge(s_hid, 1)
                    for b in range(2):
                        A(hid[:, b, :, 0:NCMP], bank[4][:, 64 * b:64 * b + 64].rearrange("p (a b) -> p a b", b=32)[:, :, 0:NCMP],
                          ACT.Gelu_apprx_tanh).then_inc(s_gelu, 1)
                if i == 1:
                    root("kc", 0)
                if i == 3:
                    act.wait_ge(s_kct, 1)
                    A(kcT, bank[4][:, 0:32], ACT.Copy, scale=V("k_norm", 0)).then_inc(s_kcr, 1)

            def cmp(qt, i):
                if i == 0:
                    act.wait_ge(s_cs, qt + 1)
                    A(cs_[qt % 2][:, :, :], cs_[qt % 2][:, :, :], ACT.Exp).then_inc(s_ce, 1)
                if i == 2:
                    act.wait_ge(s_ctr, qt + 1)
                    A(cpT[:, qt, :, :], bank[5][:, 0:256].rearrange("p (a b) -> p a b", b=P), ACT.Copy).then_inc(s_cpt, 1)

            def nsa(u):
                def read_turned(v, b):
                    kend = P * (v // NH + 1)
                    if kend <= 256 and b == 0:
                        return
                    act.wait_ge(s_ntr, 2 * v + b + 1)
                    if v >= 1:
                        act.wait_ge(s_npv, 2 * v + b - 1)
                    if kend <= 256:
                        A(npT[:, :, 0:kend], bank[BANK_WT][:, 0:2 * kend].rearrange("p (a b) -> p a b", b=kend), ACT.Copy)                            .then_inc(s_npt, 2)
                    else:
                        A(npT[:, b, 0:kend], bank[BANK_WT][:, 0:kend], ACT.Copy).then_inc(s_npt, 1)

                v, w = u - NSA_LAG, u - NSA_LAG - 1
                if 0 <= v < UNITS:
                    read_turned(v, 0)
                if u < UNITS:
                    kend = P * (u // NH + 1)
                    act.wait_ge(s_nmx, u + 1)
                    if u >= 3:
                        act.wait_ge(s_ntr, 2 * (u - 2))
                    for b in range(2):
                        A(np_[u % 3][:, b, 0:kend], nsa_logits(u, b), ACT.Exp,
                          bias=nmx[:, 2 * u + b:2 * u + b + 1], accum_out=nsum[:, 2 * u + b:2 * u + b + 1]).then_inc(s_np, 1)
                if 0 <= v < UNITS:
                    read_turned(v, 1)
                if w >= 0 and w % NH == NH - 1:
                    qt = w // NH
                    act.wait_ge(s_npv, 2 * w + 2)
                    A(b_hi[:, 0:4, P * qt:P * qt + P], bank[BANK_O][:, :].rearrange("p (a b) -> p a b", b=P), ACT.Copy)\
                        .then_inc(s_round, 1)

            for s in STEPS:
                if s == ("apply", "x", NT - 1):
                    round_small("dt")
                if s[0] == "small":
                    if s[1] == "dt":
                        round_weights(0)
                    act.wait_ge(s_tile, DONE[s[2]])
                    cols = SH if s[1] == "dt" else 24
                    if s[1] == "gates":
                        act.wait_ge(s_hlb, 1)
                        A(lbs, lbs, ACT.Sigmoid).then_inc(s_hlb, 1)
                        act.wait_ge(s_norm, norm_no("qk", NT - 1))
                    A(small_t[s[1]][0:cols, :], bank[BANK[s[2]]][0:cols, :], ACT.Copy).then_inc(s_end["S"], 1)
                if s[0] == "dt":
                    dt_part(s[1])
                if s[0] == "smallturn" and s[1] == "gates":
                    small_gates(s[2])
                if s[0] == "apply":
                    root(*s[1:])
                if s[0] == "pos":
                    round_small("gates")
                    act.wait_ge(s_pos, 1)
                    A(posr[0:1, :], bank[5][0:1, 0:2 * P], ACT.Copy).then_inc(s_posr, 1)
                if s[0] == "qkturn":
                    i, g = s[1:]
                    act.wait_ge(s_tile, DONE[g])
                    dst = qT[:, i, :] if i < 4 else kT[:, i - 4, :]
                    A(dst, bank[BANK[g]][:, :], ACT.Copy,
                      scale=V("q_norm") if i < 4 else V("k_norm", i - 3)).then_inc(s_end["S"], 1)
                if s[0] == "compress":
                    compress(s[1])
                if s[0] == "cmp":
                    cmp(*s[1:])
                if s[0] == "nsa":
                    nsa(s[1])
                if s[0] == "hout":
                    h, g = s[1:]
                    act.wait_ge(s_tile, DONE[g])
                    A(mixt[:, :, P * h:P * h + P], bank[BANK[g]][:, :].rearrange("p (a b) -> p a b", b=P), ACT.Copy)\
                        .then_inc(s_end["S"], 1)
                if s[0] == "norm":
                    norm(*s[1:])
                if s[0] == "turn":
                    turn(*s[1:])
                if s[0] == "gemm":
                    if s[2] == 0:
                        round_weights(s[1] + 1)
                    for g in closed(BLOCKS[s[1]], s[2]):
                        tile(g)
                if s[0] == "xturn":
                    c = s[1]
                    act.wait_ge(s_aux, AUX.at[("xturn", c)] + 1)
                    dst = xs[:, :, P * c:P * c + P] if c < 8 else btok[:, :, P * (c - 8):P * (c - 8) + P]
                    A(dst, bank[4 + AUX.slot(("xturn", c))][:, :].rearrange("p (a b) -> p a b", b=P), ACT.Copy)\
                        .then_inc(s_auxend["S"], 1)
                if s[0] == "ssd_decay":
                    act.wait_ge(s_dte, 3)
                    A(ecs, t64[0], ACT.Exp)
                    A(edec, t64[1], ACT.Exp)
                    A(dtend, t64[2], ACT.Exp).then_inc(s_ex, 1)
                if s[0] == "ssd" and s[2] < 4:
                    _, c, j = s
                    key = ("decay", c, j)
                    act.wait_ge(s_aux, AUX.at[key] + 1)
                    n_ = 4 * c + j
                    if n_ >= 2:
                        act.wait_ge(s_yd, n_ - 1)
                    for i in range(4):
                        col = SH * c + 4 * j + i
                        last = A(ee[:, j % 2, i, :], bank[4 + AUX.slot(key)][:, P * i:P * i + P], ACT.Exp,
                                 bias=acs_n[:, col:col + 1])
                    last.then_inc(s_auxend["S"], 1)
                if s[0] == "sb":
                    stick(s[1])
                if s[0] == "merge":
                    c = s[1]
                    if c == 0:
                        act.wait_ge(*used_by_pe(MERGE_AFTER))
                        act.wait_ge(s_mg, NK)
                    A(a_hi[:, c, :], mg[:, c, :], ACT.Copy).then_inc(s_tround, 1)

        @block.vector
        def _(dve):
            v = nc.vector
            chain, updated = [0], [0]
            h64 = lambda ap: ap.rearrange("p (a b) -> p a b", b=HD)

            def link(ins):
                chain[0] += 1
                ins.then_inc(s_vc, 1)
                dve.wait_ge(s_vc, chain[0])

            def mark(ins):
                chain[0] += 1
                ins.then_inc(s_vc, 1)
                return chain[0]

            def rest_of_weights(n):
                if n >= NB:
                    return
                dve.wait_ge(s_hi, n + 1)
                cols = width(n)
                v.tensor_tensor(wlo[n % 2][:, 0:cols], wraw[n % 2][:, 0:cols], f32(whi[n % 2][:, 0:cols]),
                                ALU.subtract).then_inc(s_lo, 1)

            def rest_of_small(kind):
                dve.wait_ge(s_shi, 1 if kind == "dt" else 2)
                cols = NK * (SH if kind == "dt" else 24)
                v.tensor_tensor(swlo[:, 0:cols], swraw[:, 0:cols], f32(swhi[:, 0:cols]), ALU.subtract).then_inc(s_slo, 1)

            def conv(i, g):
                dve.wait_ge(*ended(g))
                if i == 0:
                    dve.wait_ge(s_cst, 32)
                if i >= 2:
                    dve.wait_ge(s_cx, i - 1)
                acc, x_ = cacc[:, i % 2, :], craw[:, i % 2, :]
                link(v.tensor_scalar(acc, x_, V("conv_w", 4 * i + 3), V("conv_b", i), ALU.mult, ALU.add))
                for j in (1, 2, 3):
                    ins = v.scalar_tensor_tensor(acc[:, j:T], x_[:, 0:T - j], V("conv_w", 4 * i + 3 - j),
                                                 acc[:, j:T], ALU.mult, ALU.add)
                    if j < 3:
                        link(ins)
                ins.then_inc(s_conv, 1)

            def silu(i):
                dve.wait_ge(s_csig, i + 1)
                if 2 <= i < 8:
                    dve.wait_ge(s_aux, AUX.at[("xturn", i - 2)] + 1)
                dst = cx[:, i % 2, :] if i < 8 else bct[:, i - 8, :]
                v.tensor_tensor(dst, cacc[:, i % 2, :], csig[:, i % 2, :], ALU.mult).then_inc(s_cx, 1)

            def tile(g):
                kind, i = TILES[g]
                ps = bank[BANK[g]]
                if kind == "xbc":
                    conv(i, g)
                    if i >= 1:
                        silu(i - 1)
                    if i == XC - 1:
                        silu(i)
                if kind == "z":
                    t, half = i
                    sg = sgt[:, SIG_TILES.index(g) % 2, :]
                    y = xs[:, t, 512 * half:512 * half + 512]
                    dve.wait_ge(*sigmoid_ready(g))
                    link(v.tensor_tensor(sg, ps[:, :], sg, ALU.mult))
                    v.tensor_tensor(y, y, sg, ALU.mult).then_inc(s_yz, 1)
                    dve.wait_ge(s_yz, 4 * half + t + 1)
                    dve.sem_inc(s_end["V"], 1)
                if kind in ("y_ssd", "y_sb"):
                    dve.wait_ge(s_tile, DONE[g])
                    k = SIG_TILES.index(g - 1)
                    dve.wait_ge(*sigmoid_ready(g - 1))
                    sg = sgt[:, k % 2, :]
                    if kind == "y_ssd":
                        v.tensor_tensor(mg[:, i, :], ps[:, :], sg, ALU.mult).then_inc(s_end["V"], 1)
                    else:
                        link(v.tensor_tensor(sg, ps[:, :], sg, ALU.mult))
                        v.tensor_tensor(mg[:, i, :], mg[:, i, :], sg, ALU.add).then_inc(s_mg, 1)
                        dve.wait_ge(s_mg, i + 1)
                        dve.sem_inc(s_end["V"], 1)
                if kind == "hg":
                    dve.wait_ge(*sigmoid_ready(g))
                    link(v.tensor_tensor(hgt[:, i[0], :], ps[:, :], sgt[:, SIG_TILES.index(g) % 2, :], ALU.mult))
                    dve.sem_inc(s_end["V"], 1)
                    dve.wait_ge(s_norm, norm_no("hgrn", i[0]))
                    v.tensor_tensor(mixt[:, i[0], :], mixt[:, i[0], :], hgt[:, i[0], :], ALU.mult).then_inc(s_hg, 1)
                if kind == "hq":
                    dve.wait_ge(*sigmoid_ready(g))
                    if i == 0:
                        dve.wait_ge(s_hid, 1)
                    if i == 1:
                        dve.wait_ge(s_ctr, NT)
                    v.tensor_tensor(hset[i % 2][0], ps[:, :], sgt[:, SIG_TILES.index(g) % 2, :], ALU.mult)\
                        .then_inc(s_end["V"], 1)
                if kind == "hf":
                    dve.wait_ge(*sigmoid_ready(g))
                    _, hk_, pre, suf = hset[i % 2]
                    link(v.tensor_scalar(pre, sgt[:, SIG_TILES.index(g) % 2, :], lbn[:, i:i + 1], lbs[:, i:i + 1],
                                         ALU.mult, ALU.add))
                    dve.sem_inc(s_end["V"], 1)
                    link(v.tensor_scalar(hk_, pre, -1.0, 1.0, ALU.mult, ALU.add))
                    if i > 0:
                        dve.wait_ge(s_tile, DONE[level_tile(i - 1, LEVELS - 1)])
                    v.tensor_tensor(hqk[0][1], hset[i % 2][0], hk_, ALU.mult).then_inc(s_hlev, 1)
                if kind in ("out2", "down"):
                    t, half = i if kind == "out2" else (i[0], i[1][1])
                    dve.wait_ge(s_tile, DONE[g])
                    if kind == "out2":
                        dve.wait_ge(s_back, 16)
                    x = x2[:, t, 512 * half:512 * half + 512]
                    v.tensor_tensor(x, x, ps[:, :], ALU.add).then_inc(s_end["V"], 1)
                if kind == "ff_gate":
                    dve.wait_ge(*sigmoid_ready(g))
                    sg = sgt[:, SIG_TILES.index(g) % 2, :]
                    link(v.tensor_tensor(sg, sg, ps[:, :], ALU.mult))
                    dve.sem_inc(s_end["V"], 1)
                if kind == "ff_up":
                    p = PRODUCTS.index(("tile", g))
                    dve.wait_ge(s_tile, DONE[g])
                    sg = sgt[:, SIG_TILES.index(g - 1) % 2, :]
                    v.tensor_tensor(tt[:, p % 2, :], sg, ps[:, :], ALU.mult).then_inc(s_t, 1)
                    dve.wait_ge(s_t, T_READY[p])
                    dve.sem_inc(s_end["V"], 1)
                    dve.wait_ge(s_tround, p + 1)
                    v.tensor_tensor(b_lo[:, i[1], :], tt[:, p % 2, :], f32(b_hi[:, i[1], :]), ALU.subtract).then_inc(s_split, 1)
                if kind == "z_sb":
                    k = SIG_TILES.index(g)
                    p = PRODUCTS.index(("tile", g))
                    dve.wait_ge(*sigmoid_ready(g))
                    if i == 0:
                        dve.wait_ge(s_tr, SH * NT)
                        dve.wait_ge(s_o, SH * NT)
                    link(v.tensor_tensor(sgt[:, k % 2, :], ps[:, :], sgt[:, k % 2, :], ALU.mult))
                    v.tensor_tensor(tt[:, p % 2, :], qf[:, i, :], sgt[:, k % 2, :], ALU.mult).then_inc(s_t, 1)
                    dve.wait_ge(s_t, T_READY[p])
                    dve.sem_inc(s_end["V"], 1)
                    dve.wait_ge(s_tround, p + 1)
                    v.tensor_tensor(b_lo[:, i, :], tt[:, p % 2, :], f32(b_hi[:, i, :]), ALU.subtract).then_inc(s_split, 1)

            def norm(name, t):
                a, n = norm_cols(name, t)
                r = nss[name][0:32 if name == "kc" else P, a:a + n]
                w = {"y": 512, "qk": HD, "kc": HD, "hgrn": P}.get(name, D)
                if name == "out1":
                    dve.wait_ge(*ended(tile_of("out1", (t, 1))))
                    link(v.tensor_tensor(r, sso[:, 2 * t:2 * t + 1], sso[:, 2 * t + 1:2 * t + 2], ALU.add))
                elif name in SQUARED:
                    dve.wait_ge(s_ss, sum(x[0] in SQUARED for x in NORMS[:norm_no(name, t)]))
                elif name == "qk":
                    if t == 0:
                        dve.wait_ge(s_spill, 16 * NT)
                    dve.wait_ge(*ended(tile_of("kv", (t, 0))))
                    dve.wait_ge(*ended(tile_of("qn", (t, 0))))
                    link(v.tensor_tensor(sq_, qt_[:, t, :], qt_[:, t, :], ALU.mult))
                    link(v.tensor_reduce(r[:, 0:8], h64(sq_), AX.X, ALU.add))
                    link(v.tensor_tensor(sq_[:, 0:256], kst[:, t, :], kst[:, t, :], ALU.mult))
                    link(v.tensor_reduce(r[:, 8:12], h64(sq_[:, 0:256]), AX.X, ALU.add))
                elif name == "kc":
                    dve.wait_ge(s_hid, 2)
                    link(v.tensor_copy(kcn[0:32, :], bank[6][0:32, 0:P]))
                    link(v.tensor_tensor(nsq[0:32, :], kcn[0:32, :], kcn[0:32, :], ALU.mult))
                    link(v.tensor_reduce(r, h64(nsq[0:32, :]), AX.X, ALU.add))
                else:
                    dve.wait_ge(*ended(tile_of("hout", HH - 1)))
                    link(v.tensor_tensor(hsq, mixt[:, t, :], mixt[:, t, :], ALU.mult))
                    link(v.tensor_reduce(r, hsq.rearrange("p (a b) -> p a b", b=P), AX.X, ALU.add))
                link(v.tensor_scalar(r, r, 1.0 / w, EPS, ALU.mult, ALU.add))
                v.reciprocal(r, r).then_inc(s_rec, 1)

            def apply(name, t):
                a, n = norm_cols(name, t)
                r = nss[name][0:32 if name == "kc" else P, a:a + n]
                dve.wait_ge(s_rt, norm_no(name, t))
                if name in ROWS:
                    dve.wait_ge(s_row[name], 16)
                if name == "x":
                    last = v.scalar_tensor_tensor(xt[:, t, :], xt[:, t, :], r, rows["x"], ALU.mult, ALU.mult)
                if name == "y":
                    for g in range(2):
                        y = xs[:, t, 512 * g:512 * g + 512]
                        last = v.scalar_tensor_tensor(y, y, r[:, g:g + 1], rows["y"][:, 512 * g:512 * g + 512], ALU.mult, ALU.mult)
                if name in ("mix", "ffn"):
                    src = {"mix": xres, "ffn": x2}[name]
                    last = v.scalar_tensor_tensor(xn[:, t, :], src[:, t, :], r, rows[name], ALU.mult, ALU.mult)
                if name == "qk":
                    for g in range(NG):
                        v.tensor_tensor(qn_[:, t, :, HD * g:HD * g + HD], h64(qt_[:, t, 256 * g:256 * g + 256]),
                                        r[:, 4 * g:4 * g + 4].unsqueeze(2).to_broadcast([P, 4, HD]), ALU.mult)
                    k = h64(kst[:, t, :])
                    last = v.tensor_tensor(k, k, r[:, 8:12].unsqueeze(2).to_broadcast([P, 4, HD]), ALU.mult)
                if name == "kc":
                    k = h64(kcn[0:32, :])
                    last = v.tensor_tensor(k, k, r.unsqueeze(2).to_broadcast([32, 2, HD]), ALU.mult)
                if name == "hgrn":
                    o = mixt[:, t, :].rearrange("p (a b) -> p a b", b=P)
                    link(v.tensor_tensor(o, o, r.unsqueeze(2).to_broadcast([P, 4, P]), ALU.mult))
                    last = v.tensor_tensor(o, o, onorm.unsqueeze(1).to_broadcast([P, 4, P]), ALU.mult)
                if name == "out1":
                    dve.wait_ge(s_res, 32)
                    link(v.scalar_tensor_tensor(oraw[:, t, :], oraw[:, t, :], r, npost, ALU.mult, ALU.mult))
                    last = v.tensor_tensor(xres[:, t, :], xres[:, t, :], oraw[:, t, :], ALU.add)
                last.then_inc(s_norm, 1)

            def split_turned(s, dst, chunks, t, bank_):
                ts = slice(P * t, P * t + P)
                hi, lo = ACTS[dst]
                dve.wait_ge(s_round, TURNS.index(s) + 1)
                v.tensor_tensor(lo[:, chunks, ts], bank_[:, :].rearrange("p (a b) -> p a b", b=P), f32(hi[:, chunks, ts]),
                                ALU.subtract).then_inc(s_split, 1)

            def lower_bound():
                dve.wait_ge(s_hlb, 2)
                link(v.tensor_scalar(lbn, lbs, -1.0, 1.0, ALU.mult, ALU.add))

            def compress(i):
                if i == 0:
                    v.memset(hid, 0.0).then_inc(s_hidz, 1)
                    dve.wait_ge(s_gelu, 2)
                    for g in range(NG):
                        v.tensor_copy(hid4[:, g, :, :], hid[:, 1, g, :].unsqueeze(1).to_broadcast([P, 4, 32])).then_inc(s_hid4, 1)
                if i == 1:
                    norm("kc", 0)
                    apply("kc", 0)
                if i == 2:
                    dve.wait_ge(s_hid, 3)
                    for g in range(NG):
                        last = v.tensor_tensor(vcd[:, g, :, :], bank[7][:, HD * g:HD * g + HD].unsqueeze(1).to_broadcast([P, 4, HD]),
                                               heads4.unsqueeze(2).to_broadcast([P, 4, HD]), ALU.mult)
                    last.then_inc(s_vcd, 1)

            def cmp(qt, i):
                s3 = cs_[qt % 2]
                n3 = s3[:, :, 0:NCMP]
                mx, sm = cmx[:, 8 * (qt % 2):8 * (qt % 2) + 8], csum[:, 8 * (qt % 2):8 * (qt % 2) + 8]
                gate = gl[:, 24 * qt:24 * qt + 24].rearrange("p (a b) -> p b a", b=3)[:, 0, :]
                if i == 0:
                    if qt >= 2:
                        dve.wait_ge(s_ctr, qt - 1)
                    link(v.memset(s3, NEG))
                    dve.wait_ge(s_cqk, qt + 1)
                    for g in range(NG):
                        link(v.tensor_tensor(n3[:, 4 * g:4 * g + 4, :],
                                             bank[4 + 3 * g][:, 0:P].rearrange("p (a b) -> p a b", b=32)[:, :, 0:NCMP],
                                             cmask[:, qt, 0:NCMP].unsqueeze(1).to_broadcast([P, 4, NCMP]), ALU.add))
                    link(v.tensor_reduce(mx, n3, AX.X, ALU.max))
                    v.tensor_tensor(n3, n3, mx.unsqueeze(2).to_broadcast([P, NH, NCMP]), ALU.subtract).then_inc(s_cs, 1)
                if i == 1:
                    dve.wait_ge(s_ce, qt + 1)
                    link(v.tensor_reduce(sm, n3, AX.X, ALU.add))
                    link(v.reciprocal(sm, sm))
                    if qt == 0:
                        dve.wait_ge(*end_sem("gates"))
                    link(v.tensor_tensor(sm, sm, gate, ALU.mult))
                    link(v.tensor_scalar(sm, sm, cmask[:, qt, 31:32], None, ALU.mult))
                    v.tensor_tensor(s3, s3, sm.unsqueeze(2).to_broadcast([P, NH, 32]), ALU.mult).then_inc(s_cp, 1)

            def nsa(u):
                w = u - 1
                f = f2[:, 2 * (w % 2):2 * (w % 2) + 2]
                if 0 <= w < UNITS:
                    dve.wait_ge(s_np, 2 * w + 2)
                    if w >= 2:
                        dve.wait_ge(s_nw, w - 1)
                    qt, h = divmod(w, NH)
                    link(v.reciprocal(f, nsum[:, 2 * w:2 * w + 2]))
                    v.tensor_tensor(f, f, gl[:, 24 * qt + 3 * h + 1:24 * qt + 3 * h + 3], ALU.mult).then_inc(s_nf, 1)
                if u < UNITS:
                    kend = P * (u // NH + 1)
                    m = nmx[:, 2 * u:2 * u + 2]
                    dve.wait_ge(s_nqk, 2 * u + 2)
                    if kend <= 256:
                        last = v.tensor_reduce(m, bank[BANK_LOGITS + u % 2][:, 0:2 * kend].rearrange("p (a b) -> p a b", b=kend),
                                               AX.X, ALU.max, negate=True)
                    else:
                        for b in range(2):
                            last = v.tensor_reduce(m[:, b:b + 1], nsa_logits(u, b), AX.X, ALU.max, negate=True)
                    last.then_inc(s_nmx, 1)
                o = u - NSA_LAG - 1
                if o >= 0 and o % NH == NH - 1:
                    split_turned(("nsa", u), "B", slice(0, 4), o // NH, bank[BANK_O])
                    dve.wait_ge(s_split, SPLITS.index(("nsa", u)) + 1)
                    dve.sem_inc(s_nm, 1)

            def level(h, n):
                hq_, hk_, pre, suf = hset[h % 2]
                if (h, n) == (0, 0):
                    dve.wait_ge(s_hc, 32)
                    link(v.tensor_copy(halves, halves_f))
                if n > 0:
                    dve.wait_ge(s_tile, DONE[level_tile(h, n - 1)])
                    read(h, n - 1)
                m = n + 1
                if m > LEVELS:
                    return
                w = 2 ** n
                q_, k_ = hqk[m % 2]
                two = lambda ap: ap.rearrange("p (a b c) -> p a b c", b=2, c=w)
                if m == 1:
                    link(v.memset(suf, 1.0))
                    dve.wait_ge(s_hlev, (LEVELS + 1) * h + 1)
                else:
                    dve.wait_ge(s_vc, updated[0])
                mark_q = mark(v.tensor_tensor(two(q_)[:, :, 1, :], two(hq_)[:, :, 1, :], two(pre)[:, :, 1, :], ALU.mult))
                if m == 1:
                    dve.wait_ge(s_vc, mark_q)
                    v.tensor_tensor(two(k_)[:, :, 1, :], two(hk_)[:, :, 0, :], two(q_)[:, :, 1, :], ALU.mult).then_inc(s_hlev, 1)
                else:
                    v.tensor_tensor(two(k_)[:, :, 0, :], two(hk_)[:, :, 0, :], two(suf)[:, :, 0, :], ALU.mult).then_inc(s_hlev, 1)
                if m < LEVELS:
                    dve.wait_ge(s_hlev, (LEVELS + 1) * h + m + 1)
                    last_of = lambda i: two(pre)[:, :, i, w - 1:w].to_broadcast([P, T // (2 * w), w])
                    link(v.tensor_tensor(two(suf)[:, :, 0, :], two(suf)[:, :, 0, :], last_of(1), ALU.mult))
                    updated[0] = mark(v.tensor_tensor(two(pre)[:, :, 1, :], two(pre)[:, :, 1, :], last_of(0), ALU.mult))

            def read(h, n):
                g = level_tile(h, n)
                dve.wait_ge(s_tile, DONE[g])
                ps = bank[BANK[g]]
                if (h, n) != (0, 0):
                    dve.wait_ge(*ended(level_tile(h, n - 1) if n else level_tile(h - 1, LEVELS)))
                if n == 0:
                    if h > 0:
                        dve.wait_ge(s_tile, DONE[tile_of("hout", h - 1)])
                    r = lambda ap: ap.rearrange("p (a b) -> p a b", b=P)
                    ins = v.tensor_tensor(r(hat[:, 0:512]), r(ps[:, :]), ident.unsqueeze(1).to_broadcast([P, NT, P]), ALU.mult)
                elif n == 7:
                    up = lambda ap: ap.rearrange("p (a b) -> p a b", b=P)[:, :, HD:P]
                    ins = v.tensor_copy(up(hat[0:HD, 0:512]), up(ps[0:HD, :]))
                elif n < 7:
                    w = 2 ** (n - 1)
                    up = lambda ap: ap.rearrange("p (a b c) -> p a b c", b=2, c=w)[:, :, 1, :]
                    ins = v.copy_predicated(up(hat[:, 0:512]), halves[:, 256 * (n - 1):256 * n].rearrange("p (a b) -> p a b", b=w),
                                            up(ps[:, :]))
                elif n == 8:
                    ins = v.tensor_copy(hat[:, 512:768], ps[:, 0:256])
                else:
                    ins = v.tensor_copy(hat[:, 768:1280], ps[:, :])
                ins.then_inc(s_end["V"], 1)

            def dt_part(i):
                if i == 0:
                    g = tile_of("dt", 0)
                    dve.wait_ge(s_tile, DONE[g])
                    dve.wait_ge(s_cst, 32)
                    link(v.tensor_tensor(t64[0].rearrange("p (a b) -> p a b", b=SH),
                                         bank[BANK[g]][:, 0:64].rearrange("p (a b) -> p a b", b=SH),
                                         V("dt_bias", 0, SH).unsqueeze(1).to_broadcast([P, NT, SH]), ALU.add))
                    dve.sem_inc(s_end["V"], 1)
                    link(v.tensor_scalar(t64[1], t64[0], -1.0, None, ALU.mult))
                    link(v.tensor_tensor(t64[1], t64[1], t64[0], ALU.min))
                    dve.sem_inc(s_dte, 1)
                if i == 1:
                    dve.wait_ge(s_ex, 1)
                    link(v.tensor_scalar(t64[1], t64[1], 1.0, None, ALU.add))
                    dve.sem_inc(s_dte, 1)
                    link(v.tensor_scalar(t64[0], t64[0], 0.0, None, ALU.max))
                if i == 2:
                    dt_end()

            def dt_end():
                dve.wait_ge(s_ex, 3)
                link(v.tensor_tensor(dt_, t64[0], t64[1], ALU.add))
                v.scalar_tensor_tensor(adt.rearrange("p (a b) -> p a b", b=SH), dt_.rearrange("p (a b) -> p a b", b=SH),
                                       -1.0, aexp.unsqueeze(1).to_broadcast([P, NT, SH]), ALU.mult, ALU.mult).then_inc(s_dt, 1)
                dve.wait_ge(s_dt, 1)
                link(v.tensor_copy(adt_hi, adt))
                v.tensor_copy(ones_r, ones)
                link(v.tensor_tensor(adt_lo, adt, f32(adt_hi), ALU.subtract))
                dve.sem_inc(s_dt, 1)

            def ssd_decay():
                dve.wait_ge(s_aux, AUX.at["decay"] + 1)
                ps = bank[4 + AUX.slot("decay")]
                v.tensor_copy(t64[0], ps[:, 0:64])
                link(v.tensor_copy(t64[1], ps[:, 64:128]))
                v.tensor_scalar(acs_n, t64[0], -1.0, None, ALU.mult)
                link(v.tensor_tensor(t64[2], t64[1], t64[0], ALU.subtract))
                dve.sem_inc(s_auxend["V"], 1)
                dve.sem_inc(s_dte, 1)
                dve.wait_ge(s_ex, 4)
                v.tensor_tensor(dtend, dtend, dt_, ALU.mult).then_inc(s_dt, 1)

            def ssd(c, part):
                if part == 0:
                    key = ("scores", c)
                    dve.wait_ge(s_aux, AUX.at[key] + 1)
                    link(v.tensor_copy(sc, bank[4 + AUX.slot(key)][:, 0:2 * P].rearrange("p (a b) -> p a b", b=P)))
                    dve.sem_inc(s_auxend["V"], 1)
                if part < 4:
                    dve.wait_ge(s_auxend["S"], AUX.ends[AUX.at[("decay", c, part)]][1])
                    e = ee[:, part % 2, :, :]
                    v.tensor_tensor(e, e, sc[:, part // 2, :].unsqueeze(1).to_broadcast([P, 4, P]), ALU.mult).then_inc(s_attn, 1)
                if part == 4:
                    bc = lambda t, g: t[:, SH * c + 8 * g:SH * c + 8 * g + 8].unsqueeze(2).to_broadcast([P, 8, HD])
                    if c > 0:
                        for g in range(2):
                            key = ("y_off", c, g)
                            dve.wait_ge(s_aux, AUX.at[key] + 1)
                            link(v.tensor_tensor(h64(ytmp[:, g, :]), h64(bank[4 + AUX.slot(key)][:, :]), bc(ecs, g), ALU.mult))
                            dve.sem_inc(s_auxend["V"], 1)
                    dve.wait_ge(s_yd, 4 * c + 4)
                    dve.wait_ge(s_xd, 2 * c + 2)
                    for g in range(2):
                        y, x = ytmp[:, g, :], xs[:, c, 512 * g:512 * g + 512]
                        if c > 0:
                            link(v.tensor_tensor(y, y, bank[6 + g][:, :], ALU.add))
                            ins = v.tensor_tensor(x, x, y, ALU.add)
                        else:
                            ins = v.tensor_tensor(x, bank[6 + g][:, :], x, ALU.add)
                    ins.then_inc(s_y, 1)
                    if c < NT - 1:
                        for g in range(2):
                            key = ("state", c, g)
                            if c > 0:
                                link(v.tensor_tensor(h64(state[:, g, :]), h64(state[:, g, :]), bc(edec, g), ALU.mult))
                            dve.wait_ge(s_aux, AUX.at[key] + 1)
                            ps = bank[4 + AUX.slot(key)][:, :]
                            if c > 0:
                                ins = v.tensor_tensor(state[:, g, :], state[:, g, :], ps, ALU.add)
                            else:
                                ins = v.tensor_copy(state[:, g, :], ps)
                            ins.then_inc(s_st, 1)
                            dve.wait_ge(s_st, 2 * c + g + 1)
                            dve.sem_inc(s_auxend["V"], 1)

            def stick(u):
                if u < SH * NT:
                    kend = P * (u % NT + 1)
                    f0 = 516 * (u % 2)
                    if u == 0:
                        for i in range(2):
                            v.memset(sb_fail[:, 516 * i + 512:516 * i + 513], 1.0)
                        v.memset(zeros, 0.0).then_inc(s_zero, 1)
                        dve.wait_ge(s_zero, 1)
                        v.memset(zerob[:, :], 0.0).then_inc(s_zero, 1)
                    dve.wait_ge(s_sig, u + 1)
                    if u >= 3:
                        dve.wait_ge(s_tr, u - 2)
                    w = sb_w[:, u % 3, 0:kend]
                    fail = sb_fail[:, f0 + 513 - kend:f0 + 513]
                    v.tensor_tensor_scan(w[:, ::-1], fail[:, ::-1], zeros.to_broadcast([P, kend]), 1.0, ALU.mult, ALU.add)\
                        .then_inc(s_scan, 1)
                o = u - SB_LAG - 1
                if 0 <= o:
                    h, qt = divmod(o, NT)
                    rows_ = slice(HD * (h % 2), HD * (h % 2) + HD)
                    dve.wait_ge(s_pv, o + 1)
                    v.tensor_copy(qf[rows_, h // 2, P * qt:P * qt + P], bank[BANK_O][rows_, P * (o % 4):P * (o % 4) + P]).then_inc(s_o, 1)

            for s in STEPS:
                if s == ("apply", "x", NT - 1):
                    rest_of_small("dt")
                if s[0] == "norm":
                    norm(*s[1:])
                if s[0] == "apply":
                    apply(*s[1:])
                if s[0] == "turn":
                    split_turned(s, FILLS[s[1]], slice(4 * s[3], 4 * s[3] + 4), s[2], bank[BANK[s[4]]])
                if s[0] == "gemm":
                    if s[2] == 3:
                        rest_of_weights(s[1] + 1)
                    for g in closed(BLOCKS[s[1]], s[2]):
                        tile(g)
                if s[0] == "pos":
                    v.tensor_scalar(V("q_norm"), V("q_norm"), SCALE, None, ALU.mult)
                    v.tensor_tensor(lbs, V("lower", 0, 4), V("lower", 4, 4), ALU.subtract).then_inc(s_hlb, 1)
                    rest_of_small("gates")
                if s[0] == "small":
                    rest_of_weights(0) if s[1] == "dt" else lower_bound()
                if s[0] == "dt":
                    dt_part(s[1])
                if s[0] == "compress":
                    compress(s[1])
                if s[0] == "cmp":
                    cmp(*s[1:])
                if s[0] == "nsa":
                    nsa(s[1])
                if s[0] == "level":
                    level(s[1], s[2])
                if s[0] == "hout":
                    read(s[1], LEVELS)
                if s[0] == "ssd_decay":
                    ssd_decay()
                if s[0] == "ssd":
                    ssd(s[1], s[2])
                if s[0] == "sb":
                    stick(s[1])
                if s[0] == "merge":
                    c = s[1]
                    dve.wait_ge(s_tround, PRODUCTS.index(s) + 1)
                    v.tensor_tensor(a_lo[:, c, :], mg[:, c, :], f32(a_hi[:, c, :]), ALU.subtract).then_inc(s_split, 1)

        @block.gpsimd
        def _(pool):
            g_ = nc.gpsimd
            h16 = lambda ap: ap.rearrange("p (a b) -> p a b", b=HD)

            def decays(n):
                if n == 0:
                    pool.wait_ge(s_dt, 2)
                if n >= 4:
                    pool.wait_ge(s_aux, AUX.at[("decay", (n - 4) // 4, (n - 4) % 4)] + 1)
                for part_, a_ in ((b_hi, adt_hi), (b_lo, adt_lo)):
                    last = g_.tensor_tensor(part_[:, n % 4, :].rearrange("p (a b) -> p a b", b=P),
                                            tri.unsqueeze(1).to_broadcast([P, 4, P]),
                                            f32(a_[:, 4 * n:4 * n + 4]).unsqueeze(2).to_broadcast([P, 4, P]), ALU.mult)
                last.then_inc(s_tri, 1)

            for s in STEPS:
                if s[0] == "ssd_decay":
                    decays(0)
                if s[0] == "ssd" and s[2] < 4 and 4 * s[1] + s[2] + 1 < 4 * NT:
                    decays(4 * s[1] + s[2] + 1)
                if s[0] == "ssd" and s[2] == 0:
                    c = s[1]
                    bc = lambda t: t[:, SH * c:SH * c + SH].unsqueeze(2).to_broadcast([P, SH, HD])
                    if c == 0:
                        pool.wait_ge(s_dt, 3)
                        pool.wait_ge(s_auxend["S"], 10)
                        pool.wait_ge(s_cx, XC)
                    if c >= 2:
                        pool.wait_ge(s_yd, 4 * c - 4)
                    g_.tensor_tensor(h16(xdt[:, c % 2, :]), h16(xs[:, c, :]), bc(dt_), ALU.mult).then_inc(s_xd, 1)
                    if 1 <= c:
                        pool.wait_ge(s_st, 2 * c)
                    if c < NT - 1:
                        g_.tensor_tensor(h16(xdd), h16(xs[:, c, :]), bc(dtend), ALU.mult).then_inc(s_pc, 1)
                        pool.wait_ge(s_pc, c + 1)
                    pool.wait_ge(s_xd, 2 * c + 1)
                    g_.tensor_tensor(h16(xs[:, c, :]), h16(xs[:, c, :]), V("d_skip", 0, SH).unsqueeze(2).to_broadcast([P, SH, HD]),
                                     ALU.mult).then_inc(s_xd, 1)
                if s[0] == "nsa" and 1 <= s[1] <= UNITS:
                    u = s[1] - 1
                    w = np_[u % 3][:, :, 0:P * (u // NH + 1)]
                    pool.wait_ge(s_nf, u + 1)
                    g_.tensor_tensor(w, w, f2[:, 2 * (u % 2):2 * (u % 2) + 2].unsqueeze(2).to_broadcast(list(w.shape)), ALU.mult)\
                        .then_inc(s_nw, 1)
                if s[0] == "sb" and s[1] < SH * NT:
                    u = s[1]
                    kend = P * (u % NT + 1)
                    pool.wait_ge(s_scan, u + 1)
                    w = sb_w[:, u % 3, 0:kend]
                    g_.tensor_tensor(w, w, sb_sig[:, u % 2, 0:kend], ALU.mult).then_inc(s_wgt, 1)


def lay_out(x, norm_pre, w_in, b_gate, conv_w, conv_b, dt_bias, a_log, d_skip, ssd_norm, w_ssd_proj, w_sb_proj,
            w_out, norm_post, norm_mix_2, w_in_2, q_norm_2, k_norm_2, cmp_pos_k_2, cmp_pos_v_2, cmp_k_w1_2, cmp_k_w2_2,
            cmp_v_w1_2, cmp_v_w2_2, hgrn_lb_logits_2, hgrn_o_norm_2, w_out_2, norm_ffn_2, w_gate_up_2, w_down_2):
    w = {"w_in": (w_in[0],), "gate_ssd": (w_in[0], w_ssd_proj[0]), "gate_sb": (w_in[0], w_sb_proj[0]), "w_out": (w_out[0],),
         "w_in_2": (w_in_2[0],), "w_out_2": (w_out_2[0],), "w_gate_up": (w_gate_up_2[0],), "w_down": (w_down_2[0],)}
    blk = np.zeros((NB, P, BLK), w_in.dtype)
    for n, b in enumerate(BLOCKS):
        src = w[b["w"]]
        parts = []
        for i, (c0, cn) in enumerate(b["spans"]):
            m = src[min(i, len(src) - 1)]
            parts.append(m[P * b["k0"]:P * (b["k0"] + b["kn"]), c0:c0 + cn].reshape(b["kn"], P, cn))
        joined = np.concatenate(parts, axis=2).transpose(1, 0, 2).reshape(P, -1)
        blk[n, :, :joined.shape[1]] = joined
    cols = lambda a: a.reshape(-1, P).T
    rows = lambda a: np.broadcast_to(a.reshape(1, -1), (P, a.size))
    vec = np.empty((P, VEC.width), x.dtype)
    conv = conv_w[0].reshape(TAPS, XC, P).transpose(2, 1, 0).reshape(P, XC * TAPS)
    for name, v in dict(b_gate=cols(b_gate[0]), conv_w=conv, conv_b=cols(conv_b[0]),
                        dt_bias=rows(dt_bias[0]), a_log=rows(a_log[0]),
                        d_skip=rows(d_skip[0]),
                        q_norm=np.tile(q_norm_2[0].reshape(HD, 1), (2, 1)), k_norm=np.tile(k_norm_2[0].T, (2, 1)),
                        lower=np.concatenate([cols(hgrn_lb_logits_2[0]), cols(hgrn_lb_logits_2[1])], axis=1)).items():
        vec[:, VEC.at(name)] = v
    cst = np.empty((P, CST.width), np.float32)
    i, j = np.arange(P)[:, None], np.arange(P)[None, :]
    cst[:, CST.at("ident")] = i == j
    cst[:, CST.at("tri")] = i <= j
    cst[:, CST.at("ones")] = 1.0
    bf = mybir.dt.np(BF16)
    cstb = np.empty((P, CSTB.width), bf)
    cstb[:, CSTB.at("ident")] = i == j
    cstb[:, CSTB.at("strict")] = np.where(j < i, 0.0, NEG)
    cstb[:, CSTB.at("after")] = np.where(i <= j, 0.0, NEG)
    small = lambda m, c0, n: m[:, c0:c0 + n].reshape(NK, P, n).transpose(1, 0, 2).reshape(P, NK * n)
    w1 = lambda m: m[0].reshape(CL // 2, P, P).transpose(1, 0, 2).reshape(P, CL // 2 * P)
    cst2 = np.zeros((P, CST2.width), x.dtype)
    cst2[:, CST2.at("w2")] = np.concatenate([cmp_k_w2_2[0], cmp_v_w2_2[0]], axis=1)
    cst2[:, CST2.at("pos")] = np.concatenate([m[0].reshape(CL // 2, P).T for m in (cmp_pos_k_2, cmp_pos_v_2)], axis=1)
    cst2[:, CST2.at("one")] = 1.0
    cst2[:, CST2.at("heads")] = i // 32 == np.arange(4)[None, :]
    upto = np.where(j <= i, 0.0, NEG).astype(bf)
    token = np.arange(T).reshape(NT, P).T[:, :, None]
    ends = (CS * np.arange(32) + CL - 1)[None, None, :]
    cmask = np.where(ends <= token, 0.0, NEG).astype(np.float32)
    cmask[:, :, 31] = (token >= CL - 1)[:, :, 0]
    halves = np.zeros((P, 6, 256), np.float32)
    t = np.arange(T)
    for n in range(6):
        up = t[(t >> n) & 1 == 1]
        s = np.arange(P)[:, None]
        halves[:, n, :] = (s >> (n + 1) == (up % P)[None, :] >> (n + 1)) & ((s >> n) & 1 == 0)
    return {"x": x[0], "wblk": blk, "vec": vec, "cst": cst, "cstb": cstb, "w_dt": small(w_in[0], DT0, SH),
            "w_gates": small(w_in_2[0], GL0, 24), "norm_post": rows(norm_post[0]), "w1k": w1(cmp_k_w1_2),
            "w1v": w1(cmp_v_w1_2), "cst2": cst2, "upto": upto, "cmask": cmask.reshape(P, P),
            "halves": halves.reshape(P, 6 * 256), "onorm": rows(hgrn_o_norm_2[0]), "norm_pre": rows(norm_pre[0]),
            "ssd_norm": rows(ssd_norm[0]), "norm_mix": rows(norm_mix_2[0]), "norm_ffn": rows(norm_ffn_2[0])}


def kernel(**inputs):
    import concourse.bacc as bacc
    from concourse.bass_utils import run_bass_kernel_spmd

    nc = bacc.Bacc("TRN2", target_bir_lowering=False, num_devices=1)
    arrays = {name: np.ascontiguousarray(a) for name, a in lay_out(**inputs).items()}
    dram = {name: nc.dram_tensor("in_" + name, a.shape, mybir.dt.from_np(a.dtype), kind="ExternalInput").ap()
            for name, a in arrays.items()}
    out = nc.dram_tensor("out", (T, D), F32, kind="ExternalOutput").ap()
    spill = nc.dram_tensor("spill", (T, D), F32).ap()
    emit(nc, dram, spill, out)
    r = run_bass_kernel_spmd(nc, [{"in_" + name: a for name, a in arrays.items()}], core_ids=[0])
    return r.results[0]["out"].reshape(1, T, D)
```
